# Optimizing a Trainium2 kernel written in Bass

```python
import math
import jax, jax.numpy as jnp
from jax import lax
import numpy as np

'''Hybrid diffusion / flow-matching trunk: one inference step (DEPTH layers) for two request groups sharing weights.

Even layers: HGRN2 (bidirectional gated linear recurrence with state expansion) and Hyena (order-2, bidirectional
FFT long convolution) as parallel head groups behind one combined input projection and one output projection.
Odd layers: bidirectional multi-scale retention (chunkwise recurrent). Every layer: expert-choice SwiGLU MoE.
Each sub-layer: u = x*(1+scale)+shift (adaLN from SiLU(cond)), x <- LayerNorm(DN_ALPHA*x + gate*sublayer(u)).
Context tokens use cond = c_ctx and read only context; latent tokens use cond = c, their recurrent scans start
from the cached final context states (per direction); Hyena and MoE treat context and latent as separate sets.

Inputs:
  x_prompt   (BATCH, SEQ, D_MODEL)            context tokens of BATCH new requests
  x_sample   (DEC_BATCH, DEC_SEQ, D_MODEL)    all noisy latent tokens (grid rows = DEC_SEQ // GRID_W)
  state_hgrn (DEC_BATCH, N_EVEN, 2, A_HEADS, A_HEAD_DIM, A_HEAD_DIM)  final context HGRN2 states [fwd, bwd]
  state_ret  (DEC_BATCH, N_ODD, 2, C_HEADS, C_HEAD_DIM, C_HEAD_DIM)   final context retention states [fwd, bwd]
  c          (DEC_BATCH, D_MODEL)             conditioning vectors of the denoising requests
  c_ctx      (D_MODEL,)                       learned conditioning vector of context tokens
  followed by the weights.
Returns the tuple (y_prompt, y_sample, new_state_hgrn, new_state_ret):
  y_prompt       (BATCH, SEQ, D_MODEL)
  y_sample       (DEC_BATCH, DEC_SEQ, D_MODEL)
  new_state_hgrn (BATCH, N_EVEN, 2, A_HEADS, A_HEAD_DIM, A_HEAD_DIM)
  new_state_ret  (BATCH, N_ODD, 2, C_HEADS, C_HEAD_DIM, C_HEAD_DIM)
'''

D_MODEL = 1024
BATCH = 1
SEQ = 128
DEPTH = 2
DEC_BATCH = 1
DEC_SEQ = 1024
PAST_LEN = 128

GRID_W = 64
N_EVEN = (DEPTH + 1) // 2
N_ODD = DEPTH // 2
A_WIDTH = D_MODEL // 2
A_HEADS = 4
A_HEAD_DIM = A_WIDTH // A_HEADS
F_MIN = 1e-30
B_WIDTH = D_MODEL - A_WIDTH
HYENA_ORDER = 2
FILTER_EMB = 33
FILTER_HID = 64
SHORT_CONV = 3
DECAY_TARGET = 1e-2
FAST_DECAY = 0.3
SLOW_DECAY = 1.5
C_HEADS = 4
C_HEAD_DIM = D_MODEL // C_HEADS
ROPE_BASE = 10000.0
N_EXPERTS = 16
EXPERT_FF = 1408
CAP_FACTOR = 2
CHUNK = 64
LN_EPS = 1e-5
DN_ALPHA = (2 * DEPTH) ** 0.25
DN_BETA = (8 * DEPTH) ** -0.25
EVEN_IN = 5 * A_WIDTH + 3 * B_WIDTH
ODD_IN = 4 * D_MODEL
F32 = jnp.float32

kernel_name = 'hgrn2_hyena_retention_ecmoe_diffusion_step'

def layer_norm(x, g, b):
    xf = x.astype(F32)
    mu = jnp.mean(xf, -1, keepdims=True)
    var = jnp.mean(jnp.square(xf - mu), -1, keepdims=True)
    return ((xf - mu) * lax.rsqrt(var + LN_EPS) * g.astype(F32) + b.astype(F32)).astype(x.dtype)

def modulation(cond, w, b):
    m = jax.nn.silu(cond) @ w + b
    return jnp.split(m[..., None, :], 6, axis=-1)

def chunk_scan(q, k, v, log_f, s0):
    bn, L, H, _ = q.shape
    n = L // CHUNK

    def blocks(t):
        return t.astype(F32).reshape(bn, n, CHUNK, H, t.shape[-1]).transpose(1, 0, 3, 2, 4)

    qc, kc, vc, gc = blocks(q), blocks(k), blocks(v), blocks(log_f)
    mask = jnp.tril(jnp.ones((CHUNK, CHUNK), dtype=bool))[:, :, None]
    scalar = log_f.shape[-1] == 1

    def step(S, inp):
        qb, kb, vb, gb = inp
        b = jnp.cumsum(gb, axis=-2)
        inter = jnp.einsum('bhtd,bhde->bhte', qb * jnp.exp(b), S)
        diff = b[..., :, None, :] - b[..., None, :, :]
        rel = jnp.where(mask, jnp.exp(jnp.minimum(diff, 0.0)), 0.0)
        if scalar:
            att = jnp.einsum('bhtd,bhsd->bhts', qb, kb) * rel[..., 0]
        else:
            att = jnp.einsum('bhtd,bhsd,bhtsd->bhts', qb, kb, rel)
        intra = jnp.einsum('bhts,bhse->bhte', att, vb)
        b_end = b[..., -1:, :]
        S = S * jnp.swapaxes(jnp.exp(b_end), -1, -2) + jnp.einsum('bhsd,bhse->bhde', kb * jnp.exp(b_end - b), vb)
        return S, inter + intra

    s_fin, o = lax.scan(step, s0.astype(F32), (qc, kc, vc, gc))
    o = o.transpose(1, 0, 3, 2, 4).reshape(bn, L, H, v.shape[-1])
    return o, s_fin

def bidir_scan(q, k_f, k_b, v, lf_f, lf_b, s0):
    o_f, s_f = chunk_scan(q, k_f, v, lf_f, s0[:, 0])
    rev = lambda t: jnp.flip(t, axis=1)
    o_b, s_b = chunk_scan(rev(q), rev(k_b), rev(v), rev(lf_b), s0[:, 1])
    return o_f + rev(o_b), jnp.stack([s_f, s_b], axis=1)

def short_conv(x, w, b):
    L = x.shape[1]
    pad = SHORT_CONV // 2
    xp = jnp.pad(x, ((0, 0), (pad, pad), (0, 0)))
    return sum(xp[:, j:j + L] * w[j] for j in range(SHORT_CONV)) + b

def hyena_filters(L, w1, b1, w2, b2, w3, freq):
    t = jnp.linspace(0.0, 1.0, L, dtype=F32)[:, None]
    bands = (FILTER_EMB - 1) // 2
    ang = (2.0 * math.pi / L) * jnp.arange(L, dtype=F32)[:, None] * jnp.linspace(1e-4, bands - 1, bands, dtype=F32)[None, :]
    z = jnp.concatenate([t, jnp.cos(ang), -jnp.sin(ang)], axis=-1)
    f = freq.astype(F32)
    hdn = jnp.sin(f[0] * (z @ w1.astype(F32) + b1.astype(F32)))
    hdn = jnp.sin(f[1] * (hdn @ w2.astype(F32) + b2.astype(F32)))
    filt = (hdn @ w3.astype(F32)).reshape(L, HYENA_ORDER, 2, B_WIDTH)
    deltas = jnp.abs(jnp.linspace(math.log(DECAY_TARGET) / SLOW_DECAY, math.log(DECAY_TARGET) / FAST_DECAY, B_WIDTH, dtype=F32))
    return filt * jnp.exp(-t * deltas)[:, None, None, :]

def bidir_long_conv(u, h_fwd, h_bwd, d):
    L = u.shape[1]
    k = jnp.concatenate([h_fwd, jnp.zeros_like(h_fwd[:1]), jnp.flip(h_bwd[1:], axis=0)], axis=0)
    y = jnp.fft.irfft(jnp.fft.rfft(u, n=2 * L, axis=1) * jnp.fft.rfft(k, axis=0)[None], n=2 * L, axis=1)[:, :L]
    return y + u * d

def hyena(v, gates, filt, d):
    z = v
    for o in range(HYENA_ORDER):
        z = gates[o] * bidir_long_conv(z, filt[:, o, 0], filt[:, o, 1], d[o].astype(F32))
    return z

def rope_2d(x):
    L = x.shape[1]
    n_rows = L // GRID_W
    rows = jnp.repeat(jnp.arange(n_rows), GRID_W)
    cols = jnp.tile(jnp.arange(GRID_W), n_rows)
    half = C_HEAD_DIM // 2
    quarter = half // 2
    inv = ROPE_BASE ** (-jnp.arange(quarter, dtype=F32) / quarter)

    def rot(xa, pos):
        a = pos.astype(F32)[:, None] * inv
        cos, sin = jnp.cos(a)[None, :, None, :], jnp.sin(a)[None, :, None, :]
        x1, x2 = xa[..., :quarter], xa[..., quarter:]
        return jnp.concatenate([x1 * cos - x2 * sin, x1 * sin + x2 * cos], axis=-1)

    xf = x.astype(F32)
    return jnp.concatenate([rot(xf[..., :half], rows), rot(xf[..., half:], cols)], axis=-1).astype(x.dtype)

def ec_moe(h, router, w1, w3, w2):
    bn, N, _ = h.shape
    cap = CAP_FACTOR * N // N_EXPERTS
    aff = jax.nn.softmax(jnp.einsum('bnd,de->ben', h, router).astype(F32), axis=1)
    gate, idx = lax.top_k(aff, cap)
    bidx = jnp.arange(bn)[:, None, None]
    xs = h[bidx, idx]
    hid = jax.nn.silu(jnp.einsum('becd,edf->becf', xs, w1)) * jnp.einsum('becd,edf->becf', xs, w3)
    out = jnp.einsum('becf,efd->becd', hid, w2) * gate[..., None].astype(h.dtype)
    return jnp.zeros_like(h).at[bidx, idx].add(out)

def even_mixer(u, s0, w_in, w_out, lb, norm_w, conv_w, conv_b, fw1, fb1, fw2, fb2, fw3, freq, fbias):
    bn, L, _ = u.shape
    proj = u @ w_in
    q, i, zf, zb, g = jnp.split(proj[..., :5 * A_WIDTH], 5, axis=-1)
    hv, hx1, hx2 = jnp.split(short_conv(proj[..., 5 * A_WIDTH:], conv_w, conv_b).astype(F32), 3, axis=-1)
    heads = lambda t: t.reshape(bn, L, A_HEADS, A_HEAD_DIM)

    def forget(z, lbd):
        z = z.astype(F32)
        f = lbd + (1.0 - lbd) * jax.nn.sigmoid(z)
        log_f = jnp.log(jnp.maximum(f, F_MIN))
        return heads(log_f), heads((1.0 - lbd) * jax.nn.sigmoid(-z))

    lf_f, k_f = forget(zf, lb[0])
    lf_b, k_b = forget(zb, lb[1])
    o, s_new = bidir_scan(heads(jax.nn.silu(q.astype(F32))), k_f, k_b, heads(i), lf_f, lf_b, s0)
    o = o * lax.rsqrt(jnp.mean(o * o, -1, keepdims=True) + LN_EPS) * norm_w.astype(F32).reshape(A_HEADS, A_HEAD_DIM)
    y_a = o.reshape(bn, L, A_WIDTH) * jax.nn.silu(g.astype(F32))
    filt = hyena_filters(L, fw1, fb1, fw2, fb2, fw3, freq)
    y_b = hyena(hv, (hx1, hx2), filt, fbias)
    y = jnp.concatenate([y_a, y_b], axis=-1).astype(u.dtype) @ w_out
    return y, s_new

def retention_mixer(u, s0, latent, w_in, w_out, decay_logit):
    bn, L, _ = u.shape
    q, k, v, g = jnp.split(u @ w_in, 4, axis=-1)
    heads = lambda t: t.reshape(bn, L, C_HEADS, C_HEAD_DIM)
    q, k, v = heads(q), heads(k) * (C_HEAD_DIM ** -0.5), heads(v)
    if latent:
        q, k = rope_2d(q), rope_2d(k)
    log_gamma = jax.nn.log_sigmoid(decay_logit.astype(F32))
    lf = lambda d: jnp.broadcast_to(log_gamma[d][None, None, :, None], (bn, L, C_HEADS, 1))
    o, s_new = bidir_scan(q, k, k, v, lf(0), lf(1), s0)
    mu = jnp.mean(o, -1, keepdims=True)
    var = jnp.mean(jnp.square(o - mu), -1, keepdims=True)
    o = (o - mu) * lax.rsqrt(var + LN_EPS)
    y = (o.reshape(bn, L, D_MODEL) * jax.nn.silu(g.astype(F32))).astype(u.dtype) @ w_out
    return y, s_new

def setup_inputs(seed: int = 0) -> dict:
    key = jax.random.key(seed)
    ks = iter(jax.random.split(key, 40))

    def nrm(shape, scale=1.0):
        return jax.random.normal(next(ks), shape, F32) * scale

    even_cols = jnp.concatenate([jnp.ones(A_WIDTH), jnp.full(A_WIDTH, DN_BETA), jnp.ones(3 * A_WIDTH),
                                 jnp.full(B_WIDTH, DN_BETA), jnp.ones(2 * B_WIDTH)]).astype(F32)
    odd_cols = jnp.concatenate([jnp.ones(2 * D_MODEL), jnp.full(D_MODEL, DN_BETA), jnp.ones(D_MODEL)]).astype(F32)
    ret_init = jnp.log(2.0 ** (5.0 + jnp.arange(C_HEADS, dtype=F32)) - 1.0)
    return {
        'x_prompt': nrm((BATCH, SEQ, D_MODEL)),
        'x_sample': nrm((DEC_BATCH, DEC_SEQ, D_MODEL)),
        'state_hgrn': nrm((DEC_BATCH, N_EVEN, 2, A_HEADS, A_HEAD_DIM, A_HEAD_DIM), 0.5),
        'state_ret': nrm((DEC_BATCH, N_ODD, 2, C_HEADS, C_HEAD_DIM, C_HEAD_DIM), 0.3),
        'c': nrm((DEC_BATCH, D_MODEL)),
        'c_ctx': nrm((D_MODEL,)),
        'ada_w': nrm((DEPTH, D_MODEL, 6 * D_MODEL), D_MODEL ** -0.5),
        'ada_b': nrm((DEPTH, 6 * D_MODEL), 0.02),
        'ln_g': 1.0 + nrm((DEPTH, 2, D_MODEL), 0.02),
        'ln_b': nrm((DEPTH, 2, D_MODEL), 0.02),
        'even_w_in': nrm((N_EVEN, D_MODEL, EVEN_IN), D_MODEL ** -0.5) * even_cols,
        'even_w_out': nrm((N_EVEN, D_MODEL, D_MODEL), DN_BETA * D_MODEL ** -0.5),
        'hgrn_lb': nrm((N_EVEN, 2, A_WIDTH), 0.5),
        'hgrn_norm_w': 1.0 + nrm((N_EVEN, A_WIDTH), 0.02),
        'hyena_conv_w': nrm((N_EVEN, SHORT_CONV, 3 * B_WIDTH), SHORT_CONV ** -0.5),
        'hyena_conv_b': nrm((N_EVEN, 3 * B_WIDTH), 0.02),
        'hyena_w1': nrm((N_EVEN, FILTER_EMB, FILTER_HID), FILTER_EMB ** -0.5),
        'hyena_b1': nrm((N_EVEN, FILTER_HID), 0.02),
        'hyena_w2': nrm((N_EVEN, FILTER_HID, FILTER_HID), FILTER_HID ** -0.5),
        'hyena_b2': nrm((N_EVEN, FILTER_HID), 0.02),
        'hyena_w3': nrm((N_EVEN, FILTER_HID, HYENA_ORDER * 2 * B_WIDTH), 0.1 * FILTER_HID ** -0.5),
        'hyena_freq': 1.0 + nrm((N_EVEN, 2, FILTER_HID), 0.02),
        'hyena_bias': nrm((N_EVEN, HYENA_ORDER, B_WIDTH)),
        'odd_w_in': nrm((N_ODD, D_MODEL, ODD_IN), D_MODEL ** -0.5) * odd_cols,
        'odd_w_out': nrm((N_ODD, D_MODEL, D_MODEL), DN_BETA * D_MODEL ** -0.5),
        'ret_decay': ret_init + nrm((N_ODD, 2, C_HEADS), 0.1),
        'moe_router': nrm((DEPTH, D_MODEL, N_EXPERTS), D_MODEL ** -0.5),
        'moe_w1': nrm((DEPTH, N_EXPERTS, D_MODEL, EXPERT_FF), D_MODEL ** -0.5),
        'moe_w3': nrm((DEPTH, N_EXPERTS, D_MODEL, EXPERT_FF), D_MODEL ** -0.5),
        'moe_w2': nrm((DEPTH, N_EXPERTS, EXPERT_FF, D_MODEL), DN_BETA * EXPERT_FF ** -0.5),
    }

def reference(x_prompt, x_sample, state_hgrn, state_ret, c, c_ctx, ada_w, ada_b, ln_g, ln_b,
              even_w_in, even_w_out, hgrn_lb, hgrn_norm_w, hyena_conv_w, hyena_conv_b,
              hyena_w1, hyena_b1, hyena_w2, hyena_b2, hyena_w3, hyena_freq, hyena_bias,
              odd_w_in, odd_w_out, ret_decay, moe_router, moe_w1, moe_w3, moe_w2):
    lb_soft = jax.nn.softmax(hgrn_lb.astype(F32), axis=0)
    lb_all = jnp.cumsum(lb_soft, axis=0) - lb_soft[0]

    def trunk(h, cond, latent, hgrn_cache, ret_cache):
        bn = h.shape[0]
        hgrn_states, ret_states = [], []
        for l in range(DEPTH):
            j = l // 2
            sh1, sc1, g1, sh2, sc2, g2 = modulation(cond, ada_w[l], ada_b[l])
            u = h * (1.0 + sc1) + sh1
            if l % 2 == 0:
                s0 = hgrn_cache[:, j] if latent else jnp.zeros((bn, 2, A_HEADS, A_HEAD_DIM, A_HEAD_DIM), F32)
                mix, s_new = even_mixer(u, s0, even_w_in[j], even_w_out[j], lb_all[j], hgrn_norm_w[j],
                                        hyena_conv_w[j], hyena_conv_b[j], hyena_w1[j], hyena_b1[j],
                                        hyena_w2[j], hyena_b2[j], hyena_w3[j], hyena_freq[j], hyena_bias[j])
                hgrn_states.append(s_new)
            else:
                s0 = ret_cache[:, j] if latent else jnp.zeros((bn, 2, C_HEADS, C_HEAD_DIM, C_HEAD_DIM), F32)
                mix, s_new = retention_mixer(u, s0, latent, odd_w_in[j], odd_w_out[j], ret_decay[j])
                ret_states.append(s_new)
            h = layer_norm(DN_ALPHA * h + g1 * mix, ln_g[l, 0], ln_b[l, 0])
            u = h * (1.0 + sc2) + sh2
            h = layer_norm(DN_ALPHA * h + g2 * ec_moe(u, moe_router[l], moe_w1[l], moe_w3[l], moe_w2[l]),
                           ln_g[l, 1], ln_b[l, 1])
        return h, hgrn_states, ret_states

    y_prompt, hs_p, rs_p = trunk(x_prompt, c_ctx, False, None, None)
    new_state_hgrn = jnp.stack(hs_p, axis=1).astype(x_prompt.dtype)
    new_state_ret = jnp.stack(rs_p, axis=1).astype(x_prompt.dtype)
    y_sample, _, _ = trunk(x_sample, c, True, state_hgrn, state_ret)
    return (y_prompt, y_sample, new_state_hgrn, new_state_ret)


_drawn_inputs = setup_inputs


def setup_inputs(seed=0):
    import zlib

    import numpy as np

    out = dict(_drawn_inputs(seed))
    spreads = {}
    factors = {'state_hgrn': 21.393,
     'state_ret': 3.368,
     'hgrn_norm_w': 25.674,
     'hyena_freq': 4.26,
     'hyena_conv_b': 4.633,
     'hyena_b2': 4.973}
    for name, (base, spread) in spreads.items():
        noise = np.random.default_rng([zlib.crc32(name.encode()), seed]).standard_normal(out[name].shape)
        drawn = base * np.exp(spread * noise) if base else spread * noise
        out[name] = __import__('jax').numpy.asarray(drawn.astype(out[name].dtype))
    for name, factor in factors.items():
        out[name] = (out[name] * factor).astype(out[name].dtype)
    return out
```

```python
import math
from contextlib import ExitStack

import numpy as np

import concourse.bass as bass
from concourse import mybir

F32 = mybir.dt.float32
U32 = mybir.dt.uint32
ALU = mybir.AluOpType
ACT = mybir.ActivationFunctionType
AX = mybir.AxisListType

P = 128
D = 1024
KD = D // P
L_LAT, L_CTX = 1024, 128
NL = L_LAT // P
NT = NL + L_CTX // P
TOK = NT * P
DEPTH = 2
ALPHA = (2 * DEPTH) ** 0.25
EPS = 1e-5
A_H = 4
C_H, C_HD = 4, 256
AW = 512
E_N, FF = 16, 1408
KF = FF // P
CAP_L, CAP_C = 2 * L_LAT // E_N, 2 * L_CTX // E_N
SLOTS = CAP_L + CAP_C
BIG = float(1.5 * 2 ** 23)
NCH = 3 * P
LOG_FLOOR = 40.0


class Chain:

    def __init__(self, eng, sem):
        self.eng, self.sem, self.n, self.base = eng, sem, 0, 0

    def mark(self, ins):
        ins.then_inc(self.sem, 1)
        self.n += 1
        return ins

    def wait(self):
        self.eng.wait_ge(self.sem, self.base + self.n)

    def link(self, ins):
        self.mark(ins)
        self.wait()

    def loop(self, count, per, body):
        start = self.n
        with self.eng.Fori(0, count, 1) as i:
            self.base = i * per
            body(i)
        assert self.n - start == per, (self.n - start, per)
        self.base = 0
        self.n = start + count * per


def shape_constants():
    c = {}
    c["ident"] = np.eye(P, dtype=np.float32)
    s, t = np.arange(P)[:, None], np.arange(P)[None, :]
    masks = [s == t]
    for d in range(2):
        for l in range(7):
            hs = 64 >> l
            a, b = (s, t) if d == 0 else (t, s)
            masks.append((a // (2 * hs) == b // (2 * hs)) & (a // hs % 2 == 0) & (b // hs % 2 == 1))
    c["gram_masks"] = np.stack(masks, 1).astype(np.float32)
    c["time_dist"] = np.stack([np.where(t >= s, t - s, 0), np.where(t >= s, 1, 0),
                               np.where(s >= t, s - t, 0), np.where(s >= t, 1, 0)], 1).astype(np.float32)
    for name, L in (("lat", L_LAT), ("ctx", L_CTX)):
        k = np.arange(L)[:, None].astype(np.float64)
        n = np.arange(L)[None, :].astype(np.float64)
        ang = np.pi * (2 * k + 1) * (2 * n + 1) / (4 * L)
        nt = L // P
        tile = lambda m: m.reshape(nt, P, -1).transpose(1, 0, 2).astype(np.float32)
        c[f"dft_{name}"] = np.stack([tile(np.cos(ang)), tile(np.sin(ang))], 1)
        half = np.pi * (2 * k[:, 0] + 1) / (4 * L)
        c[f"rot_{name}"] = np.stack([(np.cos(half) / L).reshape(nt, P).T,
                                     (np.sin(half) / L).reshape(nt, P).T], 1).astype(np.float32)
        tt = np.linspace(0.0, 1.0, L, dtype=np.float32)[:, None]
        bands = 16
        aa = np.float32(2.0 * math.pi / L) * np.arange(L, dtype=np.float32)[:, None] \
            * np.linspace(1e-4, bands - 1, bands, dtype=np.float32)[None, :]
        c[f"z_{name}"] = np.ascontiguousarray(np.concatenate([tt, np.cos(aa), -np.sin(aa)], -1).T.astype(np.float32))
        deltas = np.abs(np.linspace(math.log(1e-2) / 1.5, math.log(1e-2) / 0.3, 512, dtype=np.float32))
        dec = np.exp(-tt * deltas).astype(np.float32)
        nxt = np.concatenate([dec[1:], np.zeros((1, 512), np.float32)])
        both = np.stack([dec, nxt], 1).reshape(nt, P, 2, 2, 256)
        c[f"decay_{name}"] = np.ascontiguousarray(both.transpose(3, 0, 1, 2, 4))
    quarter = 64
    inv = (10000.0 ** (-np.arange(quarter, dtype=np.float32) / np.float32(quarter))).astype(np.float32)
    pos = np.stack([np.arange(L_LAT) // 64, np.arange(L_LAT) % 64], 1).astype(np.float32)
    a = pos[:, :, None] * inv
    tr = lambda m: m.reshape(NL, P, 128).transpose(1, 0, 2).astype(np.float32)
    c["rope"] = np.stack([tr(np.cos(a)), tr(np.sin(a))], 1)
    c["slot_iota"] = np.broadcast_to(np.arange(P, dtype=np.float32), (P, P)).copy()
    r = np.arange(P, dtype=np.float32)
    c["pos_rows"] = np.broadcast_to(np.stack([r + 1, P - r]), (P, 2, P)).astype(np.float32).copy()
    c["pos_cols"] = np.stack([P - 1 - r, r], 1).astype(np.float32)
    return c


CONST = shape_constants()


def build(nc, I, O):
    ctx = ExitStack()
    with ctx:
        taken = {}

        def sem(name):
            if name not in taken:
                taken[name] = ctx.enter_context(nc.semaphore(name))
            return taken[name]

        WORDS = 53100
        arena = ctx.enter_context(nc.sbuf_tensor("arena", [P, WORDS], F32))
        PS = ctx.enter_context(nc.psum_tensor("PS", [P, 8, 512], F32))
        modD = nc.dram_tensor("mod_rows", (DEPTH, 2, 6 * D), F32, kind="Internal").ap()
        hD = nc.dram_tensor("h_rows", (TOK, D), F32, kind="Internal").ap()

        def at(off, *dims, parts=P):
            n = int(np.prod(dims))
            assert off + n <= WORDS, (off, dims)
            v = arena[0:parts, off:off + n]
            if len(dims) == 2:
                v = v.rearrange("p (a b) -> p a b", a=dims[0])
            elif len(dims) == 3:
                v = v.rearrange("p (a b c) -> p a b c", a=dims[0], b=dims[1])
            elif len(dims) == 4:
                v = v.rearrange("p (a b c d) -> p a b c d", a=dims[0], b=dims[1], c=dims[2])
            return v

        top = WORDS
        top -= 128
        ident = at(top, P)
        top -= 16
        condT = at(top, 2, KD)
        top -= 64
        modc = at(top, 4, KD, 2)
        top -= 64
        small = at(top, 64)
        FREE = top

        stage_done = sem("stage_done")
        n_stage = {}
        dve_seq, act_seq = sem("dve_seq"), sem("act_seq")

        def stage_end(eng, name):
            n_stage[name] = n_stage.get(name, 0) + 1
            eng.drain().then_inc(stage_done, 1)
            eng.wait_ge(stage_done, 4 * n_stage[name])

        def rows_of(t, l):
            if l:
                return hD[t * P:(t + 1) * P, :]
            return I["x_sample"][0, t * P:(t + 1) * P, :] if t < NL else I["x_prompt"][0, :, :]

        class Modulation:
            def __init__(s, l):
                s.l = l
                s.raw = at(0, P, parts=16)
                s.silu = at(128, P, parts=16)
                s.bias = at(256, 6 * D, parts=2)
                s.row = at(256 + 6 * D, 6 * D, parts=2)
                s.W = [at(256 + 12 * D + b * 4096, KD, 512) for b in range(4)]
                s.ld, s.wl = sem(f"mod_small_in"), [sem(f"mod_w_in_{b}") for b in range(4)]
                s.full, s.evac = sem(f"mod_full"), sem(f"mod_evac")
                s.cond, s.condps, s.st = sem(f"mod_cond"), sem(f"mod_cond_t"), sem(f"mod_store")
                s.colf = sem(f"mod_col_full")

            def sync(s, sp):
                l = s.l
                if l == 0:
                    sp.dma_start(ident, I["ident"]).then_inc(s.ld, 16)
                    sp.dma_start(s.raw[0:8, :], I["c"][0, :].rearrange("(k p) -> k p", p=P)).then_inc(s.ld, 16)
                    sp.dma_start(s.raw[8:16, :], I["c_ctx"].rearrange("(k p) -> k p", p=P)).then_inc(s.ld, 16)
                for c in range(2):
                    sp.dma_start(s.bias[c:c + 1, :], I["ada_b"][l:l + 1, :]).then_inc(s.ld, 16)
                for n in range(12):
                    if n >= 4:
                        sp.wait_ge(s.full, n - 3)
                    sp.dma_start(s.W[n % 4], I["ada_w"][l, :, n * 512:(n + 1) * 512]
                                 .rearrange("(k p) n -> p k n", p=P)).then_inc(s.wl[n % 4], 16)
                sp.wait_ge(s.evac, 12)
                sp.dma_start(modD[l], s.row).then_inc(s.st, 16)
                sp.wait_ge(s.st, 16)

            def pe(s, pe):
                if s.l == 0:
                    pe.wait_ge(s.cond, 1)
                    pe.transpose(PS[:, 7, 0:16], s.silu, ident[0:16, 0:16]).then_inc(s.condps, 1)
                    pe.wait_ge(s.cond, 2)
                for n in range(12):
                    pe.wait_ge(s.wl[n % 4], 16 * (n // 4 + 1))
                    if n >= 4:
                        pe.wait_ge(s.evac, n - 3)
                    for k in range(KD):
                        m = pe.matmul(PS[0:2, n % 4, :], condT[:, :, k], s.W[n % 4][:, k, :], start=k == 0, stop=k == KD - 1)
                    m.then_inc(s.full, 1)
                pe.wait_ge(s.evac, 12)
                for i, kind in enumerate((0, 1, 3, 4)):
                    for k in range(KD):
                        j = kind * KD + k
                        m = pe.transpose(PS[:, 6, (i * KD + k) * 2:(i * KD + k) * 2 + 2], s.row[:, j * P:(j + 1) * P],
                                         ident[0:2, 0:2])
                m.then_inc(s.colf, 1)

            def act(s, act, ch):
                if s.l == 0:
                    act.wait_ge(s.ld, 80)
                    act.activation(s.silu, s.raw, ACT.Silu).then_inc(s.cond, 1)
                    act.wait_ge(s.condps, 1)
                    act.copy(condT.rearrange("p a b -> p (a b)"), PS[:, 7, 0:16]).then_inc(s.cond, 1)

            def dve(s, dve, ch):
                dve.wait_ge(s.ld, 32 if s.l else 80)
                for n in range(12):
                    dve.wait_ge(s.full, n + 1)
                    dve.tensor_tensor(s.row[:, n * 512:(n + 1) * 512], PS[0:2, n % 4, :],
                                      s.bias[:, n * 512:(n + 1) * 512], ALU.add).then_inc(s.evac, 1)
                dve.wait_ge(s.colf, 1)
                ch.link(dve.tensor_copy(modc.rearrange("p a b c -> p (a b c)"), PS[:, 6, 0:64]))
                for kind in (1, 3):
                    v = modc[:, kind, :, :].rearrange("p a b -> p (a b)")
                    ch.link(dve.tensor_scalar(v, v, 1.0, None, ALU.add))

        def modulate_tile(eng, out, psum, kind, k, lat, act):
            g = 0 if lat else 1
            sc, sh = modc[:, kind + 1, k, g:g + 1], modc[:, kind, k, g:g + 1]
            if act:
                return eng.activation(out, psum, ACT.Identity, bias=sh, scale=sc)
            return eng.tensor_scalar(out, psum, sc, sh, ALU.mult, ALU.add)

        class MixerInput:
            def __init__(s, l, uT, scratch):
                s.l, s.uT = l, uT
                s.x = [at(scratch + b * D, D) for b in range(3)]
                s.ld = [sem(f"u_in_{b}") for b in range(3)]
                s.full, s.ea, s.ed = sem(f"u_full"), sem(f"u_evac_act"), sem(f"u_evac_dve")

            def sync(s, sp):
                for t in range(NT):
                    if t >= 3:
                        sp.wait_ge(s.full, t - 2)
                    sp.dma_start(s.x[t % 3], rows_of(t, s.l)).then_inc(s.ld[t % 3], 16)

            def pe(s, pe):
                for t in range(NT):
                    pe.wait_ge(s.ld[t % 3], 16 * (t // 3 + 1))
                    if t >= 2:
                        pe.wait_ge(s.ea, t - 1)
                        pe.wait_ge(s.ed, t - 1)
                    for k in range(KD):
                        m = pe.transpose(PS[:, t % 2 * 2 + k // 4, k % 4 * P:k % 4 * P + P],
                                         s.x[t % 3][:, k * P:(k + 1) * P], ident)
                    m.then_inc(s.full, 1)

            def evac(s, eng, bank, sm):
                for t in range(NT):
                    eng.wait_ge(s.full, t + 1)
                    for k in range(bank * 4, bank * 4 + 4):
                        m = modulate_tile(eng, s.uT[:, k, t * P:(t + 1) * P],
                                          PS[:, t % 2 * 2 + bank, k % 4 * P:k % 4 * P + P], 0, k, t < NL, bank == 0)
                    m.then_inc(sm, 1)

            def act(s, act, ch):
                s.evac(act, 0, s.ea)

            def dve(s, dve, ch):
                s.evac(dve, 1, s.ed)

        JOBS = ["q", "zf", "zb", "vg0", "vg1", "vg2", "diag"] + [f"lev{d}{l}" for d in range(2) for l in range(7)] \
            + ["tk0", "tk1", "U0", "U1", "o", "yt"]
        BY_ACT = [j for j in JOBS if j[0] in "qzv" or j[:2] in ("tk", "yt") or j == "o"]
        BY_DVE = [j for j in JOBS if j not in BY_ACT]

        class Hgrn:
            def __init__(s, uT, yT, a, b):
                s.uT, s.yT = uT, yT
                o = [a, b]

                def take(n, which=0):
                    r = o[which]
                    o[which] += n
                    return r
                s.W = at(take(5 * 1024), 5, KD, P)
                s.qT = at(take(TOK), NT, P)
                s.z = [at(take(TOK), NT, P) for _ in range(2)]
                s.kT = [at(take(TOK), NT, P) for _ in range(2)]
                s.f = [at(take(TOK), NT, P) for _ in range(2)]
                s.X = [at(take(NT * 129), NT, 129) for _ in range(2)]
                s.v = at(take(TOK), NT, P)
                s.g = at(take(TOK), NT, P)
                s.dist = [at(take(TOK), NT, P) for _ in range(2)]
                s.G = [at(take(TOK), NT, P) for _ in range(2)]
                s.attn = at(take(TOK, 1), NT, P)
                s.ks = [at(take(TOK, 1), NT, P) for _ in range(2)]
                s.S = [at(take(TOK, 1), NT, P) for _ in range(2)]
                s.masks = at(take(15 * P, 1), 15, P)
                s.eT = [at(take(NT, 1), NT) for _ in range(2)]
                s.nw = at(take(AW, 1), AW)
                s.ss = at(take(2 * NT, 1), 2, NT)
                s.ones = at(take(P, 1), P)
                assert o[0] <= 33792 and o[1] <= FREE, o
                s.Aq, s.Bk = s.z, s.f
                s.o, s.ksum = s.G[0], s.dist[0]
                s.wld, s.wfree = sem("hg_w_in"), sem("hg_w_free")
                s.cld, s.s0 = sem("hg_const_in"), sem("hg_s0_in")
                s.full, s.ea, s.ed = sem("hg_full"), sem("hg_evac_act"), sem("hg_evac_dve")
                s.floor, s.ln, s.prep = sem("hg_floor"), sem("hg_ln"), sem("hg_prep")
                s.dd, s.ex, s.gg = sem("hg_dist"), sem("hg_exp"), sem("hg_scaled")
                s.sok, s.sv = sem("hg_states"), sem("hg_state_out")
                s.ssum, s.rt, s.yok = sem("hg_sumsq"), sem("hg_sqrt"), sem("hg_y")

            def free_count(s, eng, job, h):
                n = JOBS.index(job)
                p = n - 2
                if p < 0:
                    if h == 0:
                        return
                    h, p = h - 1, len(JOBS) - 1 - n
                prev = JOBS[p]
                if prev in BY_ACT:
                    eng.wait_ge(s.ea, h * len(BY_ACT) + BY_ACT.index(prev) + 1)
                else:
                    eng.wait_ge(s.ed, h * len(BY_DVE) + BY_DVE.index(prev) + 1)

            def banks(s, job):
                g = JOBS.index(job) % 2 * 3
                return PS[:, g:g + 3, :]

            def wait_full(s, eng, job, h):
                eng.wait_ge(s.full, h * len(JOBS) + JOBS.index(job) + 1)

            def wait_act(s, eng, job, h):
                eng.wait_ge(s.ea, h * len(BY_ACT) + BY_ACT.index(job) + 1)

            def sync(s, sp):
                sp.dma_start(s.masks, I["gram_masks"]).then_inc(s.cld, 16)
                nw = I["hgrn_norm_w"][0:1, :]
                sp.dma_start(s.nw, nw.to_broadcast((P, AW))).then_inc(s.cld, 16)
                for h in range(A_H):
                    if h:
                        sp.wait_ge(s.full, (h - 1) * len(JOBS) + JOBS.index("vg2") + 1)
                    for j, part in enumerate((0, 2, 3, 1, 4)):
                        c0 = part * AW + h * P
                        sp.dma_start(s.W[:, j, :, :], I["even_w_in"][0, :, c0:c0 + P]
                                     .rearrange("(k p) n -> p k n", p=P)).then_inc(s.wld, 16)
                    if h:
                        sp.wait_ge(s.full, (h - 1) * len(JOBS) + JOBS.index("o") + 1)
                        sp.wait_ge(s.sv, 32 * h)
                    for d in range(2):
                        sp.dma_start(s.S[d][:, 0 if d == 0 else NL - 1, :], I["state_hgrn"][0, 0, d, h]).then_inc(s.s0, 16)
                    sp.wait_ge(s.sok, 2 * h + 2)
                    for d in range(2):
                        sp.dma_start(O["new_state_hgrn"][0, 0, d, h], s.S[d][:, NL, :]).then_inc(s.sv, 16)
                sp.wait_ge(s.sv, 32 * A_H)

            def pe(s, pe):
                for h in range(A_H):
                    pe.wait_ge(s.wld, 80 * (h + 1))
                    for j, job in enumerate(("q", "zf", "zb")):
                        s.free_count(pe, job, h)
                        ps = s.banks(job)
                        for n in range(3):
                            for k in range(KD):
                                m = pe.matmul(ps[:, n, 0:NCH], s.W[:, j, k, :], s.uT[:, k, n * NCH:(n + 1) * NCH],
                                              start=k == 0, stop=k == KD - 1)
                        m.then_inc(s.full, 1)
                    for j in range(3):
                        job = f"vg{j}"
                        s.free_count(pe, job, h)
                        ps = s.banks(job)
                        for n in range(3):
                            t = 3 * j + n
                            for k in range(KD):
                                m = pe.matmul(ps[:, n, 0:256], s.uT[:, k, t * P:(t + 1) * P], s.W[:, 3:5, k, :],
                                              start=k == 0, stop=k == KD - 1)
                        m.then_inc(s.full, 1)
                    s.free_count(pe, "diag", h)
                    s.wait_act(pe, "vg2", h)
                    pe.wait_ge(s.prep, h + 1)
                    ps = s.banks("diag")
                    for c in range(NT):
                        m = pe.matmul(ps[:, c // 3, c % 3 * P:c % 3 * P + P], s.ksum[:, c, :], s.qT[:, c, :])
                    m.then_inc(s.full, 1)
                    for n in range(14):
                        job = f"lev{n // 7}{n % 7}"
                        s.free_count(pe, job, h)
                        pe.wait_ge(s.gg, h * 18 + n + 1)
                        ps = s.banks(job)
                        for c in range(NT):
                            g = s.G[n % 2][:, c, :]
                            m = pe.matmul(ps[:, c // 3, c % 3 * P:c % 3 * P + P], g, g)
                        m.then_inc(s.full, 1)
                    for d in range(2):
                        s.free_count(pe, f"tk{d}", h)
                        pe.wait_ge(s.gg, h * 18 + 14 + 2 * d + 2)
                        ps = s.banks(f"tk{d}")
                        for c in range(NT):
                            m = pe.transpose(ps[:, c // 3, c % 3 * P:c % 3 * P + P], s.Bk[d][:, c, :], ident)
                        m.then_inc(s.full, 1)
                    for d in range(2):
                        s.free_count(pe, f"U{d}", h)
                        s.wait_act(pe, f"tk{d}", h)
                        ps = s.banks(f"U{d}")
                        for c in range(NT):
                            m = pe.matmul(ps[:, c // 3, c % 3 * P:c % 3 * P + P], s.ks[d][:, c, :], s.v[:, c, :])
                        m.then_inc(s.full, 1)
                    s.free_count(pe, "o", h)
                    pe.wait_ge(s.sok, 2 * h + 2)
                    ps = s.banks("o")
                    for c in range(NT):
                        out = ps[:, c // 3, c % 3 * P:c % 3 * P + P]
                        m = pe.matmul(out, s.attn[:, c, :], s.v[:, c, :], start=True, stop=c == NL)
                        if c < NL:
                            for d in range(2):
                                m = pe.matmul(out, s.Aq[d][:, c, :], s.S[d][:, c, :], start=False, stop=d == 1)
                    m.then_inc(s.full, 1)
                    s.free_count(pe, "yt", h)
                    pe.wait_ge(s.yok, h + 1)
                    ps = s.banks("yt")
                    for c in range(NT):
                        m = pe.transpose(ps[:, c // 3, c % 3 * P:c % 3 * P + P], s.o[:, c, :], ident)
                    m.then_inc(s.full, 1)

            def act(s, act, ch):
                third = lambda v, n: v[:, 3 * n:3 * n + 3, :]
                ps3 = lambda ps, n: ps[:, n, 0:NCH].rearrange("p (a b) -> p a b", a=3)
                for h in range(A_H):
                    s.wait_full(act, "q", h)
                    for n in range(3):
                        m = act.activation(third(s.qT, n), ps3(s.banks("q"), n), ACT.Silu)
                    m.then_inc(s.ea, 1)
                    for d, job in enumerate(("zf", "zb")):
                        s.wait_full(act, job, h)
                        for n in range(3):
                            m = act.copy(third(s.z[d], n), ps3(s.banks(job), n))
                        m.then_inc(s.ea, 1)
                    for j in range(3):
                        s.wait_full(act, f"vg{j}", h)
                        ps = s.banks(f"vg{j}")[:, :, 0:256].rearrange("p a (b c) -> p a b c", b=2)
                        act.activation(third(s.g, j), ps[:, :, 1, :], ACT.Silu)
                        act.copy(third(s.v, j), ps[:, :, 0, :]).then_inc(s.ea, 1)
                    for d in range(2):
                        s.wait_act(act, ("zf", "zb")[d], h)
                        act.activation(s.kT[d], s.z[d], ACT.Sigmoid, scale=-1.0)
                        act.activation(s.f[d], s.z[d], ACT.Sigmoid).then_inc(s.floor, 1)
                    for d in range(2):
                        act.wait_ge(s.ln, h * 4 + d + 1)
                        act.activation(s.f[d], s.f[d], ACT.Ln).then_inc(s.floor, 1)
                    for n in range(14):
                        act.wait_ge(s.dd, h * 16 + n + 1)
                        act.activation(s.dist[n % 2], s.dist[n % 2], ACT.Exp).then_inc(s.ex, 1)
                    for d in range(2):
                        act.wait_ge(s.dd, h * 16 + 14 + d + 1)
                        x = s.X[d][:, :, 1 - d:129 - d]
                        act.activation(s.dist[0], s.dist[0], ACT.Exp)
                        act.activation(s.dist[1], x, ACT.Exp)
                        act.activation(s.eT[d], s.X[d][:, :, 128], ACT.Exp).then_inc(s.ex, 1)
                    for d in range(2):
                        s.wait_full(act, f"tk{d}", h)
                        for n in range(3):
                            m = act.copy(third(s.ks[d], n), ps3(s.banks(f"tk{d}"), n))
                        m.then_inc(s.ea, 1)
                    s.wait_full(act, "o", h)
                    for n in range(3):
                        m = act.copy(third(s.o, n), ps3(s.banks("o"), n))
                    m.then_inc(s.ea, 1)
                    act.wait_ge(s.ssum, h + 1)
                    act.activation(s.ss[:, 1, :], s.ss[:, 0, :], ACT.Sqrt).then_inc(s.rt, 1)
                    s.wait_full(act, "yt", h)
                    for n in range(3):
                        m = act.copy(s.yT[:, h, n * NCH:(n + 1) * NCH], s.banks("yt")[:, n, 0:NCH])
                    m.then_inc(s.ea, 1)

            def dve(s, dve, ch):
                ch.link(dve.memset(s.ones, 1.0))
                for d in range(2):
                    ch.link(dve.memset(s.X[d][:, :, 0:1], 0.0))
                dve.wait_ge(s.cld, 32)
                ch.link(dve.memset(s.attn, 0.0))
                for h in range(A_H):
                    for d in range(2):
                        dve.wait_ge(s.floor, h * 4 + d + 1)
                        dve.tensor_scalar(s.z[d], s.z[d], LOG_FLOOR, 0.0, ALU.add, ALU.min)
                        dve.tensor_scalar(s.f[d], s.f[d], math.exp(-LOG_FLOOR), None, ALU.max).then_inc(s.ln, 1)
                    for d in range(2):
                        dve.wait_ge(s.floor, h * 4 + 3 + d)
                        ch.link(dve.scalar_tensor_tensor(s.z[d], s.z[d], math.log(1e-30) + LOG_FLOOR, s.f[d],
                                                         ALU.max, ALU.add))
                        for c in range(NT):
                            m = dve.tensor_tensor_scan(s.X[d][:, c, 1:129], s.ones, s.z[d][:, c, :], 0.0, ALU.mult, ALU.add)
                        m.then_inc(s.ln, 1)
                    if h:
                        s.wait_full(dve, "yt", h - 1)
                    dve.tensor_tensor(s.ksum, s.kT[0], s.kT[1], ALU.add).then_inc(s.prep, 1)
                    s.wait_full(dve, "diag", h)
                    s.dve_keep(dve, h, "diag", 0)
                    dve.wait_ge(s.ln, h * 4 + 4)
                    for n in range(15):
                        if n < 14:
                            s.level_dist(dve, h, n)
                        if n > 0:
                            s.level_scale(dve, h, n - 1)
                            if n > 1:
                                job = f"lev{(n - 2) // 7}{(n - 2) % 7}"
                                s.wait_full(dve, job, h)
                                s.dve_keep(dve, h, job, n - 1)
                    s.wait_full(dve, "lev16", h)
                    s.dve_keep(dve, h, "lev16", 14)
                    for d in range(2):
                        x = s.X[d][:, :, 1 - d:129 - d]
                        tot = s.X[d][:, :, 128:129].to_broadcast((P, NT, P))
                        if d:
                            dve.wait_ge(s.gg, h * 18 + 16)
                        dve.tensor_tensor(s.dist[0], tot, x, ALU.subtract).then_inc(s.dd, 1)
                        dve.wait_ge(s.ex, h * 16 + 14 + d + 1)
                        to_end, from_start = (0, 1) if d == 0 else (1, 0)
                        dve.tensor_tensor(s.Aq[d], s.qT, s.dist[from_start], ALU.mult).then_inc(s.gg, 1)
                        dve.tensor_tensor(s.Bk[d], s.kT[d], s.dist[to_end], ALU.mult).then_inc(s.gg, 1)
                    dve.wait_ge(s.s0, 32 * (h + 1))
                    for d in range(2):
                        s.wait_full(dve, f"U{d}", h)
                        ps = s.banks(f"U{d}")
                        U = lambda c: ps[:, c // 3, c % 3 * P:c % 3 * P + P]
                        order = range(NL - 1) if d == 0 else range(NL - 1, 0, -1)
                        for c in order:
                            nxt = c + 1 if d == 0 else c - 1
                            ch.link(dve.scalar_tensor_tensor(s.S[d][:, nxt, :], s.S[d][:, c, :], s.eT[d][:, c:c + 1], U(c),
                                                             ALU.mult, ALU.add))
                        ch.link(dve.tensor_copy(s.S[d][:, NL, :], U(NL)))
                        dve.engine_nop().then_inc(s.sok, 1)
                        dve.engine_nop().then_inc(s.ed, 1)
                    s.wait_act(dve, "o", h)
                    ch.link(dve.tensor_tensor(s.G[1], s.o, s.o, ALU.mult))
                    ch.link(dve.tensor_reduce(s.ss[:, 0, :], s.G[1], AX.X, ALU.add))
                    dve.tensor_scalar(s.ss[:, 0, :], s.ss[:, 0, :], 1.0 / P, EPS, ALU.mult, ALU.add).then_inc(s.ssum, 1)
                    dve.wait_ge(s.rt, h + 1)
                    ch.link(dve.reciprocal(s.ss[:, 1, :], s.ss[:, 1, :]))
                    rstd = s.ss[:, 1, :].rearrange("p (a b) -> p a b", b=1).to_broadcast((P, NT, P))
                    nw = s.nw[:, h * P:(h + 1) * P].rearrange("p (a b) -> p a b", a=1).to_broadcast((P, NT, P))
                    ch.link(dve.tensor_tensor(s.o, s.o, rstd, ALU.mult))
                    ch.link(dve.tensor_tensor(s.o, s.o, nw, ALU.mult))
                    dve.tensor_tensor(s.o, s.o, s.g, ALU.mult).then_inc(s.yok, 1)

            def dve_keep(s, dve, h, job, mask):
                if h and job == "diag":
                    s.wait_full(dve, "o", h - 1)
                if job != "diag":
                    dve.wait_ge(s.ed, h * len(BY_DVE) + BY_DVE.index(job))
                for n in range(3):
                    m = dve.copy_predicated(s.attn[:, 3 * n:3 * n + 3, :],
                                            s.masks[:, mask:mask + 1, :].bitcast(U32).to_broadcast((P, 3, P)),
                                            s.banks(job)[:, n, 0:NCH].rearrange("p (a b) -> p a b", a=3))
                m.then_inc(s.ed, 1)

            def halves(s, v, hs):
                w = v.rearrange("p c (b two s) -> p c b two s", two=2, s=hs)
                return w[:, :, :, 0, :], w[:, :, :, 1, :]

            def level_dist(s, dve, h, n):
                d, hs = n // 7, 64 >> (n % 7)
                nb = 64 // hs
                first, second = s.halves(s.X[d][:, :, 1 - d:129 - d], hs)
                o1, o2 = s.halves(s.dist[n % 2], hs)
                ref = s.X[d][:, :, 0:128].rearrange("p c (b s) -> p c b s", s=2 * hs)[:, :, :, hs:hs + 1] \
                    .to_broadcast((P, NT, nb, hs))
                if n >= 2:
                    dve.wait_ge(s.gg, h * 18 + n - 1)
                else:
                    s.wait_full(dve, "diag", h)
                dve.tensor_tensor(o1, ref, first, ALU.subtract)
                dve.tensor_tensor(o2, second, ref, ALU.subtract).then_inc(s.dd, 1)

            def level_scale(s, dve, h, n):
                d, hs = n // 7, 64 >> (n % 7)
                dve.wait_ge(s.ex, h * 16 + n + 1)
                if n >= 2:
                    s.wait_full(dve, f"lev{(n - 2) // 7}{(n - 2) % 7}", h)
                e1, e2 = s.halves(s.dist[n % 2], hs)
                g1, g2 = s.halves(s.G[n % 2], hs)
                q1, q2 = s.halves(s.qT, hs)
                k1, k2 = s.halves(s.kT[d], hs)
                a, b = (k1, q2) if d == 0 else (q1, k2)
                dve.tensor_tensor(g1, e1, a, ALU.mult)
                dve.tensor_tensor(g2, e2, b, ALU.mult).then_inc(s.gg, 1)

        class HyenaIn:
            def __init__(s, uT, base, hv, hx1, yT):
                s.uT, s.hv, s.hx1, s.yT = uT, hv, hx1, yT
                s.W = [at(base + b * 1024, KD, P) for b in range(2)]
                s.raw = [at(base + 2048 + b * 1156, 1155) for b in range(2)]
                s.y = [at(base + 2048 + 2312 + b * 1156, 1153) for b in range(2)]
                s.cw = at(base + 7000, P, parts=48)
                s.cols = at(base + 7200, 4, 12)
                s.wl = [sem(f"hyi_w_in{b}") for b in range(2)]
                s.cl, s.ct, s.cok = sem("hyi_conv_in"), sem("hyi_conv_t"), sem("hyi_conv_cols")
                s.pads = sem("hyi_pads")
                s.full, s.evac, s.conv = sem("hyi_full"), sem("hyi_evac"), sem("hyi_conv")
                s.tfull, s.tevac = sem("hyi_t_full"), sem("hyi_t_evac")

            def sync(s, sp):
                sp.dma_start(s.cw[0:36, :], I["hyena_conv_w"][0].rearrange("j (c p) -> (j c) p", p=P)).then_inc(s.cl, 16)
                sp.dma_start(s.cw[36:48, :], I["hyena_conv_b"][0].rearrange("(c p) -> c p", p=P)).then_inc(s.cl, 16)
                for c in range(12):
                    if c >= 2:
                        sp.wait_ge(s.full, c - 1)
                    c0 = 5 * AW + c * P
                    sp.dma_start(s.W[c % 2], I["even_w_in"][0, :, c0:c0 + P]
                                 .rearrange("(k p) n -> p k n", p=P)).then_inc(s.wl[c % 2], 16)

            def pe(s, pe):
                pe.wait_ge(s.cl, 32)
                pe.transpose(PS[:, 7, 0:48], s.cw, ident[0:48, 0:48]).then_inc(s.ct, 1)

                def turn(c):
                    pe.wait_ge(s.conv, c + 1)
                    if c:
                        pe.wait_ge(s.tevac, c)
                    for t in range(NT):
                        src = s.y[c % 2][:, t * P + t // NL:t * P + t // NL + P]
                        m = pe.transpose(PS[:, 3 + t // 3, t % 3 * P:t % 3 * P + P], src, ident)
                    m.then_inc(s.tfull, 1)
                for c in range(12):
                    pe.wait_ge(s.wl[c % 2], 16 * (c // 2 + 1))
                    if c:
                        pe.wait_ge(s.evac, c)
                    for n in range(3):
                        for k in range(KD):
                            m = pe.matmul(PS[:, n, 0:NCH], s.W[c % 2][:, k, :], s.uT[:, k, n * NCH:(n + 1) * NCH],
                                          start=k == 0, stop=k == KD - 1)
                    m.then_inc(s.full, 1)
                    if 0 < c <= 8:
                        turn(c - 1)

            def act(s, act, ch):
                act.wait_ge(s.pads, 1)
                for c in range(12):
                    act.wait_ge(s.full, c + 1)
                    if c >= 2:
                        act.wait_ge(s.conv, c - 1)
                    raw = s.raw[c % 2]
                    act.copy(raw[:, 1:385], PS[:, 0, 0:NCH])
                    act.copy(raw[:, 385:769], PS[:, 1, 0:NCH])
                    act.copy(raw[:, 769:1025], PS[:, 2, 0:256])
                    act.copy(raw[:, 1026:1154], PS[:, 2, 256:384]).then_inc(s.evac, 1)
                    if 0 < c <= 8:
                        s.act_turn(act, c - 1)

            def act_turn(s, act, c):
                act.wait_ge(s.tfull, c + 1)
                dst = s.hv if c < 4 else s.hx1
                for n in range(3):
                    m = act.copy(dst[:, 3 * n:3 * n + 3, c % 4 * P:c % 4 * P + P],
                                 PS[:, 3 + n, 0:NCH].rearrange("p (a b) -> p a b", a=3))
                m.then_inc(s.tevac, 1)

            def dve(s, dve, ch):
                for b in range(2):
                    dve.memset(s.raw[b][:, 0:1], 0.0)
                    dve.memset(s.raw[b][:, 1025:1026], 0.0)
                    m = dve.memset(s.raw[b][:, 1154:1155], 0.0)
                m.then_inc(s.pads, 1)
                dve.wait_ge(s.ct, 1)
                ch.link(dve.tensor_copy(s.cols.rearrange("p a b -> p (a b)"), PS[:, 7, 0:48]))
                for c in range(12):
                    raw, y = s.raw[c % 2], s.y[c % 2]
                    dve.wait_ge(s.evac, c + 1)
                    if c >= 2 and c <= 9:
                        dve.wait_ge(s.tfull, c - 1)
                    w = [s.cols[:, j, c:c + 1] for j in range(4)]
                    ch.link(dve.tensor_scalar(y, raw[:, 0:1153], w[0], w[3], ALU.mult, ALU.add))
                    ch.link(dve.scalar_tensor_tensor(y, raw[:, 1:1154], w[1], y, ALU.mult, ALU.add))
                    if c < 8:
                        dve.scalar_tensor_tensor(y, raw[:, 2:1155], w[2], y, ALU.mult, ALU.add).then_inc(s.conv, 1)
                    else:
                        o = s.yT[:, c - 4, :]
                        dve.scalar_tensor_tensor(o[:, 0:1024], raw[:, 2:1026], w[2], y[:, 0:1024], ALU.mult, ALU.add)
                        dve.scalar_tensor_tensor(o[:, 1024:1152], raw[:, 1027:1155], w[2], y[:, 1025:1153],
                                                 ALU.mult, ALU.add).then_inc(s.conv, 1)

        class HyenaConv:

            def __init__(s, name, hv, hx1, yT, dft, hbase, scratch):
                s.name, s.hv, s.hx1, s.yT = name, hv, hx1, yT
                s.L = L_LAT if name == "lat" else L_CTX
                s.nt = s.L // P
                s.t0 = 0 if name == "lat" else NL
                s.tw = min(s.L, 512)
                nt = s.nt
                s.C, s.S = dft[:, 0], dft[:, 1]
                s.dft = dft
                s.Hr, s.Hi = at(hbase, nt, 256), at(hbase + nt * 256, nt, 256)
                s.A, s.B = at(hbase + nt * 512, nt, 256), at(hbase + nt * 768, nt, 256)
                o = scratch
                s.hdn = at(o, s.L + 1, parts=64)
                s.arg = at(o + 1026, s.L, parts=64)
                s.rnd = at(o + 2052, s.L, parts=64)
                s.dec = [at(o + 1026 + b * 512, 2, 256) for b in range(2)]
                s.tmp = [at(o + 2050 + b * 256, 256) for b in range(4)]
                s.drow = at(o + 3078, 2, 512, parts=1)
                s.z = at(o + 4102, L_LAT, parts=33)[:, 0:s.L]
                s.w3 = at(o + 4102 + 1024, 2, 2, 512, parts=64)
                s.w1, s.w2 = at(o + 7174, 64, parts=33), at(o + 7238, 64, parts=64)
                s.v4 = at(o + 7302, 64, parts=4)
                s.c4 = at(o + 7366, 4, parts=64)
                s.rot = at(o + 7370, 2, nt)
                sm = lambda n: sem(f"hy_{n}")
                s.ld, s.dl = sm("in"), [sm("decay_in0"), sm("decay_in1")]
                s.full, s.hok = sm("mlp_full"), sm("mlp_ok")
                s.a1, s.sn = sm("arg"), sm("sin")
                s.ff, s.fe = sm("filt_full"), sm("filt_evac")
                s.pf, s.pe_ = sm("spec_full"), sm("spec_evac")
                s.uf, s.ue = sm("fwd_full"), sm("fwd_evac")
                s.yf, s.ye = sm("inv_full"), sm("inv_evac")

            def sync(s, sp):
                n = s.name
                for dst, src in ((s.dft, I[f"dft_{n}"]), (s.rot, I[f"rot_{n}"]), (s.z, I[f"z_{n}"]),
                                 (s.w1, I["hyena_w1"][0]), (s.w2, I["hyena_w2"][0]),
                                 (s.w3, I["hyena_w3"][0].rearrange("h (o d c) -> h o d c", o=2, d=2)),
                                 (s.drow, I["hyena_bias"][0:1]),
                                 (s.v4[0:1, :], I["hyena_b1"][0:1, :]), (s.v4[1:2, :], I["hyena_b2"][0:1, :]),
                                 (s.v4[2:4, :], I["hyena_freq"][0])):
                    sp.dma_start(dst, src).then_inc(s.ld, 16)
                for r in range(4):
                    for j in range(s.nt):
                        i = r * s.nt + j
                        if i >= 2:
                            sp.wait_ge(s.fe, i - 1)
                        else:
                            sp.wait_ge(s.hok, 3)
                        sp.dma_start(s.dec[i % 2], I[f"decay_{n}"][r // 2, j]).then_inc(s.dl[i % 2], 16)

            def pe(s, pe):
                pe.wait_ge(s.ld, 160)
                pe.transpose(PS[0:64, 7, 0:4], s.v4, ident[0:4, 0:4]).then_inc(s.full, 1)
                nw = s.L // s.tw
                for layer in range(2):
                    if layer:
                        pe.wait_ge(s.hok, 2)
                    for n in range(nw):
                        sl = slice(n * s.tw, (n + 1) * s.tw)
                        lhs, rhs = (s.w2, s.hdn[:, sl]) if layer else (s.w1, s.z[:, sl])
                        m = pe.matmul(PS[0:64, n + 2 * layer, 0:s.tw], lhs, rhs, start=True, stop=True)
                    m.then_inc(s.full, 1)
                pe.wait_ge(s.hok, 3)
                nt = s.nt
                n_t = n_p = n_u = n_y = 0
                for r in range(4):
                    half, o = r // 2, r % 2
                    cs = slice(half * 256, half * 256 + 256)
                    for j in range(nt):
                        if n_t >= 2:
                            pe.wait_ge(s.fe, n_t - 1)
                        for d in range(2):
                            m = pe.matmul(PS[:, n_t % 2, d * 256:d * 256 + 256], s.hdn[:, j * P + d:j * P + d + P],
                                          s.w3[:, o, d, cs], start=True, stop=True)
                        m.then_inc(s.ff, 1)
                        n_t += 1
                    pe.wait_ge(s.fe, n_t)
                    for kt in range(nt):
                        if n_p >= 2:
                            pe.wait_ge(s.pe_, n_p - 1)
                        b = 2 + n_p % 2 * 2
                        for tab, x, q in ((s.C, s.A, 0), (s.S, s.B, 1)):
                            for j in range(nt):
                                m = pe.matmul(PS[:, b + q, 0:256], tab[:, j, kt * P:kt * P + P], x[:, j, :],
                                              start=j == 0, stop=j == nt - 1)
                        m.then_inc(s.pf, 1)
                        n_p += 1
                    if o == 1:
                        pe.wait_ge(s.ye, n_y)
                    pe.wait_ge(s.pe_, n_p)
                    for kt in range(nt):
                        if n_u >= 1:
                            pe.wait_ge(s.ue, n_u - (1 if kt % 2 else 1))
                        b = 2 + n_u % 2 * 2
                        for tab, q in ((s.C, 0), (s.S, 1)):
                            for j in range(nt):
                                m = pe.matmul(PS[:, b + q, 0:256], tab[:, j, kt * P:kt * P + P], s.hv[:, s.t0 + j, cs],
                                              start=j == 0, stop=j == nt - 1)
                        m.then_inc(s.uf, 1)
                        n_u += 1
                    pe.wait_ge(s.ue, n_u)
                    if o == 0:
                        for j in range(nt):
                            if n_y >= 2:
                                pe.wait_ge(s.ye, n_y - 1)
                            q = 0
                            for tab, x in ((s.C, s.A), (s.S, s.B)):
                                for kt in range(nt):
                                    m = pe.matmul(PS[:, 6 + n_y % 2, 0:256], tab[:, kt, j * P:j * P + P], x[:, kt, :],
                                                  start=q == 0, stop=q == 2 * nt - 1)
                                    q += 1
                            m.then_inc(s.yf, 1)
                            n_y += 1
                    else:
                        for ct in range(2):
                            for n in range(s.L // s.tw):
                                if n_y >= 2:
                                    pe.wait_ge(s.ye, n_y - 1)
                                q = 0
                                for tab, x in ((s.C, s.A), (s.S, s.B)):
                                    for kt in range(nt):
                                        m = pe.matmul(PS[:, 6 + n_y % 2, 0:s.tw], x[:, kt, ct * P:ct * P + P],
                                                      tab[:, kt, n * s.tw:(n + 1) * s.tw], start=q == 0, stop=q == 2 * nt - 1)
                                        q += 1
                                m.then_inc(s.yf, 1)
                                n_y += 1

            def act(s, act, ch):
                act.wait_ge(s.full, 1)
                act.copy(s.c4, PS[0:64, 7, 0:4]).then_inc(s.hok, 1)
                for layer in range(2):
                    act.wait_ge(s.a1, layer + 1)
                    m = act.activation(s.hdn[:, 0:s.L], s.arg, ACT.Sin)
                    m.then_inc(s.hok, 1)

            def dve(s, dve, ch):
                ch.link(dve.memset(s.hdn[:, s.L:s.L + 1], 0.0))
                for layer in range(2):
                    dve.wait_ge(s.hok, layer + 1)
                    dve.wait_ge(s.full, layer + 2)
                    for n in range(s.L // s.tw):
                        sl = slice(n * s.tw, (n + 1) * s.tw)
                        ch.link(dve.tensor_scalar(s.arg[:, sl], PS[0:64, n + 2 * layer, 0:s.tw], s.c4[:, layer:layer + 1],
                                                  s.c4[:, 2 + layer:3 + layer], ALU.add, ALU.mult))
                    ch.link(dve.tensor_scalar(s.rnd, s.arg, 1.0 / (2 * math.pi), None, ALU.mult))
                    ch.link(dve.tensor_scalar(s.rnd, s.rnd, BIG, None, ALU.add))
                    ch.link(dve.tensor_scalar(s.rnd, s.rnd, -BIG, None, ALU.add))
                    hi = 6.28125
                    ch.link(dve.scalar_tensor_tensor(s.arg, s.rnd, -hi, s.arg, ALU.mult, ALU.add))
                    ch.link(dve.scalar_tensor_tensor(s.arg, s.rnd, -(2 * math.pi - hi), s.arg, ALU.mult, ALU.add))
                    dve.tensor_scalar(s.arg, s.arg, 3.1415925, -3.1415925, ALU.min, ALU.max).then_inc(s.a1, 1)
                nt = s.nt
                n_t = n_p = n_u = n_y = 0
                dve.wait_ge(s.hok, 3)
                for r in range(4):
                    half, o = r // 2, r % 2
                    cs = slice(half * 256, half * 256 + 256)
                    if r:
                        dve.wait_ge(s.yf, n_y)
                    for j in range(nt):
                        dve.wait_ge(s.dl[n_t % 2], 16 * (n_t // 2 + 1))
                        dve.wait_ge(s.ff, n_t + 1)
                        a, b = s.tmp[0], s.tmp[1]
                        dve.tensor_tensor(a, PS[:, n_t % 2, 0:256], s.dec[n_t % 2][:, 0, :], ALU.mult)
                        ch.link(dve.tensor_tensor(b, PS[:, n_t % 2, 256:512], s.dec[n_t % 2][:, 1, :], ALU.mult))
                        if j == 0:
                            ch.link(dve.tensor_tensor(a[0:1, :], a[0:1, :], s.drow[:, o, cs], ALU.add))
                        dve.tensor_tensor(s.B[:, j, :], a, b, ALU.subtract)
                        ch.link(dve.tensor_tensor(s.A[:, j, :], a, b, ALU.add))
                        dve.engine_nop().then_inc(s.fe, 1)
                        n_t += 1
                    for kt in range(nt):
                        dve.wait_ge(s.pf, n_p + 1)
                        b = 2 + n_p % 2 * 2
                        c, sn = s.rot[:, 0, kt:kt + 1], s.rot[:, 1, kt:kt + 1]
                        dve.tensor_scalar(s.tmp[0], PS[:, b + 1, 0:256], sn, None, ALU.mult)
                        ch.link(dve.tensor_scalar(s.tmp[1], PS[:, b + 1, 0:256], c, None, ALU.mult))
                        dve.scalar_tensor_tensor(s.Hr[:, kt, :], PS[:, b, 0:256], c, s.tmp[0], ALU.mult, ALU.add)
                        ch.link(dve.scalar_tensor_tensor(s.Hi[:, kt, :], PS[:, b, 0:256], sn, s.tmp[1], ALU.mult, ALU.subtract))
                        dve.engine_nop().then_inc(s.pe_, 1)
                        n_p += 1
                    for kt in range(nt):
                        dve.wait_ge(s.uf, n_u + 1)
                        b = 2 + n_u % 2 * 2
                        dve.tensor_tensor(s.tmp[0], PS[:, b, 0:256], s.Hr[:, kt, :], ALU.mult)
                        dve.tensor_tensor(s.tmp[1], PS[:, b + 1, 0:256], s.Hi[:, kt, :], ALU.mult)
                        dve.tensor_tensor(s.tmp[2], PS[:, b + 1, 0:256], s.Hr[:, kt, :], ALU.mult)
                        ch.link(dve.tensor_tensor(s.tmp[3], PS[:, b, 0:256], s.Hi[:, kt, :], ALU.mult))
                        dve.tensor_tensor(s.A[:, kt, :], s.tmp[0], s.tmp[1], ALU.add)
                        ch.link(dve.tensor_tensor(s.B[:, kt, :], s.tmp[2], s.tmp[3], ALU.subtract))
                        dve.engine_nop().then_inc(s.ue, 1)
                        n_u += 1
                    if o == 0:
                        for j in range(nt):
                            dve.wait_ge(s.yf, n_y + 1)
                            dve.tensor_tensor(s.hv[:, s.t0 + j, cs], PS[:, 6 + n_y % 2, 0:256], s.hx1[:, s.t0 + j, cs],
                                              ALU.mult).then_inc(s.ye, 1)
                            n_y += 1
                    else:
                        for ct in range(2):
                            for n in range(s.L // s.tw):
                                dve.wait_ge(s.yf, n_y + 1)
                                c0 = s.t0 * P + n * s.tw
                                v = s.yT[:, 4 + half * 2 + ct, c0:c0 + s.tw]
                                dve.tensor_tensor(v, PS[:, 6 + n_y % 2, 0:s.tw], v, ALU.mult).then_inc(s.ye, 1)
                                n_y += 1

        def layer_norm_tile(dve, ch, r, y, grow, lng, lnb, sd_ready, sd_need, var_ready, out):
            st = small[:, 0:12].rearrange("p (a b) -> p a b", a=2)
            for n in range(2):
                ch.link(dve.tensor_tensor(out[:, n * 512:(n + 1) * 512], y[n], grow[:, n * 512:(n + 1) * 512], ALU.mult))
            ch.link(dve.scalar_tensor_tensor(r, r, ALPHA, out, ALU.mult, ALU.add))
            for n in range(2):
                ch.link(dve.bn_stats(st[:, n, :], r[:, n * 512:(n + 1) * 512]))
            ch.link(dve.bn_aggr(small[:, 12:14], small[:, 0:12]))
            dve.tensor_scalar(small[:, 14:15], small[:, 13:14], EPS, None, ALU.add).then_inc(var_ready, 1)
            dve.wait_ge(sd_ready, sd_need)
            ch.link(dve.reciprocal(small[:, 16:17], small[:, 15:16]))
            ch.link(dve.tensor_scalar(r, r, small[:, 12:13], small[:, 16:17], ALU.subtract, ALU.mult))
            ch.link(dve.tensor_tensor(r, r, lng, ALU.mult))
            return dve.tensor_tensor(out, r, lnb, ALU.add)

        class OutProj:
            def __init__(s, l, yT, h, base):
                s.l, s.yT, s.h = l, yT, h
                s.W = at(base, KD, D)
                s.g = at(base + 8192, 2, D)
                s.ln = at(base + 10240, 2, D)
                s.x = [at(base + 12288 + b * D, D) for b in range(2)]
                s.wl, s.cl = sem(f"op_w_in"), sem(f"op_rows_in")
                s.xl = [sem(f"op_x_in_{b}") for b in range(2)]
                s.full, s.evac = sem(f"op_full"), sem(f"op_evac")
                s.var, s.sd, s.done = sem(f"op_var"), sem(f"op_sd"), sem(f"op_done")

            def sync(s, sp):
                w = I["even_w_out"] if s.l == 0 else I["odd_w_out"]
                sp.dma_start(s.W, w[0].rearrange("(k p) n -> p k n", p=P)).then_inc(s.wl, 16)
                for c in range(2):
                    sp.dma_start(s.g[:, c, :], modD[s.l, c:c + 1, 2 * D:3 * D].to_broadcast((P, D))).then_inc(s.cl, 16)
                sp.dma_start(s.ln[:, 0, :], I["ln_g"][s.l, 0:1, :].to_broadcast((P, D))).then_inc(s.cl, 16)
                sp.dma_start(s.ln[:, 1, :], I["ln_b"][s.l, 0:1, :].to_broadcast((P, D))).then_inc(s.cl, 16)
                for t in range(NT):
                    if t >= 2:
                        sp.wait_ge(s.done, t - 1)
                    sp.dma_start(s.x[t % 2], rows_of(t, s.l)).then_inc(s.xl[t % 2], 16)

            def pe(s, pe):
                pe.wait_ge(s.wl, 16)
                for t in range(NT):
                    if t >= 4:
                        pe.wait_ge(s.done, t - 3)
                    for n in range(2):
                        for k in range(KD):
                            m = pe.matmul(PS[:, t % 4 * 2 + n, :], s.yT[:, k, t * P:(t + 1) * P], s.W[:, k, n * 512:(n + 1) * 512],
                                          start=k == 0, stop=k == KD - 1)
                    m.then_inc(s.full, 1)

            def act(s, act, ch):
                for t in range(NT):
                    act.wait_ge(s.var, t + 1)
                    act.activation(small[:, 15:16], small[:, 14:15], ACT.Sqrt).then_inc(s.sd, 1)

            def dve(s, dve, ch):
                dve.wait_ge(s.cl, 64)
                for t in range(NT):
                    dve.wait_ge(s.full, t + 1)
                    dve.wait_ge(s.xl[t % 2], 16 * (t // 2 + 1))
                    b = t % 4 * 2
                    layer_norm_tile(dve, ch, s.x[t % 2], (PS[:, b, :], PS[:, b + 1, :]), s.g[:, t // NL, :],
                                    s.ln[:, 0, :], s.ln[:, 1, :], s.sd, t + 1, s.var,
                                    s.h[:, t, :]).then_inc(s.done, 1)

        class Router:
            def __init__(s, l, h, base, aff, slot):
                s.l, s.h, s.aff, s.slot = l, h, aff, slot
                s.uT = at(base, KD, TOK)
                s.w = at(base + 9216, KD, E_N)
                o = base + 9216 + 128
                s.affT = at(o, TOK, parts=16)
                s.work = at(o + 1152, TOK, parts=16)
                s.ge = at(o + 2304, TOK, parts=16)
                s.eq = at(o + 3456, TOK, parts=16)
                s.cum = at(o + 4608, TOK, parts=16)
                s.m8 = at(o + 5760, 8 * 18, parts=16)
                s.one = at(o + 5904, TOK, parts=16)
                s.red = at(o + 7056, 2, NT)
                s.cnt = at(o + 7080, 4, parts=16)
                sm = lambda n: sem(f"rt_{n}")
                s.ld = sm("w_in")
                s.full, s.ea, s.ed = sm("u_full"), sm("u_evac_act"), sm("u_evac_dve")
                s.lf, s.sub, s.ex, s.affok, s.tf, s.sl, s.sf = (sm(n) for n in (
                    "logits", "shifted", "exp", "aff", "aff_t", "slots", "slots_t"))

            def sync(s, sp):
                sp.dma_start(s.w, I["moe_router"][s.l].rearrange("(k p) e -> p k e", p=P)).then_inc(s.ld, 16)

            def pe(s, pe):
                for t in range(NT):
                    if t >= 2:
                        pe.wait_ge(s.ea, t - 1)
                        pe.wait_ge(s.ed, t - 1)
                    for k in range(KD):
                        m = pe.transpose(PS[:, t % 2 * 2 + k // 4, k % 4 * P:k % 4 * P + P],
                                         s.h[:, t, k * P:(k + 1) * P], ident)
                    m.then_inc(s.full, 1)
                pe.wait_ge(s.ea, NT)
                pe.wait_ge(s.ed, NT)
                pe.wait_ge(s.ld, 16)
                for t in range(NT):
                    for k in range(KD):
                        m = pe.matmul(PS[:, 4, t * E_N:(t + 1) * E_N], s.uT[:, k, t * P:(t + 1) * P], s.w[:, k, :],
                                      start=k == 0, stop=k == KD - 1)
                m.then_inc(s.lf, 1)
                pe.wait_ge(s.affok, 1)
                for t in range(NT):
                    m = pe.transpose(PS[0:16, 5 + t // 4, t % 4 * P:t % 4 * P + P], s.aff[:, t, :], ident)
                m.then_inc(s.tf, 1)
                pe.wait_ge(s.sl, 1)
                for t in range(NT):
                    m = pe.transpose(PS[:, 4, t * E_N:(t + 1) * E_N], s.ge[:, t * P:(t + 1) * P], ident[0:16, 0:16])
                m.then_inc(s.sf, 1)

            def evac(s, eng, bank, sm):
                for t in range(NT):
                    eng.wait_ge(s.full, t + 1)
                    for k in range(bank * 4, bank * 4 + 4):
                        m = modulate_tile(eng, s.uT[:, k, t * P:(t + 1) * P],
                                          PS[:, t % 2 * 2 + bank, k % 4 * P:k % 4 * P + P], 2, k, t < NL, bank == 0)
                    m.then_inc(sm, 1)

            def act(s, act, ch):
                s.evac(act, 0, s.ea)
                act.wait_ge(s.sub, 1)
                act.activation(s.aff, s.aff, ACT.Exp).then_inc(s.ex, 1)

            def dve(s, dve, ch):
                s.evac(dve, 1, s.ed)
                dve.wait_ge(s.lf, 1)
                lg = PS[:, 4, 0:NT * E_N].rearrange("p (a b) -> p a b", a=NT)
                col = lambda i: s.red[:, i, :].rearrange("p (a b) -> p a b", b=1).to_broadcast((P, NT, E_N))
                ch.link(dve.tensor_reduce(s.red[:, 0, :], lg, AX.X, ALU.max))
                dve.tensor_tensor(s.aff, lg, col(0), ALU.subtract).then_inc(s.sub, 1)
                dve.wait_ge(s.ex, 1)
                ch.link(dve.tensor_reduce(s.red[:, 1, :], s.aff, AX.X, ALU.add))
                ch.link(dve.reciprocal(s.red[:, 1, :], s.red[:, 1, :]))
                dve.tensor_tensor(s.aff, s.aff, col(1), ALU.mult).then_inc(s.affok, 1)
                ch.link(dve.memset(s.one, 1.0))
                dve.wait_ge(s.tf, 1)
                for b in range(3):
                    w = 512 if b < 2 else 128
                    dve.tensor_copy(s.affT[:, b * 512:b * 512 + w], PS[0:16, 5 + b, 0:w])
                    ch.link(dve.tensor_copy(s.work[:, b * 512:b * 512 + w], PS[0:16, 5 + b, 0:w]))
                i = 0
                for off, L, cap in ((0, L_LAT, CAP_L), (L_LAT, L_CTX, CAP_C)):
                    w = s.work[:, off:off + L]
                    a = s.affT[:, off:off + L]
                    ge, eq, cum, one = (v[:, off:off + L] for v in (s.ge, s.eq, s.cum, s.one))
                    for r in range(cap // 8):
                        m8 = s.m8[:, 8 * i:8 * i + 8]
                        i += 1
                        ch.link(dve.max(m8, w))
                        if r < cap // 8 - 1:
                            ch.link(dve.match_replace(w, m8, w, -1.0))
                    thr = m8[:, 7:8]
                    ch.link(dve.tensor_scalar(ge, a, thr, None, ALU.is_gt))
                    ch.link(dve.tensor_reduce(s.cnt[:, 0:1], ge, AX.X, ALU.add))
                    ch.link(dve.tensor_scalar(s.cnt[:, 1:2], s.cnt[:, 0:1], -1.0, float(cap), ALU.mult, ALU.add))
                    ch.link(dve.tensor_scalar(eq, a, thr, None, ALU.is_equal))
                    ch.link(dve.tensor_tensor_scan(cum, one, eq, 0.0, ALU.mult, ALU.add))
                    ch.link(dve.tensor_scalar(cum, cum, s.cnt[:, 1:2], None, ALU.is_le))
                    ch.link(dve.tensor_tensor(eq, eq, cum, ALU.mult))
                    ch.link(dve.tensor_tensor(eq, eq, ge, ALU.add))
                    ch.link(dve.tensor_tensor_scan(cum, one, eq, 0.0, ALU.mult, ALU.add))
                    ch.link(dve.tensor_tensor(ge, cum, eq, ALU.mult))
                    ch.link(dve.tensor_scalar(ge, ge, -1.0, None, ALU.add))
                dve.engine_nop().then_inc(s.sl, 1)
                dve.wait_ge(s.sf, 1)
                ch.link(dve.tensor_copy(s.slot.rearrange("p a b -> p (a b)"), PS[:, 4, 0:NT * E_N]))

        RING, EB = 4, 4

        class Experts:
            def __init__(s, l, h, yacc, aff, slot, base):
                s.l, s.h, s.yacc, s.aff, s.slot = l, h, yacc, aff, slot
                o = [base]

                def take(n):
                    o[0] += n
                    return o[0] - n
                s.w13 = [at(take(2048), 2, KD, P) for _ in range(RING)]
                s.w2 = [at(take(D), D) for _ in range(RING)]
                s.Pm, s.Pc = at(take(NL * P), NL, P), at(take(CAP_C), CAP_C)
                s.G, s.Gc = at(take(NL * P), NL, P), at(take(CAP_C), CAP_C)
                s.GT = at(take(L_LAT), L_LAT)
                s.GTc = at(take(L_CTX), L_CTX, parts=CAP_C)
                s.xs = at(take(KD * SLOTS), KD, SLOTS)
                s.hid = at(take(KF * SLOTS), KF, SLOTS)
                s.sil = [at(take(SLOTS), SLOTS) for _ in range(2)]
                s.oT = at(take(KD * SLOTS), KD, SLOTS)
                s.out = at(take(D), D)
                s.outc = at(take(D), D, parts=CAP_C)
                s.iota = at(take(P), P)
                s.cur = at(take(2 * NT), 2, NT)
                assert o[0] <= FREE, o
                sm = lambda n: sem(f"ex_{n}")
                s.il = sm("iota_in")
                s.wl = [sm(f"panel_in{r}") for r in range(RING)]
                s.used = sm("panel_used")
                s.sel, s.gf, s.ge = sm("chosen"), sm("gather_full"), sm("gather_evac")
                s.gtf, s.gte = sm("gate_t_full"), sm("gate_t_evac")
                s.ab, s.sl, s.hd = sm("ab_full"), sm("silu"), sm("hid")
                s.oe = sm("out_evac")
                s.tf, s.te = sm("out_t_full"), sm("out_t_evac")
                s.sf, s.se = sm("scatter_full"), sm("scatter_added")

            def sync(s, sp):
                sp.dma_start(s.iota, I["slot_iota"]).then_inc(s.il, 16)
                w1, w3, w2 = I["moe_w1"][s.l], I["moe_w3"][s.l], I["moe_w2"][s.l]
                per = EB * KF
                with sp.Fori(0, E_N // EB, 1) as b:
                    for n in range(per):
                        r = n % RING
                        e = b * EB + n // KF
                        f = n % KF
                        sp.wait_ge(s.used, b * per + n + 1)
                        for q, w in enumerate((w1, w3)):
                            src = w[bass.ds(e, 1), :, f * P:(f + 1) * P].rearrange("o (k p) n -> p (o k) n", p=P)
                            sp.dma_start(s.w13[r][:, q], src).then_inc(s.wl[r], 16)
                        src = w2[bass.ds(e, 1), f * P:(f + 1) * P, :].rearrange("o p n -> p (o n)")
                        sp.dma_start(s.w2[r], src).then_inc(s.wl[r], 16)

            def pe(s, pe):
                per = EB * KF
                pe.nop().then_inc(s.used, RING)
                for one_ahead in (s.te, s.se, s.gtf):
                    pe.nop().then_inc(one_ahead, 1)
                slots = lambda b0, m: PS[:, b0 + m // 3, m % 3 * SLOTS:m % 3 * SLOTS + SLOTS]
                with pe.Fori(0, E_N // EB, 1) as b:
                    for x in range(EB):
                        e = b * EB + x
                        pe.wait_ge(s.sel, e + 1)
                        pe.wait_ge(s.te, e * 2 + 1)
                        for m_ in range(KD):
                            for t in range(NL):
                                pe.matmul(slots(0, m_)[:, 0:CAP_L], s.h[:, t, m_ * P:(m_ + 1) * P], s.Pm[:, t, :],
                                          start=t == 0, stop=t == NL - 1)
                            m = pe.matmul(slots(0, m_)[:, CAP_L:SLOTS], s.h[:, NL, m_ * P:(m_ + 1) * P], s.Pc, start=True, stop=True)
                        m.then_inc(s.gf, 1)
                        for t in range(NL):
                            pe.transpose(PS[:, 3 + t // 4, t % 4 * P:t % 4 * P + P], s.G[:, t, :], ident)
                        pe.wait_ge(s.se, e * 18 + 1)
                        pe.transpose(PS[0:CAP_C, 5, 0:P], s.Gc, ident).then_inc(s.gtf, 1)
                        pe.wait_ge(s.ge, e + 1)

                        def down(f):
                            n = x * KF + f
                            pe.wait_ge(s.hd, b * per + n + 1)
                            for m_ in range(KD):
                                m = pe.matmul(slots(0, m_), s.w2[n % RING][:, m_ * P:(m_ + 1) * P], s.hid[:, f, :],
                                              start=f == 0 and m_ % 3 == 0, stop=f == KF - 1, skip_group_check=True)
                            m.then_inc(s.used, 1)

                        for f in range(KF):
                            n = x * KF + f
                            pe.wait_ge(s.wl[n % RING], b * (48 * per // RING) + 48 * (n // RING + 1))
                            if f >= 2:
                                pe.wait_ge(s.hd, b * per + n - 1)
                            for q in range(2):
                                for k in range(KD):
                                    m = pe.matmul(PS[:, 6 + f % 2, q * 256:q * 256 + SLOTS], s.w13[n % RING][:, q, k, :],
                                                  s.xs[:, k, :], start=k == 0, stop=k == KD - 1)
                            m.then_inc(s.ab, 1)
                            if f:
                                down(f - 1)
                        down(KF - 1)
                        pe.wait_ge(s.oe, e + 1)
                        pe.wait_ge(s.gte, e + 1)
                        for m_ in range(KD):
                            m = pe.transpose(PS[:, 3 + m_ // 4, m_ % 4 * P:m_ % 4 * P + P], s.oT[:, m_, 0:CAP_L], ident)
                        m.then_inc(s.tf, 1)
                        for m_ in range(KD):
                            m = pe.transpose(PS[0:CAP_C, m_ // 4, m_ % 4 * P:m_ % 4 * P + P], s.oT[:, m_, CAP_L:SLOTS], ident)
                        m.then_inc(s.tf, 1)
                        pe.wait_ge(s.te, e * 2 + 3)
                        for i in range(2 * NT):
                            t, n = i // 2, i % 2
                            if i >= 3:
                                pe.wait_ge(s.se, e * 18 + i - 1)
                            lhs, rhs = (s.GT[:, t * P:(t + 1) * P], s.out) if t < NL else (s.GTc, s.outc)
                            pe.matmul(PS[:, 5 + i % 3, :], lhs, rhs[:, n * 512:(n + 1) * 512], start=True, stop=True).then_inc(s.sf, 1)

            def act(s, act, ch):
                per = EB * KF
                with act.Fori(0, E_N // EB, 1) as b:
                    for x in range(EB):
                        e = b * EB + x
                        act.wait_ge(s.gf, e + 1)
                        for m_ in range(KD):
                            ps = PS[:, m_ // 3, m_ % 3 * SLOTS:m_ % 3 * SLOTS + SLOTS]
                            modulate_tile(act, s.xs[:, m_, 0:CAP_L], ps[:, 0:CAP_L], 2, m_, True, True)
                            m = modulate_tile(act, s.xs[:, m_, CAP_L:SLOTS], ps[:, CAP_L:SLOTS], 2, m_, False, True)
                        m.then_inc(s.ge, 1)
                        act.wait_ge(s.gtf, e + 2)
                        act.copy(s.GT[:, 0:512], PS[:, 3, :])
                        act.copy(s.GT[:, 512:1024], PS[:, 4, :])
                        act.copy(s.GTc, PS[0:CAP_C, 5, 0:P]).then_inc(s.gte, 1)
                        for f in range(KF):
                            n = x * KF + f
                            act.wait_ge(s.ab, b * per + n + 1)
                            act.activation(s.sil[f % 2], PS[:, 6 + f % 2, 0:SLOTS], ACT.Silu).then_inc(s.sl, 1)
                        act.wait_ge(s.used, b * per + (x + 1) * KF + RING)
                        for i in range(3):
                            w = 3 if i < 2 else 2
                            m = act.copy(s.oT[:, 3 * i:3 * i + w, :].rearrange("p a b -> p (a b)"), PS[:, i, 0:w * SLOTS])
                        m.then_inc(s.oe, 1)
                        act.wait_ge(s.tf, e * 2 + 1)
                        act.copy(s.out[:, 0:512], PS[:, 3, :])
                        act.copy(s.out[:, 512:1024], PS[:, 4, :]).then_inc(s.te, 1)
                        act.wait_ge(s.tf, e * 2 + 2)
                        act.copy(s.outc[:, 0:512], PS[0:CAP_C, 0, :])
                        act.copy(s.outc[:, 512:1024], PS[0:CAP_C, 1, :]).then_inc(s.te, 1)

            def dve(s, dve, ch):
                per = EB * KF
                ch.link(dve.memset(s.yacc, 0.0))
                dve.wait_ge(s.il, 16)

                def body(b):
                    for x in range(EB):
                        e = b * EB + x
                        dve.tensor_copy(s.cur[:, 0, :].rearrange("p (a b) -> p a b", b=1), s.slot[:, :, bass.ds(e, 1)])
                        ch.link(dve.tensor_copy(s.cur[:, 1, :].rearrange("p (a b) -> p a b", b=1), s.aff[:, :, bass.ds(e, 1)]))
                        dve.wait_ge(s.gtf, e + 1)
                        for t in range(NT):
                            w = P if t < NL else CAP_C
                            pm, g = (s.Pm[:, t, :], s.G[:, t, :]) if t < NL else (s.Pc, s.Gc)
                            dve.tensor_scalar(pm, s.iota[:, 0:w], s.cur[:, 0, t:t + 1], None, ALU.is_equal)
                            m = dve.tensor_scalar(g, s.iota[:, 0:w], s.cur[:, 0, t:t + 1], s.cur[:, 1, t:t + 1],
                                                  ALU.is_equal, ALU.mult)
                        m.then_inc(s.sel, 1)
                        for f in range(KF):
                            n = x * KF + f
                            dve.wait_ge(s.sl, b * per + n + 1)
                            dve.tensor_tensor(s.hid[:, f, :], PS[:, 6 + f % 2, 256:256 + SLOTS], s.sil[f % 2],
                                              ALU.mult).then_inc(s.hd, 1)
                        for i in range(2 * NT):
                            t, n = i // 2, i % 2
                            dve.wait_ge(s.sf, e * 18 + i + 1)
                            v = s.yacc[:, t, n * 512:(n + 1) * 512]
                            dve.tensor_tensor(v, v, PS[:, 5 + i % 3, :], ALU.add).then_inc(s.se, 1)
                ch.loop(E_N // EB, EB, body)

        class MoeEnd:
            def __init__(s, l, h, yacc, base):
                s.l, s.h, s.yacc = l, h, yacc
                s.g, s.ln = at(base, 2, D), at(base + 2048, 2, D)
                s.o = [at(base + 4096 + b * D, D) for b in range(2)]
                sm = lambda n: sem(f"me_{n}")
                s.cl, s.var, s.sd, s.done = sm("rows_in"), sm("var"), sm("sd"), sm("done")
                s.st = [sm("stored0"), sm("stored1")]

            def sync(s, sp):
                for c in range(2):
                    sp.dma_start(s.g[:, c, :], modD[s.l, c:c + 1, 5 * D:6 * D].to_broadcast((P, D))).then_inc(s.cl, 16)
                sp.dma_start(s.ln[:, 0, :], I["ln_g"][s.l, 1:2, :].to_broadcast((P, D))).then_inc(s.cl, 16)
                sp.dma_start(s.ln[:, 1, :], I["ln_b"][s.l, 1:2, :].to_broadcast((P, D))).then_inc(s.cl, 16)
                for t in range(NT):
                    sp.wait_ge(s.done, t + 1)
                    if s.l < DEPTH - 1:
                        dst = hD[t * P:(t + 1) * P, :]
                    else:
                        dst = O["y_sample"][0, t * P:(t + 1) * P, :] if t < NL else O["y_prompt"][0]
                    sp.dma_start(dst, s.o[t % 2]).then_inc(s.st[t % 2], 16)
                sp.wait_ge(s.st[0], 16 * 5)
                sp.wait_ge(s.st[1], 16 * 4)

            def pe(s, pe):
                pass

            def act(s, act, ch):
                for t in range(NT):
                    act.wait_ge(s.var, t + 1)
                    act.activation(small[:, 15:16], small[:, 14:15], ACT.Sqrt).then_inc(s.sd, 1)

            def dve(s, dve, ch):
                dve.wait_ge(s.cl, 64)
                for t in range(NT):
                    if t >= 2:
                        dve.wait_ge(s.st[t % 2], 16 * (t // 2))
                    y = s.yacc[:, t, :]
                    layer_norm_tile(dve, ch, s.h[:, t, :], (y[:, 0:512], y[:, 512:1024]), s.g[:, t // NL, :],
                                    s.ln[:, 0, :], s.ln[:, 1, :], s.sd, t + 1, s.var, s.o[t % 2]).then_inc(s.done, 1)

        class Retention:
            def __init__(s, uT, yT, base):
                s.uT, s.yT = uT, yT
                o = [base]

                def take(n):
                    o[0] += n
                    return o[0] - n
                s.W = at(take(KD * 512), KD, 2, 256)
                s.v = at(take(NT * 256), NT, 256)
                s.g = at(take(NT * 256), NT, 256)
                s.k = [at(take(NT * 256), NT, 256) for _ in range(2)]
                s.qT = at(take(2 * TOK), 2, TOK)
                s.kT = at(take(2 * TOK), 2, TOK)
                s.qd = [at(take(2 * L_LAT), 2, L_LAT) for _ in range(2)]
                s.attn = at(take(TOK), NT, P)
                s.Sb = at(take(2 * NL * 256), 2, NL, 256)
                s.Sf = [at(take(512), 2, 256) for _ in range(2)]
                s.rope = at(take(2 * L_LAT), 2, NL, 128)
                s.qk = at(take(512), 2, 256)
                s.rp = [at(take(256), 256) for _ in range(2)]
                s.dist = at(take(4 * P), 4, P)
                s.prow = at(take(2 * P), 2, P)
                s.pcol = at(take(2), 2)
                s.lg = at(take(8), 8)
                s.gstep = at(take(8), 8)
                s.cd = at(take(4), 4)
                s.dm = at(take(P), P)
                s.dt = at(take(P), P)
                s.gr = at(take(2 * P), 2, P)
                s.stt = at(take(16), 16)
                assert o[0] <= FREE, (o, FREE)
                sm = lambda n: sem(f"re_{n}")
                s.cl, s.s0 = sm("const_in"), sm("s0_in")
                s.wl, s.wu = sm("w_in"), sm("w_used")
                s.lgq, s.lgx = sm("lg_req"), sm("lg_ok")
                s.pf, s.pe_ = sm("proj_full"), sm("proj_evac")
                s.ro, s.tf, s.te = sm("rope"), sm("t_full"), sm("t_evac")
                s.vf, s.ve = sm("vg_full"), sm("vg_evac")
                s.dreq, s.dok, s.mok = sm("decay_req"), sm("decay_exp"), sm("decay_ok")
                s.af, s.ae = sm("att_full"), sm("att_ok")
                s.uf, s.ub = sm("upd_full"), sm("state_ok")
                s.of, s.oe, s.var, s.sd, s.yo = sm("o_full"), sm("o_read"), sm("o_var"), sm("o_sd"), sm("y_ok")
                s.yf, s.yv = sm("y_t_full"), sm("y_t_evac")
                s.st = sm("state_stored")

            def sync(s, sp):
                for dst, src in ((s.rope, I["rope"]), (s.dist, I["time_dist"]), (s.prow, I["pos_rows"]),
                                 (s.pcol, I["pos_cols"]),
                                 (s.lg, I["ret_decay"].rearrange("o d h -> o (d h)").to_broadcast((P, 8)))):
                    sp.dma_start(dst, src).then_inc(s.cl, 16)
                for h in range(C_H):
                    for part in range(2):
                        if h or part:
                            sp.wait_ge(s.wu, 2 * h + part)
                        for j in range(2):
                            c0 = (2 * part + j) * D + h * 256
                            sp.dma_start(s.W[:, :, j, :], I["odd_w_in"][0, :, c0:c0 + 256]
                                         .rearrange("(k p) n -> p k n", p=P)).then_inc(s.wl, 16)
                        if part == 1:
                            if h:
                                sp.wait_ge(s.st, 64 * h)
                                sp.wait_ge(s.of, NT * h)
                            for dst, d in ((s.Sf[0], 0), (s.Sb[:, :, NL - 1, :], 1)):
                                sp.dma_start(dst, I["state_ret"][0, 0, d, h].rearrange("(a p) e -> p a e", p=P)).then_inc(s.s0, 16)
                    for i, d in enumerate((1, 0)):
                        sp.wait_ge(s.ub, h * 32 + (16 if d == 1 else 32))
                        src = s.Sf[1] if d == 1 else s.Sf[0]
                        for a in range(2):
                            sp.dma_start(O["new_state_ret"][0, 0, d, h, a * P:(a + 1) * P, :], src[:, a, :]).then_inc(s.st, 16)
                sp.wait_ge(s.st, 64 * C_H)

            def pe(s, pe):
                for h in range(C_H):
                    pe.wait_ge(s.wl, 64 * h + 32)

                    def turn(t):
                        pe.wait_ge(s.ro, h * NT + t + 1)
                        n = h * NT + t
                        if n:
                            pe.wait_ge(s.te, n)
                        for i in range(4):
                            m = pe.transpose(PS[:, 2, i * P:(i + 1) * P], s.qk[:, i // 2, i % 2 * P:i % 2 * P + P], ident)
                        m.then_inc(s.tf, 1)
                    for t in range(NT):
                        n = h * NT + t
                        if n >= 2:
                            pe.wait_ge(s.pe_, n - 1)
                        for k in range(KD):
                            m = pe.matmul(PS[:, n % 2, :], s.uT[:, k, t * P:(t + 1) * P],
                                          s.W[:, k, :, :].rearrange("p a b -> p (a b)"), start=k == 0, stop=k == KD - 1)
                        m.then_inc(s.pf, 1)
                        if t:
                            turn(t - 1)
                    pe.wait_ge(s.pf, (h + 1) * NT)
                    pe.nop().then_inc(s.wu, 1)
                    turn(NT - 1)
                    pe.wait_ge(s.wl, 64 * h + 64)
                    for t in range(NT):
                        n = h * NT + t
                        if n >= 2:
                            pe.wait_ge(s.ve, n - 1)
                        for k in range(KD):
                            m = pe.matmul(PS[:, 6 + n % 2, :], s.uT[:, k, t * P:(t + 1) * P],
                                          s.W[:, k, :, :].rearrange("p a b -> p (a b)"), start=k == 0, stop=k == KD - 1)
                        m.then_inc(s.vf, 1)
                    pe.wait_ge(s.vf, (h + 1) * NT)
                    pe.nop().then_inc(s.wu, 1)
                    pe.wait_ge(s.te, (h + 1) * NT)
                    for t in range(NT):
                        n = h * NT + t
                        if n:
                            pe.wait_ge(s.ae, n)
                        for a in range(2):
                            m = pe.matmul(PS[:, 4, 0:P], s.kT[:, a, t * P:(t + 1) * P], s.qT[:, a, t * P:(t + 1) * P],
                                          start=a == 0, stop=a == 1)
                        m.then_inc(s.af, 1)
                    pe.wait_ge(s.ve, (h + 1) * NT)
                    pe.wait_ge(s.ae, (h + 1) * NT)
                    u = 0

                    def update(d, c):
                        nonlocal u
                        for a in range(2):
                            if h * 32 + u:
                                pe.wait_ge(s.ub, h * 32 + u)
                            pe.matmul(PS[:, 4, 0:256], s.k[d][:, c, a * P:(a + 1) * P], s.v[:, c, :],
                                      start=True, stop=True).then_inc(s.uf, 1)
                            u += 1
                    for c in range(NL - 1, 0, -1):
                        update(1, c)
                    update(1, NL)
                    for c in range(NT):
                        n = h * NT + c
                        if n >= 1:
                            pe.wait_ge(s.oe, n)
                        out = PS[:, 5, 0:256]
                        m = pe.matmul(out, s.attn[:, c, :], s.v[:, c, :], start=True, stop=c == NL)
                        if c < NL:
                            pe.wait_ge(s.ub, h * 32 + 16 + 2 * c)
                            if c == 0:
                                pe.wait_ge(s.mok, 2 * h + 2)
                            sl = slice(c * P, (c + 1) * P)
                            for a in range(2):
                                pe.matmul(out, s.qd[1][:, a, sl], s.Sb[:, a, c, :], start=False, stop=False)
                            for a in range(2):
                                m = pe.matmul(out, s.qd[0][:, a, sl], s.Sf[c % 2][:, a, :], start=False, stop=a == 1)
                        m.then_inc(s.of, 1)
                        if c < NL - 1:
                            update(0, c)
                        if c == NL:
                            update(0, NL)
                        if c:
                            s.turn_y(pe, h, c - 1)
                    s.turn_y(pe, h, NT - 1)

            def turn_y(s, pe, h, c):
                n = h * NT + c
                pe.wait_ge(s.yo, n + 1)
                if n:
                    pe.wait_ge(s.yv, n)
                for a in range(2):
                    m = pe.transpose(PS[:, 3, a * P:(a + 1) * P], s.rp[n % 2][:, a * P:(a + 1) * P], ident)
                m.then_inc(s.yf, 1)

            def act(s, act, ch):
                act.wait_ge(s.cl, 80)
                act.activation(s.lg, s.lg, ACT.Exp, scale=-1.0).then_inc(s.lgx, 1)
                act.wait_ge(s.lgq, 1)
                act.activation(s.lg, s.lg, ACT.Ln).then_inc(s.lgx, 1)
                act.wait_ge(s.lgq, 2)
                act.activation(s.gstep, s.gstep, ACT.Exp).then_inc(s.lgx, 1)
                for h in range(C_H):
                    for n in range(2):
                        act.wait_ge(s.dreq, 2 * h + n + 1)
                        if n == 0:
                            act.activation(s.gr, s.gr, ACT.Exp)
                            act.activation(s.cd[:, 0:2], s.cd[:, 0:2], ACT.Exp)
                            act.activation(s.dm, s.dm, ACT.Exp).then_inc(s.dok, 1)
                        else:
                            act.activation(s.dt, s.dt, ACT.Exp).then_inc(s.dok, 1)

                    def turn(t):
                        n = h * NT + t
                        act.wait_ge(s.tf, n + 1)
                        if t == 0 and h:
                            act.wait_ge(s.of, h * NT)
                        act.copy(s.qT[:, :, t * P:(t + 1) * P], PS[:, 2, 0:256].rearrange("p (a b) -> p a b", a=2))
                        act.copy(s.kT[:, :, t * P:(t + 1) * P],
                                 PS[:, 2, 256:512].rearrange("p (a b) -> p a b", a=2)).then_inc(s.te, 1)
                    for t in range(NT):
                        turn(t)
                    for t in range(NT):
                        n = h * NT + t
                        act.wait_ge(s.vf, n + 1)
                        if t == 0 and h:
                            act.wait_ge(s.uf, h * 32)
                            act.wait_ge(s.yo, h * NT)
                        act.copy(s.v[:, t, :], PS[:, 6 + n % 2, 0:256])
                        act.activation(s.g[:, t, :], PS[:, 6 + n % 2, 256:512], ACT.Silu).then_inc(s.ve, 1)
                    for c in range(NT):
                        act.wait_ge(s.var, h * NT + c + 1)
                        act.activation(s.stt[:, 9:10], s.stt[:, 8:9], ACT.Sqrt).then_inc(s.sd, 1)
                        if c:
                            s.act_y(act, h, c - 1)
                    s.act_y(act, h, NT - 1)

            def act_y(s, act, h, c):
                n = h * NT + c
                act.wait_ge(s.yf, n + 1)
                act.copy(s.yT[:, 2 * h:2 * h + 2, c * P:(c + 1) * P],
                         PS[:, 3, 0:256].rearrange("p (a b) -> p a b", a=2)).then_inc(s.yv, 1)

            def dve(s, dve, ch):
                dve.wait_ge(s.cl, 80)
                dve.wait_ge(s.lgx, 1)
                dve.tensor_scalar(s.lg, s.lg, 1.0, None, ALU.add).then_inc(s.lgq, 1)
                dve.wait_ge(s.lgx, 2)
                ch.link(dve.tensor_scalar(s.lg, s.lg, -1.0, None, ALU.mult))
                dve.tensor_scalar(s.gstep, s.lg, float(P), None, ALU.mult).then_inc(s.lgq, 1)
                dve.wait_ge(s.lgx, 3)
                for h in range(C_H):
                    lg = [s.lg[:, d * C_H + h:d * C_H + h + 1] for d in range(2)]
                    gc = [s.gstep[:, d * C_H + h:d * C_H + h + 1] for d in range(2)]
                    for d in range(2):
                        dve.tensor_scalar(s.gr[:, d, :], s.prow[:, d, :], lg[d], None, ALU.mult)
                        dve.tensor_scalar(s.cd[:, d:d + 1], s.pcol[:, d:d + 1], lg[d], None, ALU.mult)
                    dve.tensor_scalar(s.dt, s.dist[:, 2, :], lg[1], None, ALU.mult)
                    dve.tensor_scalar(s.dm, s.dist[:, 0, :], lg[0], None, ALU.mult).then_inc(s.dreq, 1)
                    dve.wait_ge(s.dok, 2 * h + 1)
                    ch.link(dve.tensor_tensor(s.dm, s.dm, s.dist[:, 1, :], ALU.mult))
                    dve.engine_nop().then_inc(s.dreq, 1)
                    dve.wait_ge(s.dok, 2 * h + 2)
                    ch.link(dve.tensor_tensor(s.dt, s.dt, s.dist[:, 3, :], ALU.mult))
                    ch.link(dve.tensor_tensor(s.dm, s.dm, s.dt, ALU.add))
                    dve.engine_nop().then_inc(s.mok, 1)
                    for t in range(NT):
                        n = h * NT + t
                        dve.wait_ge(s.pf, n + 1)
                        if n:
                            dve.wait_ge(s.tf, n)
                        ps = PS[:, n % 2, :]
                        if t < NL:
                            x = ps.rearrange("p (a b c) -> p a b c", a=4, b=2)
                            o = s.qk.rearrange("p a b -> p (a b)").rearrange("p (a b c) -> p a b c", a=4, b=2)
                            tmp = s.rp[0].rearrange("p (a c) -> p a c", a=4)
                            for i in range(2):
                                for j in range(2):
                                    tab = s.rope[:, i if j == 0 else 1 - i, t, :].rearrange("p (b c) -> p b c", b=2)
                                    for qk in range(2):
                                        dst = (o[:, 2 * qk:2 * qk + 2, i, :] if j == 0 else tmp[:, 2 * qk:2 * qk + 2, :])
                                        m = dve.tensor_tensor(dst, x[:, 2 * qk:2 * qk + 2, j, :], tab, ALU.mult)
                                ch.link(m)
                                ch.link(dve.tensor_tensor(o[:, :, i, :], o[:, :, i, :], tmp, ALU.subtract if i == 0 else ALU.add))
                        else:
                            ch.link(dve.tensor_copy(s.qk.rearrange("p a b -> p (a b)"), ps))
                        dve.engine_nop().then_inc(s.pe_, 1)
                        ch.link(dve.tensor_scalar(s.qk[:, 1, :], s.qk[:, 1, :], C_HD ** -0.5, None, ALU.mult))
                        for d in range(2):
                            m = dve.tensor_scalar(s.k[d][:, t, :], s.qk[:, 1, :], s.cd[:, d:d + 1], None, ALU.mult)
                        m.then_inc(s.ro, 1)
                    dve.wait_ge(s.te, (h + 1) * NT)
                    for d in range(2):
                        gr = s.gr[:, d:d + 1, :].to_broadcast((P, NL, P))
                        for a in range(2):
                            m = dve.tensor_tensor(s.qd[d][:, a, :].rearrange("p (c t) -> p c t", t=P),
                                                  s.qT[:, a, 0:L_LAT].rearrange("p (c t) -> p c t", t=P), gr, ALU.mult)
                    m.then_inc(s.mok, 1)
                    for t in range(NT):
                        dve.wait_ge(s.af, h * NT + t + 1)
                        dve.tensor_tensor(s.attn[:, t, :], PS[:, 4, 0:P], s.dm, ALU.mult).then_inc(s.ae, 1)
                    dve.wait_ge(s.s0, 32 * (h + 1))
                    u = h * 32
                    for c in range(NL - 1, 0, -1):
                        for a in range(2):
                            u += 1
                            dve.wait_ge(s.uf, u)
                            ch.link(dve.scalar_tensor_tensor(s.Sb[:, a, c - 1, :], s.Sb[:, a, c, :], gc[1], PS[:, 4, 0:256],
                                                             ALU.mult, ALU.add))
                            dve.engine_nop().then_inc(s.ub, 1)
                    for a in range(2):
                        u += 1
                        dve.wait_ge(s.uf, u)
                        dve.tensor_copy(s.Sf[1][:, a, :], PS[:, 4, 0:256]).then_inc(s.ub, 1)
                    for c in range(NT):
                        n = h * NT + c
                        dve.wait_ge(s.of, n + 1)
                        st = s.stt[:, 0:6]
                        ch.link(dve.bn_stats(st, PS[:, 5, 0:256]))
                        ch.link(dve.bn_aggr(s.stt[:, 6:8], st))
                        dve.tensor_scalar(s.stt[:, 8:9], s.stt[:, 7:8], EPS, None, ALU.add).then_inc(s.var, 1)
                        if c < NL - 1 or c == NL:
                            if c == 0:
                                dve.wait_ge(s.st, 64 * h + 32)
                            for a in range(2):
                                u += 1
                                dve.wait_ge(s.uf, u)
                                if c < NL - 1:
                                    ch.link(dve.scalar_tensor_tensor(s.Sf[(c + 1) % 2][:, a, :], s.Sf[c % 2][:, a, :], gc[0],
                                                                     PS[:, 4, 0:256], ALU.mult, ALU.add))
                                else:
                                    ch.link(dve.tensor_copy(s.Sf[0][:, a, :], PS[:, 4, 0:256]))
                                dve.engine_nop().then_inc(s.ub, 1)
                        dve.wait_ge(s.sd, n + 1)
                        ch.link(dve.reciprocal(s.stt[:, 10:11], s.stt[:, 9:10]))
                        if n >= 2:
                            dve.wait_ge(s.yf, n - 1)
                        ch.link(dve.tensor_scalar(s.rp[n % 2], PS[:, 5, 0:256], s.stt[:, 6:7], s.stt[:, 10:11],
                                                  ALU.subtract, ALU.mult))
                        dve.engine_nop().then_inc(s.oe, 1)
                        dve.tensor_tensor(s.rp[n % 2], s.rp[n % 2], s.g[:, c, :], ALU.mult).then_inc(s.yo, 1)

        uT0 = at(0, KD, TOK)
        yT0 = at(33792, KD, TOK)
        dft_l = at(0, 2, NL, L_LAT)
        hv, hx1 = at(24576, NT, 512), at(29184, NT, 512)
        h_res = at(0, NT, D)
        yacc = at(9216, NT, D)
        aff, slot = at(18432, NT, E_N), at(18576, NT, E_N)
        uT1, yT1 = at(0, KD, TOK), at(9216, KD, TOK)
        stages = [
            Modulation(0), MixerInput(0, uT0, 9216), Hgrn(uT0, yT0, 9216, 43008),
            HyenaIn(uT0, 9216, hv, hx1, yT0),
            HyenaConv("lat", hv, hx1, yT0, dft_l, 16384, 43008),
            HyenaConv("ctx", hv, hx1, yT0, at(0, 2, 1, P), 16384, 43008),
            OutProj(0, yT0, h_res, 18432), Router(0, h_res, 18720, aff, slot),
            Experts(0, h_res, yacc, aff, slot, 18720), MoeEnd(0, h_res, yacc, 18720),
            Modulation(1), MixerInput(1, uT1, 9216), Retention(uT1, yT1, 18432),
        ]
        stages += [OutProj(1, yT1, at(18432, NT, D), 27648), Router(1, at(18432, NT, D), 28000, at(27648, NT, E_N), at(27792, NT, E_N))]
        h1, yacc1 = at(18432, NT, D), at(0, NT, D)
        stages += [Experts(1, h1, yacc1, at(27648, NT, E_N), at(27792, NT, E_N), 28000), MoeEnd(1, h1, yacc1, 28000)]
        if I.get("_stop"):
            stages = stages[:I["_stop"]]

        cuts = [c for c in (0, 5, 10) if c < len(stages)] + [len(stages)]
        for lo, hi in zip(cuts, cuts[1:]):
            run_block(nc, stages[lo:hi], stage_end, n_stage, act_seq, dve_seq)
            if hi < len(stages):
                nums = sorted(v.num for v in taken.values())
                assert nums == list(range(nums[0], nums[-1] + 1))
                nc.all_engine_barrier(sems_to_clear=range(nums[0], nums[-1] + 1))
                n_stage.clear()


def run_block(nc, stages, stage_end, n_stage, act_seq, dve_seq):
    with nc.Block() as block:
        @block.sync
        def _(sp):
            for s in stages:
                s.sync(sp)
                stage_end(sp, "sp")

        @block.tensor
        def _(pe):
            for s in stages:
                s.pe(pe)
                stage_end(pe, "pe")

        @block.scalar
        def _(act):
            ch = Chain(act, act_seq)
            for s in stages:
                s.act(act, ch)
                stage_end(act, "act")

        @block.vector
        def _(dve):
            ch = Chain(dve, dve_seq)
            for s in stages:
                s.dve(dve, ch)
                stage_end(dve, "dve")


OUTS = {"y_prompt": (1, L_CTX, D), "y_sample": (1, L_LAT, D),
        "new_state_hgrn": (1, 1, 2, A_H, P, P), "new_state_ret": (1, 1, 2, C_H, C_HD, C_HD)}


def kernel(**inputs):
    from concourse import bacc
    from concourse.bass_utils import run_bass_kernel_spmd

    nc = bacc.Bacc("TRN2", target_bir_lowering=False, num_devices=1)
    arrays = {n: np.ascontiguousarray(a) for n, a in inputs.items() if n != "hgrn_lb"}
    arrays.update({n: np.ascontiguousarray(a) for n, a in CONST.items()})
    I = {n: nc.dram_tensor(n, a.shape, F32, kind="ExternalInput").ap() for n, a in arrays.items()}
    O = {n: nc.dram_tensor(n + "_out", shape, F32, kind="ExternalOutput").ap() for n, shape in OUTS.items()}
    build(nc, I, O)
    r = run_bass_kernel_spmd(nc, [arrays], core_ids=[0])
    return tuple(r.results[0][n + "_out"] for n in OUTS)
```

```python
import math
from contextlib import ExitStack

import numpy as np

import concourse.bass as bass
from concourse import mybir

F32 = mybir.dt.float32
U32 = mybir.dt.uint32
BF16 = mybir.dt.bfloat16
ALU = mybir.AluOpType
ACT = mybir.ActivationFunctionType
AX = mybir.AxisListType

P = 128
D = 1024
KD = D // P
L_LAT, L_CTX = 1024, 128
NL = L_LAT // P
NT = NL + L_CTX // P
TOK = NT * P
DEPTH = 2
ALPHA = (2 * DEPTH) ** 0.25
EPS = 1e-5
A_H = 4
C_H, C_HD = 4, 256
AW = 512
E_N, FF = 16, 1408
KF = FF // P
CAP_L, CAP_C = 2 * L_LAT // E_N, 2 * L_CTX // E_N
SLOTS = CAP_L + CAP_C
BIG = float(1.5 * 2 ** 23)
NCH = 3 * P
LOG_FLOOR = 40.0


class Chain:

    def __init__(self, eng, sem):
        self.eng, self.sem, self.n, self.base = eng, sem, 0, 0

    def mark(self, ins):
        ins.then_inc(self.sem, 1)
        self.n += 1
        return ins

    def wait(self):
        self.eng.wait_ge(self.sem, self.base + self.n)

    def link(self, ins):
        self.mark(ins)
        self.wait()

    def loop(self, count, per, body):
        start = self.n
        with self.eng.Fori(0, count, 1) as i:
            self.base = i * per
            body(i)
        assert self.n - start == per, (self.n - start, per)
        self.base = 0
        self.n = start + count * per


def shape_constants():
    c = {}
    c["ident"] = np.eye(P, dtype=np.float32)
    s, t = np.arange(P)[:, None], np.arange(P)[None, :]
    masks = [s == t]
    for d in range(2):
        for l in range(7):
            hs = 64 >> l
            a, b = (s, t) if d == 0 else (t, s)
            masks.append((a // (2 * hs) == b // (2 * hs)) & (a // hs % 2 == 0) & (b // hs % 2 == 1))
    c["gram_masks"] = np.stack(masks, 1).astype(np.float32)
    c["time_dist"] = np.stack([np.where(t >= s, t - s, 0), np.where(t >= s, 1, 0),
                               np.where(s >= t, s - t, 0), np.where(s >= t, 1, 0)], 1).astype(np.float32)
    for name, L in (("lat", L_LAT), ("ctx", L_CTX)):
        k = np.arange(L)[:, None].astype(np.float64)
        n = np.arange(L)[None, :].astype(np.float64)
        ang = np.pi * (2 * k + 1) * (2 * n + 1) / (4 * L)
        nt = L // P
        tile = lambda m: m.reshape(nt, P, -1).transpose(1, 0, 2).astype(np.float32)
        if name == "ctx":
            c["dft_ctx"] = np.stack([tile(np.cos(ang)), tile(np.sin(ang))], 1)
        else:
            both = np.stack([np.cos(ang) + np.sin(ang), np.cos(ang) - np.sin(ang)])[:, :, :L // 2]
            both = np.concatenate([both[:, 0::2], both[:, 1::2]], 1)
            c["fold_inv"] = both.reshape(2, nt, P, L // 2).transpose(2, 0, 1, 3).astype(np.float32)
            c["fold_fwd"] = both.reshape(2, L, nt // 2, P).transpose(3, 0, 2, 1).astype(np.float32)
        order = k[:, 0] if name == "ctx" else np.concatenate([k[0::2, 0], k[1::2, 0]])
        half = np.pi * (2 * order + 1) / (4 * L)
        scale = L if name == "ctx" else 8 * L
        c[f"rot_{name}"] = np.stack([(np.cos(half) / scale).reshape(nt, P).T,
                                     (np.sin(half) / scale).reshape(nt, P).T], 1).astype(np.float32)
        tt = np.linspace(0.0, 1.0, L, dtype=np.float32)[:, None]
        bands = 16
        aa = np.float32(2.0 * math.pi / L) * np.arange(L, dtype=np.float32)[:, None] \
            * np.linspace(1e-4, bands - 1, bands, dtype=np.float32)[None, :]
        c[f"z_{name}"] = np.ascontiguousarray(np.concatenate([tt, np.cos(aa), -np.sin(aa)], -1).T.astype(np.float32))
        deltas = np.abs(np.linspace(math.log(1e-2) / 1.5, math.log(1e-2) / 0.3, 512, dtype=np.float32))
        dec = np.exp(-tt * deltas).astype(np.float32)
        nxt = np.concatenate([dec[1:], np.zeros((1, 512), np.float32)])
        both = np.stack([dec, nxt], 1)
        if name == "ctx":
            both = both.reshape(nt, P, 2, 2, 256)
            c["decay_ctx"] = np.ascontiguousarray(both.transpose(3, 0, 1, 2, 4))
        else:
            both = np.stack([both[:L // 2], both[L // 2:][::-1]], 1).reshape(nt // 2, P, 2, 2, 2, 256)
            c["decay_lat"] = np.ascontiguousarray(both.transpose(4, 0, 1, 2, 3, 5))
    quarter = 64
    inv = (10000.0 ** (-np.arange(quarter, dtype=np.float32) / np.float32(quarter))).astype(np.float32)
    pos = np.stack([np.arange(L_LAT) // 64, np.arange(L_LAT) % 64], 1).astype(np.float32)
    a = pos[:, :, None] * inv
    tr = lambda m: m.reshape(NL, P, 128).transpose(1, 0, 2).astype(np.float32)
    c["rope"] = np.stack([tr(np.cos(a)), tr(np.sin(a))], 1)
    c["slot_iota"] = np.broadcast_to(np.arange(P, dtype=np.float32), (P, P)).copy()
    r = np.arange(P, dtype=np.float32)
    c["token_parts"] = np.stack([np.broadcast_to(np.arange(NT, dtype=np.float32), (P, NT)),
                                 np.broadcast_to(r[:, None], (P, NT))], 2).copy()
    c["pos_rows"] = np.broadcast_to(np.stack([r + 1, P - r]), (P, 2, P)).astype(np.float32).copy()
    c["pos_cols"] = np.stack([P - 1 - r, r], 1).astype(np.float32)
    return c


CONST = shape_constants()


def build(nc, I, O):
    ctx = ExitStack()
    with ctx:
        indirect = [[ctx.enter_context(nc.semaphore(f"{n}_l{l}")) for n in ("rows_in0", "rows_in1", "rows_adding")]
                    for l in range(DEPTH)]
        taken = {}

        def sem(name):
            if name not in taken:
                taken[name] = ctx.enter_context(nc.semaphore(name))
            return taken[name]

        WORDS = 53100
        arena = ctx.enter_context(nc.sbuf_tensor("arena", [P, WORDS], F32))
        PS = ctx.enter_context(nc.psum_tensor("PS", [P, 8, 512], F32))
        modD = nc.dram_tensor("mod_rows", (DEPTH, 2, 6 * D), F32, kind="Internal").ap()
        hD = nc.dram_tensor("h_rows", (TOK, D), F32, kind="Internal").ap()
        mD = nc.dram_tensor("mid_rows", (TOK, D), F32, kind="Internal").ap()
        yD = nc.dram_tensor("expert_sum", (TOK, D), F32, kind="Internal").ap()

        def at(off, *dims, parts=P):
            n = int(np.prod(dims))
            assert off + n <= WORDS, (off, dims)
            v = arena[0:parts, off:off + n]
            if len(dims) == 2:
                v = v.rearrange("p (a b) -> p a b", a=dims[0])
            elif len(dims) == 3:
                v = v.rearrange("p (a b c) -> p a b c", a=dims[0], b=dims[1])
            elif len(dims) == 4:
                v = v.rearrange("p (a b c d) -> p a b c d", a=dims[0], b=dims[1], c=dims[2])
            return v

        top = WORDS
        top -= 128
        ident = at(top, P)
        top -= 16
        condT = at(top, 2, KD)
        top -= 64
        modc = at(top, 4, KD, 2)
        top -= 64
        small = at(top, 64)
        FREE = top

        stage_done = sem("stage_done")
        n_stage = {}
        dve_seq, act_seq = sem("dve_seq"), sem("act_seq")

        def stage_end(eng, name):
            n_stage[name] = n_stage.get(name, 0) + 1
            eng.drain().then_inc(stage_done, 1)
            eng.wait_ge(stage_done, 5 * n_stage[name])

        def rows_of(t, l):
            if l:
                return hD[t * P:(t + 1) * P, :]
            return I["x_sample"][0, t * P:(t + 1) * P, :] if t < NL else I["x_prompt"][0, :, :]

        class Modulation:
            def __init__(s, l, base):
                s.l = l
                s.raw = at(base, P, parts=16)
                s.silu = at(base + 128, P, parts=16)
                s.bias = at(base + 256, 6 * D, parts=2)
                s.row = at(base + 256 + 6 * D, 6 * D, parts=2)
                s.W = [at(base + 256 + 12 * D + b * 4096, KD, 512) for b in range(4)]
                s.ld, s.wl = sem(f"mod_small_in"), [sem(f"mod_w_in_{b}") for b in range(4)]
                s.full, s.evac = sem(f"mod_full"), sem(f"mod_evac")
                s.cond, s.condps, s.st = sem(f"mod_cond"), sem(f"mod_cond_t"), sem(f"mod_store")
                s.colf = sem(f"mod_col_full")

            def sync(s, sp):
                l = s.l
                if l == 0:
                    sp.dma_start(ident, I["ident"]).then_inc(s.ld, 16)
                    sp.dma_start(s.raw[0:8, :], I["c"][0, :].rearrange("(k p) -> k p", p=P)).then_inc(s.ld, 16)
                    sp.dma_start(s.raw[8:16, :], I["c_ctx"].rearrange("(k p) -> k p", p=P)).then_inc(s.ld, 16)
                for c in range(2):
                    sp.dma_start(s.bias[c:c + 1, :], I["ada_b"][l:l + 1, :]).then_inc(s.ld, 16)
                for n in range(12):
                    s.load(sp, n)
                s.store(sp)

            def load(s, sp, n):
                if n >= 4:
                    sp.wait_ge(s.full, n - 3)
                sp.dma_start(s.W[n % 4], I["ada_w"][s.l, :, n * 512:(n + 1) * 512]
                             .rearrange("(k p) n -> p k n", p=P)).then_inc(s.wl[n % 4], 16)

            def store(s, sp):
                l = s.l
                sp.wait_ge(s.evac, 12)
                sp.dma_start(modD[l], s.row).then_inc(s.st, 16)
                sp.wait_ge(s.st, 16)

            def pe(s, pe):
                if s.l == 0:
                    pe.wait_ge(s.cond, 1)
                    pe.transpose(PS[:, 7, 0:16], s.silu, ident[0:16, 0:16]).then_inc(s.condps, 1)
                    pe.wait_ge(s.cond, 2)
                for n in range(12):
                    pe.wait_ge(s.wl[n % 4], 16 * (n // 4 + 1))
                    if n >= 4:
                        pe.wait_ge(s.evac, n - 3)
                    for k in range(KD):
                        m = pe.matmul(PS[0:2, n % 4, :], condT[:, :, k], s.W[n % 4][:, k, :], start=k == 0, stop=k == KD - 1)
                    m.then_inc(s.full, 1)
                pe.wait_ge(s.evac, 12)
                for i, kind in enumerate((0, 1, 3, 4)):
                    for k in range(KD):
                        j = kind * KD + k
                        m = pe.transpose(PS[:, 6, (i * KD + k) * 2:(i * KD + k) * 2 + 2], s.row[:, j * P:(j + 1) * P],
                                         ident[0:2, 0:2])
                m.then_inc(s.colf, 1)

            def act(s, act, ch):
                if s.l == 0:
                    act.wait_ge(s.ld, 80)
                    act.activation(s.silu, s.raw, ACT.Silu).then_inc(s.cond, 1)
                    act.wait_ge(s.condps, 1)
                    act.copy(condT.rearrange("p a b -> p (a b)"), PS[:, 7, 0:16]).then_inc(s.cond, 1)

            def dve(s, dve, ch):
                dve.wait_ge(s.ld, 32 if s.l else 80)
                for n in range(12):
                    s.add_bias(dve, n)
                s.columns(dve, ch)

            def add_bias(s, dve, n):
                dve.wait_ge(s.full, n + 1)
                dve.tensor_tensor(s.row[:, n * 512:(n + 1) * 512], PS[0:2, n % 4, :],
                                  s.bias[:, n * 512:(n + 1) * 512], ALU.add).then_inc(s.evac, 1)

            def columns(s, dve, ch):
                dve.wait_ge(s.colf, 1)
                ch.link(dve.tensor_copy(modc.rearrange("p a b c -> p (a b c)"), PS[:, 6, 0:64]))
                for kind in (1, 3):
                    v = modc[:, kind, :, :].rearrange("p a b -> p (a b)")
                    ch.link(dve.tensor_scalar(v, v, 1.0, None, ALU.add))

        def modulate_tile(eng, out, psum, kind, k, lat, act):
            g = 0 if lat else 1
            sc, sh = modc[:, kind + 1, k, g:g + 1], modc[:, kind, k, g:g + 1]
            if act:
                return eng.activation(out, psum, ACT.Identity, bias=sh, scale=sc)
            return eng.tensor_scalar(out, psum, sc, sh, ALU.mult, ALU.add)

        class MixerInput:
            def __init__(s, l, uT, scratch):
                s.l, s.uT = l, uT
                s.x = [at(scratch + b * D, D) for b in range(3)]
                s.ld = [sem(f"u_in_{b}") for b in range(3)]
                s.full, s.ea, s.ed = sem(f"u_full"), sem(f"u_evac_act"), sem(f"u_evac_dve")

            def sync(s, sp):
                for t in range(NT):
                    if t >= 3:
                        sp.wait_ge(s.full, t - 2)
                    sp.dma_start(s.x[t % 3], rows_of(t, s.l)).then_inc(s.ld[t % 3], 16)

            def pe(s, pe):
                for t in range(NT):
                    pe.wait_ge(s.ld[t % 3], 16 * (t // 3 + 1))
                    if t >= 2:
                        pe.wait_ge(s.ea, t - 1)
                        pe.wait_ge(s.ed, t - 1)
                    for k in range(KD):
                        m = pe.transpose(PS[:, t % 2 * 2 + k // 4, k % 4 * P:k % 4 * P + P],
                                         s.x[t % 3][:, k * P:(k + 1) * P], ident)
                    m.then_inc(s.full, 1)

            def evac(s, eng, bank, sm):
                for t in range(NT):
                    eng.wait_ge(s.full, t + 1)
                    for k in range(bank * 4, bank * 4 + 4):
                        m = modulate_tile(eng, s.uT[:, k, t * P:(t + 1) * P],
                                          PS[:, t % 2 * 2 + bank, k % 4 * P:k % 4 * P + P], 0, k, t < NL, bank == 0)
                    m.then_inc(sm, 1)

            def act(s, act, ch):
                s.evac(act, 0, s.ea)

            def dve(s, dve, ch):
                s.evac(dve, 1, s.ed)

        JOBS = ["diag"] + [f"lev{d}{l}" for d in range(2) for l in range(7)] + ["tk0", "tk1", "U0", "U1", "o", "yt"]
        BY_ACT = [j for j in JOBS if j[:2] in ("tk", "yt") or j == "o"]
        PT = 18
        BY_DVE = [j for j in JOBS if j not in BY_ACT]

        class Hgrn:

            def __init__(s, uT, yT, a, b, c):
                s.uT, s.yT = uT, yT
                o = [a, b, c]

                def take(n, which=0):
                    r = o[which]
                    o[which] += n
                    return r
                s.W = at(take(5 * 1024), 5, KD, P)
                two = lambda w: [at(take(TOK), NT, P), at(take(TOK, w), NT, P)]
                s.qT = two(2)
                s.z = [list(zz) for zz in zip(two(2), two(2))]
                s.kT = [at(take(TOK), NT, P) for _ in range(2)]
                s.f = [at(take(TOK), NT, P) for _ in range(2)]
                s.X = [at(take(NT * 129), NT, 129) for _ in range(2)]
                s.v = two(2)
                s.g = two(0)
                s.dist = [at(take(TOK), NT, P) for _ in range(2)]
                s.G = [at(take(TOK), NT, P) for _ in range(2)]
                s.attn = at(take(TOK, 1), NT, P)
                s.ks = [at(take(TOK, 1), NT, P) for _ in range(2)]
                s.S = [at(take(TOK, 1), NT, P) for _ in range(2)]
                s.masks = at(take(15 * P, 1), 15, P)
                s.eT = [at(take(NT, 1), NT) for _ in range(2)]
                s.nw = at(take(AW, 1), AW)
                s.ss = at(take(2 * NT, 1), 2, NT)
                s.ones = at(take(P, 1), P)
                assert o[0] <= 33792 and o[1] <= FREE and o[2] <= c + 4 * TOK, o
                s.Aq, s.Bk = s.z, s.f
                s.o, s.ksum = s.G[0], s.dist[0]
                s.wld, s.wfree = sem("hg_w_in"), sem("hg_w_free")
                s.cld, s.s0 = sem("hg_const_in"), sem("hg_s0_in")
                s.full, s.ea, s.ed = sem("hg_full"), sem("hg_evac_act"), sem("hg_evac_dve")
                s.silu = sem("hg_silu")
                s.pfull, s.pevac = sem("hg_proj_full"), sem("hg_proj_evac")
                s.floor, s.ln, s.prep = sem("hg_floor"), sem("hg_ln"), sem("hg_prep")
                s.dd, s.ex, s.gg = sem("hg_dist"), sem("hg_exp"), sem("hg_scaled")
                s.sok, s.sv = sem("hg_states"), sem("hg_state_out")
                s.ssum, s.rt, s.yok = sem("hg_sumsq"), sem("hg_sqrt"), sem("hg_y")

            def free_count(s, eng, job, h):
                n = JOBS.index(job)
                p = n - 2
                if p < 0:
                    if h == 0:
                        return
                    h, p = h - 1, len(JOBS) - 1 - n
                prev = JOBS[p]
                if prev in BY_ACT:
                    eng.wait_ge(s.ea, h * len(BY_ACT) + BY_ACT.index(prev) + 1)
                else:
                    eng.wait_ge(s.ed, h * len(BY_DVE) + BY_DVE.index(prev) + 1)

            def banks(s, job):
                g = JOBS.index(job) % 2 * 3
                return PS[:, g:g + 3, :]

            def wait_full(s, eng, job, h):
                eng.wait_ge(s.full, h * len(JOBS) + JOBS.index(job) + 1)

            def wait_act(s, eng, job, h):
                eng.wait_ge(s.ea, h * len(BY_ACT) + BY_ACT.index(job) + 1)

            def sync(s, sp):
                sp.dma_start(s.masks, I["gram_masks"]).then_inc(s.cld, 16)
                nw = I["hgrn_norm_w"][0:1, :]
                sp.dma_start(s.nw, nw.to_broadcast((P, AW))).then_inc(s.cld, 16)
                def weights(h):
                    if h:
                        sp.wait_ge(s.pfull, PT * h)
                    for j, part in enumerate((0, 2, 3, 1, 4)):
                        c0 = part * AW + h * P
                        sp.dma_start(s.W[:, j, :, :], I["even_w_in"][0, :, c0:c0 + P]
                                     .rearrange("(k p) n -> p k n", p=P)).then_inc(s.wld, 16)
                weights(0)
                for h in range(A_H):
                    if h:
                        sp.wait_ge(s.full, (h - 1) * len(JOBS) + JOBS.index("o") + 1)
                        sp.wait_ge(s.sv, 32 * h)
                    for d in range(2):
                        sp.dma_start(s.S[d][:, 0 if d == 0 else NL - 1, :], I["state_hgrn"][0, 0, d, h]).then_inc(s.s0, 16)
                    if h + 1 < A_H:
                        weights(h + 1)
                    sp.wait_ge(s.sok, 2 * h + 2)
                    for d in range(2):
                        sp.dma_start(O["new_state_hgrn"][0, 0, d, h], s.S[d][:, NL, :]).then_inc(s.sv, 16)
                sp.wait_ge(s.sv, 32 * A_H)

            def pe_project(s, pe, h, i):
                n = h * PT + i
                if n >= 2:
                    pe.wait_ge(s.pevac, n - 1)
                if i == 0:
                    pe.wait_ge(s.wld, 80 * (h + 1))
                for k in range(KD):
                    if i < 9:
                        m = pe.matmul(PS[:, 6 + n % 2, 0:NCH], s.W[:, i // 3, k, :], s.uT[:, k, i % 3 * NCH:(i % 3 + 1) * NCH],
                                      start=k == 0, stop=k == KD - 1)
                    else:
                        t = i - 9
                        m = pe.matmul(PS[:, 6 + n % 2, 0:256], s.uT[:, k, t * P:(t + 1) * P], s.W[:, 3:5, k, :],
                                      start=k == 0, stop=k == KD - 1)
                m.then_inc(s.pfull, 1)

            def act_project(s, act, h, i):
                n = h * PT + i
                act.wait_ge(s.pfull, n + 1)
                if i < 9:
                    ps = PS[:, 6 + n % 2, 0:NCH].rearrange("p (a b) -> p a b", a=3)
                    third = slice(i % 3 * 3, i % 3 * 3 + 3)
                    dst = s.qT[h % 2] if i < 3 else s.z[h % 2][i // 3 - 1]
                    m = act.copy(dst[:, third, :], ps)
                else:
                    act.copy(s.g[h % 2][:, i - 9, :], PS[:, 6 + n % 2, P:2 * P])
                    m = act.copy(s.v[h % 2][:, i - 9, :], PS[:, 6 + n % 2, 0:P])
                m.then_inc(s.pevac, 1)

            def pe(s, pe):
                for i in range(PT):
                    s.pe_project(pe, 0, i)
                for h in range(A_H):
                    ahead = (lambda i: s.pe_project(pe, h + 1, i)) if h + 1 < A_H else (lambda i: None)
                    s.free_count(pe, "diag", h)
                    pe.wait_ge(s.prep, h + 1)
                    ps = s.banks("diag")
                    for c in range(NT):
                        m = pe.matmul(ps[:, c // 3, c % 3 * P:c % 3 * P + P], s.ksum[:, c, :], s.qT[h % 2][:, c, :])
                    m.then_inc(s.full, 1)
                    ahead(0)
                    for n in range(14):
                        job = f"lev{n // 7}{n % 7}"
                        s.free_count(pe, job, h)
                        pe.wait_ge(s.gg, h * 18 + n + 1)
                        ps = s.banks(job)
                        for c in range(NT):
                            g = s.G[n % 2][:, c, :]
                            m = pe.matmul(ps[:, c // 3, c % 3 * P:c % 3 * P + P], g, g)
                        m.then_inc(s.full, 1)
                        ahead(n + 1)
                    for d in range(2):
                        s.free_count(pe, f"tk{d}", h)
                        pe.wait_ge(s.gg, h * 18 + 14 + 2 * d + 2)
                        ps = s.banks(f"tk{d}")
                        for c in range(NT):
                            m = pe.transpose(ps[:, c // 3, c % 3 * P:c % 3 * P + P], s.Bk[d][:, c, :], ident)
                        m.then_inc(s.full, 1)
                        ahead(15 + d)
                    for d in range(2):
                        s.free_count(pe, f"U{d}", h)
                        s.wait_act(pe, f"tk{d}", h)
                        ps = s.banks(f"U{d}")
                        for c in range(NT):
                            m = pe.matmul(ps[:, c // 3, c % 3 * P:c % 3 * P + P], s.ks[d][:, c, :], s.v[h % 2][:, c, :])
                        m.then_inc(s.full, 1)
                        if d == 0:
                            ahead(17)
                    s.free_count(pe, "o", h)
                    pe.wait_ge(s.sok, 2 * h + 2)
                    ps = s.banks("o")
                    for c in range(NT):
                        out = ps[:, c // 3, c % 3 * P:c % 3 * P + P]
                        m = pe.matmul(out, s.attn[:, c, :], s.v[h % 2][:, c, :], start=True, stop=c == NL)
                        if c < NL:
                            for d in range(2):
                                m = pe.matmul(out, s.Aq[h % 2][d][:, c, :], s.S[d][:, c, :], start=False, stop=d == 1)
                    m.then_inc(s.full, 1)
                    s.free_count(pe, "yt", h)
                    pe.wait_ge(s.yok, h + 1)
                    ps = s.banks("yt")
                    for c in range(NT):
                        m = pe.transpose(ps[:, c // 3, c % 3 * P:c % 3 * P + P], s.o[:, c, :], ident)
                    m.then_inc(s.full, 1)

            def act(s, act, ch):
                third = lambda v, n: v[:, 3 * n:3 * n + 3, :]
                ps3 = lambda ps, n: ps[:, n, 0:NCH].rearrange("p (a b) -> p a b", a=3)
                for i in range(PT):
                    s.act_project(act, 0, i)
                for h in range(A_H):
                    z = s.z[h % 2]
                    ahead = (lambda i: s.act_project(act, h + 1, i)) if h + 1 < A_H else (lambda i: None)
                    act.wait_ge(s.pevac, PT * (h + 1))
                    for d in range(2):
                        act.activation(s.kT[d], z[d], ACT.Sigmoid, scale=-1.0)
                        act.activation(s.f[d], z[d], ACT.Sigmoid).then_inc(s.floor, 1)
                    act.activation(s.qT[h % 2], s.qT[h % 2], ACT.Silu)
                    act.activation(s.g[h % 2], s.g[h % 2], ACT.Silu).then_inc(s.silu, 1)
                    for d in range(2):
                        act.wait_ge(s.ln, h * 4 + d + 1)
                        act.activation(s.f[d], s.f[d], ACT.Ln).then_inc(s.floor, 1)
                    for n in range(14):
                        act.wait_ge(s.dd, h * 16 + n + 1)
                        act.activation(s.dist[n % 2], s.dist[n % 2], ACT.Exp).then_inc(s.ex, 1)
                        if n >= 1:
                            ahead(n - 1)
                    for d in range(2):
                        act.wait_ge(s.dd, h * 16 + 14 + d + 1)
                        x = s.X[d][:, :, 1 - d:129 - d]
                        act.activation(s.dist[0], s.dist[0], ACT.Exp)
                        act.activation(s.dist[1], x, ACT.Exp)
                        act.activation(s.eT[d], s.X[d][:, :, 128], ACT.Exp).then_inc(s.ex, 1)
                        ahead(13 + d)
                    for d in range(2):
                        s.wait_full(act, f"tk{d}", h)
                        for n in range(3):
                            m = act.copy(third(s.ks[d], n), ps3(s.banks(f"tk{d}"), n))
                        m.then_inc(s.ea, 1)
                    for i in range(15, PT):
                        ahead(i)
                    s.wait_full(act, "o", h)
                    for n in range(3):
                        m = act.copy(third(s.o, n), ps3(s.banks("o"), n))
                    m.then_inc(s.ea, 1)
                    act.wait_ge(s.ssum, h + 1)
                    act.activation(s.ss[:, 1, :], s.ss[:, 0, :], ACT.Sqrt).then_inc(s.rt, 1)
                    s.wait_full(act, "yt", h)
                    for n in range(3):
                        m = act.copy(s.yT[:, h, n * NCH:(n + 1) * NCH], s.banks("yt")[:, n, 0:NCH])
                    m.then_inc(s.ea, 1)

            def dve(s, dve, ch):
                ch.link(dve.memset(s.ones, 1.0))
                for d in range(2):
                    ch.link(dve.memset(s.X[d][:, :, 0:1], 0.0))
                dve.wait_ge(s.cld, 32)
                ch.link(dve.memset(s.attn, 0.0))
                for h in range(A_H):
                    z, Aq, qT = s.z[h % 2], s.Aq[h % 2], s.qT[h % 2]
                    for d in range(2):
                        dve.wait_ge(s.floor, h * 4 + d + 1)
                        dve.tensor_scalar(z[d], z[d], LOG_FLOOR, 0.0, ALU.add, ALU.min)
                        dve.tensor_scalar(s.f[d], s.f[d], math.exp(-LOG_FLOOR), None, ALU.max).then_inc(s.ln, 1)
                    for d in range(2):
                        dve.wait_ge(s.floor, h * 4 + 3 + d)
                        ch.link(dve.scalar_tensor_tensor(z[d], z[d], math.log(1e-30) + LOG_FLOOR, s.f[d],
                                                         ALU.max, ALU.add))
                        for c in range(NT):
                            m = dve.tensor_tensor_scan(s.X[d][:, c, 1:129], s.ones, z[d][:, c, :], 0.0, ALU.mult, ALU.add)
                        m.then_inc(s.ln, 1)
                    if h:
                        s.wait_full(dve, "yt", h - 1)
                    dve.wait_ge(s.silu, h + 1)
                    dve.tensor_tensor(s.ksum, s.kT[0], s.kT[1], ALU.add).then_inc(s.prep, 1)
                    s.wait_full(dve, "diag", h)
                    s.dve_keep(dve, h, "diag", 0)
                    dve.wait_ge(s.ln, h * 4 + 4)
                    for n in range(15):
                        if n < 14:
                            s.level_dist(dve, h, n)
                        if n > 0:
                            s.level_scale(dve, h, n - 1)
                            if n > 1:
                                job = f"lev{(n - 2) // 7}{(n - 2) % 7}"
                                s.wait_full(dve, job, h)
                                s.dve_keep(dve, h, job, n - 1)
                    s.wait_full(dve, "lev16", h)
                    s.dve_keep(dve, h, "lev16", 14)
                    for d in range(2):
                        x = s.X[d][:, :, 1 - d:129 - d]
                        tot = s.X[d][:, :, 128:129].to_broadcast((P, NT, P))
                        if d:
                            dve.wait_ge(s.gg, h * 18 + 16)
                        dve.tensor_tensor(s.dist[0], tot, x, ALU.subtract).then_inc(s.dd, 1)
                        dve.wait_ge(s.ex, h * 16 + 14 + d + 1)
                        to_end, from_start = (0, 1) if d == 0 else (1, 0)
                        dve.tensor_tensor(Aq[d], qT, s.dist[from_start], ALU.mult).then_inc(s.gg, 1)
                        dve.tensor_tensor(s.Bk[d], s.kT[d], s.dist[to_end], ALU.mult).then_inc(s.gg, 1)
                    dve.wait_ge(s.s0, 32 * (h + 1))
                    for d in range(2):
                        s.wait_full(dve, f"U{d}", h)
                        ps = s.banks(f"U{d}")
                        U = lambda c: ps[:, c // 3, c % 3 * P:c % 3 * P + P]
                        order = range(NL - 1) if d == 0 else range(NL - 1, 0, -1)
                        for c in order:
                            nxt = c + 1 if d == 0 else c - 1
                            ch.link(dve.scalar_tensor_tensor(s.S[d][:, nxt, :], s.S[d][:, c, :], s.eT[d][:, c:c + 1], U(c),
                                                             ALU.mult, ALU.add))
                        ch.link(dve.tensor_copy(s.S[d][:, NL, :], U(NL)))
                        dve.engine_nop().then_inc(s.sok, 1)
                        dve.engine_nop().then_inc(s.ed, 1)
                    s.wait_act(dve, "o", h)
                    ch.link(dve.tensor_tensor(s.G[1], s.o, s.o, ALU.mult))
                    ch.link(dve.tensor_reduce(s.ss[:, 0, :], s.G[1], AX.X, ALU.add))
                    dve.tensor_scalar(s.ss[:, 0, :], s.ss[:, 0, :], 1.0 / P, EPS, ALU.mult, ALU.add).then_inc(s.ssum, 1)
                    dve.wait_ge(s.rt, h + 1)
                    ch.link(dve.reciprocal(s.ss[:, 1, :], s.ss[:, 1, :]))
                    rstd = s.ss[:, 1, :].rearrange("p (a b) -> p a b", b=1).to_broadcast((P, NT, P))
                    nw = s.nw[:, h * P:(h + 1) * P].rearrange("p (a b) -> p a b", a=1).to_broadcast((P, NT, P))
                    ch.link(dve.tensor_tensor(s.o, s.o, rstd, ALU.mult))
                    ch.link(dve.tensor_tensor(s.o, s.o, nw, ALU.mult))
                    dve.tensor_tensor(s.o, s.o, s.g[h % 2], ALU.mult).then_inc(s.yok, 1)

            def dve_keep(s, dve, h, job, mask):
                if h and job == "diag":
                    s.wait_full(dve, "o", h - 1)
                if job != "diag":
                    dve.wait_ge(s.ed, h * len(BY_DVE) + BY_DVE.index(job))
                for n in range(3):
                    m = dve.copy_predicated(s.attn[:, 3 * n:3 * n + 3, :],
                                            s.masks[:, mask:mask + 1, :].bitcast(U32).to_broadcast((P, 3, P)),
                                            s.banks(job)[:, n, 0:NCH].rearrange("p (a b) -> p a b", a=3))
                m.then_inc(s.ed, 1)

            def halves(s, v, hs):
                w = v.rearrange("p c (b two s) -> p c b two s", two=2, s=hs)
                return w[:, :, :, 0, :], w[:, :, :, 1, :]

            def level_dist(s, dve, h, n):
                d, hs = n // 7, 64 >> (n % 7)
                nb = 64 // hs
                first, second = s.halves(s.X[d][:, :, 1 - d:129 - d], hs)
                o1, o2 = s.halves(s.dist[n % 2], hs)
                ref = s.X[d][:, :, 0:128].rearrange("p c (b s) -> p c b s", s=2 * hs)[:, :, :, hs:hs + 1] \
                    .to_broadcast((P, NT, nb, hs))
                if n >= 2:
                    dve.wait_ge(s.gg, h * 18 + n - 1)
                else:
                    s.wait_full(dve, "diag", h)
                dve.tensor_tensor(o1, ref, first, ALU.subtract)
                dve.tensor_tensor(o2, second, ref, ALU.subtract).then_inc(s.dd, 1)

            def level_scale(s, dve, h, n):
                d, hs = n // 7, 64 >> (n % 7)
                dve.wait_ge(s.ex, h * 16 + n + 1)
                if n >= 2:
                    s.wait_full(dve, f"lev{(n - 2) // 7}{(n - 2) % 7}", h)
                e1, e2 = s.halves(s.dist[n % 2], hs)
                g1, g2 = s.halves(s.G[n % 2], hs)
                q1, q2 = s.halves(s.qT[h % 2], hs)
                k1, k2 = s.halves(s.kT[d], hs)
                a, b = (k1, q2) if d == 0 else (q1, k2)
                dve.tensor_tensor(g1, e1, a, ALU.mult)
                dve.tensor_tensor(g2, e2, b, ALU.mult).then_inc(s.gg, 1)

        class HyenaIn:
            def __init__(s, uT, base, hv, hx1, yT):
                s.uT, s.hv, s.hx1, s.yT = uT, hv, hx1, yT
                s.W = [at(base + b * 1024, KD, P) for b in range(2)]
                s.raw = [at(base + 2048 + b * 1156, 1155) for b in range(2)]
                s.y = [at(base + 2048 + 2312 + b * 1156, 1153) for b in range(2)]
                s.cw = at(base + 7000, P, parts=48)
                s.cols = at(base + 7200, 4, 12)
                s.wl = [sem(f"hyi_w_in{b}") for b in range(2)]
                s.cl, s.ct, s.cok = sem("hyi_conv_in"), sem("hyi_conv_t"), sem("hyi_conv_cols")
                s.pads = sem("hyi_pads")
                s.full, s.evac, s.conv = sem("hyi_full"), sem("hyi_evac"), sem("hyi_conv")
                s.tfull, s.tevac = sem("hyi_t_full"), sem("hyi_t_evac")

            def sync(s, sp):
                sp.dma_start(s.cw[0:36, :], I["hyena_conv_w"][0].rearrange("j (c p) -> (j c) p", p=P)).then_inc(s.cl, 16)
                sp.dma_start(s.cw[36:48, :], I["hyena_conv_b"][0].rearrange("(c p) -> c p", p=P)).then_inc(s.cl, 16)
                for c in range(12):
                    if c >= 2:
                        sp.wait_ge(s.full, c - 1)
                    c0 = 5 * AW + c * P
                    sp.dma_start(s.W[c % 2], I["even_w_in"][0, :, c0:c0 + P]
                                 .rearrange("(k p) n -> p k n", p=P)).then_inc(s.wl[c % 2], 16)

            def pe(s, pe):
                pe.wait_ge(s.cl, 32)
                pe.transpose(PS[:, 7, 0:48], s.cw, ident[0:48, 0:48]).then_inc(s.ct, 1)

                def turn(c):
                    pe.wait_ge(s.conv, c + 1)
                    if c:
                        pe.wait_ge(s.tevac, c)
                    for t in range(NT):
                        src = s.y[c % 2][:, t * P + t // NL:t * P + t // NL + P]
                        m = pe.transpose(PS[:, 3 + t // 3, t % 3 * P:t % 3 * P + P], src, ident)
                    m.then_inc(s.tfull, 1)
                for c in range(12):
                    pe.wait_ge(s.wl[c % 2], 16 * (c // 2 + 1))
                    if c:
                        pe.wait_ge(s.evac, c)
                    for n in range(3):
                        for k in range(KD):
                            m = pe.matmul(PS[:, n, 0:NCH], s.W[c % 2][:, k, :], s.uT[:, k, n * NCH:(n + 1) * NCH],
                                          start=k == 0, stop=k == KD - 1)
                    m.then_inc(s.full, 1)
                    if 0 < c <= 8:
                        turn(c - 1)

            def act(s, act, ch):
                act.wait_ge(s.pads, 1)
                for c in range(12):
                    act.wait_ge(s.full, c + 1)
                    if c >= 2:
                        act.wait_ge(s.conv, c - 1)
                    raw = s.raw[c % 2]
                    act.copy(raw[:, 1:385], PS[:, 0, 0:NCH])
                    act.copy(raw[:, 385:769], PS[:, 1, 0:NCH])
                    act.copy(raw[:, 769:1025], PS[:, 2, 0:256])
                    act.copy(raw[:, 1026:1154], PS[:, 2, 256:384]).then_inc(s.evac, 1)
                    if 0 < c <= 8:
                        s.act_turn(act, c - 1)

            def act_turn(s, act, c):
                act.wait_ge(s.tfull, c + 1)
                dst = s.hv if c < 4 else s.hx1
                for n in range(3):
                    m = act.copy(dst[:, 3 * n:3 * n + 3, c % 4 * P:c % 4 * P + P],
                                 PS[:, 3 + n, 0:NCH].rearrange("p (a b) -> p a b", a=3))
                m.then_inc(s.tevac, 1)

            def dve(s, dve, ch):
                for b in range(2):
                    dve.memset(s.raw[b][:, 0:1], 0.0)
                    dve.memset(s.raw[b][:, 1025:1026], 0.0)
                    m = dve.memset(s.raw[b][:, 1154:1155], 0.0)
                m.then_inc(s.pads, 1)
                dve.wait_ge(s.ct, 1)
                ch.link(dve.tensor_copy(s.cols.rearrange("p a b -> p (a b)"), PS[:, 7, 0:48]))
                for c in range(12):
                    raw, y = s.raw[c % 2], s.y[c % 2]
                    dve.wait_ge(s.evac, c + 1)
                    if c >= 2 and c <= 9:
                        dve.wait_ge(s.tfull, c - 1)
                    w = [s.cols[:, j, c:c + 1] for j in range(4)]
                    if c < 8:
                        pieces = [(y[:, 0:512], [raw[:, q:q + 512] for q in range(3)]),
                                  (y[:, 512:1024], [raw[:, 1023 + q:511 + q:-1] for q in range(3)]),
                                  (y[:, 1025:1153], [raw[:, 1025 + q:1153 + q] for q in range(3)])]
                        for o, x in pieces:
                            m = dve.tensor_scalar(o, x[0], w[0], w[3], ALU.mult, ALU.add)
                        ch.link(m)
                        for o, x in pieces:
                            m = dve.scalar_tensor_tensor(o, x[1], w[1], o, ALU.mult, ALU.add)
                        ch.link(m)
                        for o, x in pieces:
                            m = dve.scalar_tensor_tensor(o, x[2], w[2], o, ALU.mult, ALU.add)
                        m.then_inc(s.conv, 1)
                    else:
                        ch.link(dve.tensor_scalar(y, raw[:, 0:1153], w[0], w[3], ALU.mult, ALU.add))
                        ch.link(dve.scalar_tensor_tensor(y, raw[:, 1:1154], w[1], y, ALU.mult, ALU.add))
                        o = s.yT[:, c - 4, :]
                        dve.scalar_tensor_tensor(o[:, 0:1024], raw[:, 2:1026], w[2], y[:, 0:1024], ALU.mult, ALU.add)
                        dve.scalar_tensor_tensor(o[:, 1024:1152], raw[:, 1027:1155], w[2], y[:, 1025:1153],
                                                 ALU.mult, ALU.add).then_inc(s.conv, 1)

        class HyenaConv:

            def __init__(s, name, hv, hx1, yT, dft, hbase, scratch):
                s.name, s.hv, s.hx1, s.yT = name, hv, hx1, yT
                s.L = L_LAT if name == "lat" else L_CTX
                s.nt = s.L // P
                s.t0 = 0 if name == "lat" else NL
                s.tw = min(s.L, 512)
                nt = s.nt
                s.C, s.S = dft[:, 0], dft[:, 1]
                s.dft = dft
                s.Hr, s.Hi = at(hbase, nt, 256), at(hbase + nt * 256, nt, 256)
                s.A, s.B = at(hbase + nt * 512, nt, 256), at(hbase + nt * 768, nt, 256)
                o = scratch
                s.hdn = at(o, s.L + 1, parts=64)
                s.arg = at(o + 1026, s.L, parts=64)
                s.rnd = at(o + 2052, s.L, parts=64)
                s.dec = [at(o + 1026 + b * 512, 2, 256) for b in range(2)]
                s.tmp = [at(o + 2050 + b * 256, 256) for b in range(4)]
                s.drow = at(o + 3078, 2, 512, parts=1)
                s.z = at(o + 4102, L_LAT, parts=33)[:, 0:s.L]
                s.w3 = at(o + 4102 + 1024, 2, 2, 512, parts=64)
                s.w1, s.w2 = at(o + 7174, 64, parts=33), at(o + 7238, 64, parts=64)
                s.v4 = at(o + 7302, 64, parts=4)
                s.c4 = at(o + 7366, 4, parts=64)
                s.rot = at(o + 7370, 2, nt)
                sm = lambda n: sem(f"hy_{n}")
                s.ld, s.dl = sm("in"), [sm("decay_in0"), sm("decay_in1")]
                s.full, s.hok = sm("mlp_full"), sm("mlp_ok")
                s.a1, s.sn = sm("arg"), sm("sin")
                s.ff, s.fe = sm("filt_full"), sm("filt_evac")
                s.pf, s.pe_ = sm("spec_full"), sm("spec_evac")
                s.uf, s.ue = sm("fwd_full"), sm("fwd_evac")
                s.yf, s.ye = sm("inv_full"), sm("inv_evac")

            def sync(s, sp):
                n = s.name
                for dst, src in ((s.dft, I[f"dft_{n}"]), (s.rot, I[f"rot_{n}"]), (s.z, I[f"z_{n}"]),
                                 (s.w1, I["hyena_w1"][0]), (s.w2, I["hyena_w2"][0]),
                                 (s.w3, I["hyena_w3"][0].rearrange("h (o d c) -> h o d c", o=2, d=2)),
                                 (s.drow, I["hyena_bias"][0:1]),
                                 (s.v4[0:1, :], I["hyena_b1"][0:1, :]), (s.v4[1:2, :], I["hyena_b2"][0:1, :]),
                                 (s.v4[2:4, :], I["hyena_freq"][0])):
                    sp.dma_start(dst, src).then_inc(s.ld, 16)
                for r in range(4):
                    for j in range(s.nt):
                        i = r * s.nt + j
                        if i >= 2:
                            sp.wait_ge(s.fe, i - 1)
                        else:
                            sp.wait_ge(s.hok, 3)
                        sp.dma_start(s.dec[i % 2], I[f"decay_{n}"][r // 2, j]).then_inc(s.dl[i % 2], 16)

            def pe(s, pe):
                pe.wait_ge(s.ld, 160)
                pe.transpose(PS[0:64, 7, 0:4], s.v4, ident[0:4, 0:4]).then_inc(s.full, 1)
                nw = s.L // s.tw
                for layer in range(2):
                    if layer:
                        pe.wait_ge(s.hok, 2)
                    for n in range(nw):
                        sl = slice(n * s.tw, (n + 1) * s.tw)
                        lhs, rhs = (s.w2, s.hdn[:, sl]) if layer else (s.w1, s.z[:, sl])
                        m = pe.matmul(PS[0:64, n + 2 * layer, 0:s.tw], lhs, rhs, start=True, stop=True)
                    m.then_inc(s.full, 1)
                pe.wait_ge(s.hok, 3)
                nt = s.nt
                n_t = n_p = n_u = n_y = 0
                for r in range(4):
                    half, o = r // 2, r % 2
                    cs = slice(half * 256, half * 256 + 256)
                    for j in range(nt):
                        if n_t >= 2:
                            pe.wait_ge(s.fe, n_t - 1)
                        for d in range(2):
                            m = pe.matmul(PS[:, n_t % 2, d * 256:d * 256 + 256], s.hdn[:, j * P + d:j * P + d + P],
                                          s.w3[:, o, d, cs], start=True, stop=True)
                        m.then_inc(s.ff, 1)
                        n_t += 1
                    pe.wait_ge(s.fe, n_t)
                    for kt in range(nt):
                        if n_p >= 2:
                            pe.wait_ge(s.pe_, n_p - 1)
                        b = 2 + n_p % 2 * 2
                        for tab, x, q in ((s.C, s.A, 0), (s.S, s.B, 1)):
                            for j in range(nt):
                                m = pe.matmul(PS[:, b + q, 0:256], tab[:, j, kt * P:kt * P + P], x[:, j, :],
                                              start=j == 0, stop=j == nt - 1)
                        m.then_inc(s.pf, 1)
                        n_p += 1
                    if o == 1:
                        pe.wait_ge(s.ye, n_y)
                    pe.wait_ge(s.pe_, n_p)
                    for kt in range(nt):
                        if n_u >= 1:
                            pe.wait_ge(s.ue, n_u - (1 if kt % 2 else 1))
                        b = 2 + n_u % 2 * 2
                        for tab, q in ((s.C, 0), (s.S, 1)):
                            for j in range(nt):
                                m = pe.matmul(PS[:, b + q, 0:256], tab[:, j, kt * P:kt * P + P], s.hv[:, s.t0 + j, cs],
                                              start=j == 0, stop=j == nt - 1)
                        m.then_inc(s.uf, 1)
                        n_u += 1
                    pe.wait_ge(s.ue, n_u)
                    if o == 0:
                        for j in range(nt):
                            if n_y >= 2:
                                pe.wait_ge(s.ye, n_y - 1)
                            q = 0
                            for tab, x in ((s.C, s.A), (s.S, s.B)):
                                for kt in range(nt):
                                    m = pe.matmul(PS[:, 6 + n_y % 2, 0:256], tab[:, kt, j * P:j * P + P], x[:, kt, :],
                                                  start=q == 0, stop=q == 2 * nt - 1)
                                    q += 1
                            m.then_inc(s.yf, 1)
                            n_y += 1
                    else:
                        for ct in range(2):
                            for n in range(s.L // s.tw):
                                if n_y >= 2:
                                    pe.wait_ge(s.ye, n_y - 1)
                                q = 0
                                for tab, x in ((s.C, s.A), (s.S, s.B)):
                                    for kt in range(nt):
                                        m = pe.matmul(PS[:, 6 + n_y % 2, 0:s.tw], x[:, kt, ct * P:ct * P + P],
                                                      tab[:, kt, n * s.tw:(n + 1) * s.tw], start=q == 0, stop=q == 2 * nt - 1)
                                        q += 1
                                m.then_inc(s.yf, 1)
                                n_y += 1

            def act(s, act, ch):
                act.wait_ge(s.full, 1)
                act.copy(s.c4, PS[0:64, 7, 0:4]).then_inc(s.hok, 1)
                for layer in range(2):
                    act.wait_ge(s.a1, layer + 1)
                    m = act.activation(s.hdn[:, 0:s.L], s.arg, ACT.Sin)
                    m.then_inc(s.hok, 1)

            def dve(s, dve, ch):
                ch.link(dve.memset(s.hdn[:, s.L:s.L + 1], 0.0))
                for layer in range(2):
                    dve.wait_ge(s.hok, layer + 1)
                    dve.wait_ge(s.full, layer + 2)
                    for n in range(s.L // s.tw):
                        sl = slice(n * s.tw, (n + 1) * s.tw)
                        ch.link(dve.tensor_scalar(s.arg[:, sl], PS[0:64, n + 2 * layer, 0:s.tw], s.c4[:, layer:layer + 1],
                                                  s.c4[:, 2 + layer:3 + layer], ALU.add, ALU.mult))
                    ch.link(dve.tensor_scalar(s.rnd, s.arg, 1.0 / (2 * math.pi), None, ALU.mult))
                    ch.link(dve.tensor_scalar(s.rnd, s.rnd, BIG, None, ALU.add))
                    ch.link(dve.tensor_scalar(s.rnd, s.rnd, -BIG, None, ALU.add))
                    hi = 6.28125
                    ch.link(dve.scalar_tensor_tensor(s.arg, s.rnd, -hi, s.arg, ALU.mult, ALU.add))
                    ch.link(dve.scalar_tensor_tensor(s.arg, s.rnd, -(2 * math.pi - hi), s.arg, ALU.mult, ALU.add))
                    dve.tensor_scalar(s.arg, s.arg, 3.1415925, -3.1415925, ALU.min, ALU.max).then_inc(s.a1, 1)
                nt = s.nt
                n_t = n_p = n_u = n_y = 0
                dve.wait_ge(s.hok, 3)
                for r in range(4):
                    half, o = r // 2, r % 2
                    cs = slice(half * 256, half * 256 + 256)
                    if r:
                        dve.wait_ge(s.yf, n_y)
                    for j in range(nt):
                        dve.wait_ge(s.dl[n_t % 2], 16 * (n_t // 2 + 1))
                        dve.wait_ge(s.ff, n_t + 1)
                        a, b = s.tmp[0], s.tmp[1]
                        dve.tensor_tensor(a, PS[:, n_t % 2, 0:256], s.dec[n_t % 2][:, 0, :], ALU.mult)
                        ch.link(dve.tensor_tensor(b, PS[:, n_t % 2, 256:512], s.dec[n_t % 2][:, 1, :], ALU.mult))
                        if j == 0:
                            ch.link(dve.tensor_tensor(a[0:1, :], a[0:1, :], s.drow[:, o, cs], ALU.add))
                        dve.tensor_tensor(s.B[:, j, :], a, b, ALU.subtract)
                        ch.link(dve.tensor_tensor(s.A[:, j, :], a, b, ALU.add))
                        dve.engine_nop().then_inc(s.fe, 1)
                        n_t += 1
                    for kt in range(nt):
                        dve.wait_ge(s.pf, n_p + 1)
                        b = 2 + n_p % 2 * 2
                        c, sn = s.rot[:, 0, kt:kt + 1], s.rot[:, 1, kt:kt + 1]
                        dve.tensor_scalar(s.tmp[0], PS[:, b + 1, 0:256], sn, None, ALU.mult)
                        ch.link(dve.tensor_scalar(s.tmp[1], PS[:, b + 1, 0:256], c, None, ALU.mult))
                        dve.scalar_tensor_tensor(s.Hr[:, kt, :], PS[:, b, 0:256], c, s.tmp[0], ALU.mult, ALU.add)
                        ch.link(dve.scalar_tensor_tensor(s.Hi[:, kt, :], PS[:, b, 0:256], sn, s.tmp[1], ALU.mult, ALU.subtract))
                        dve.engine_nop().then_inc(s.pe_, 1)
                        n_p += 1
                    for kt in range(nt):
                        dve.wait_ge(s.uf, n_u + 1)
                        b = 2 + n_u % 2 * 2
                        dve.tensor_tensor(s.tmp[0], PS[:, b, 0:256], s.Hr[:, kt, :], ALU.mult)
                        dve.tensor_tensor(s.tmp[1], PS[:, b + 1, 0:256], s.Hi[:, kt, :], ALU.mult)
                        dve.tensor_tensor(s.tmp[2], PS[:, b + 1, 0:256], s.Hr[:, kt, :], ALU.mult)
                        ch.link(dve.tensor_tensor(s.tmp[3], PS[:, b, 0:256], s.Hi[:, kt, :], ALU.mult))
                        dve.tensor_tensor(s.A[:, kt, :], s.tmp[0], s.tmp[1], ALU.add)
                        ch.link(dve.tensor_tensor(s.B[:, kt, :], s.tmp[2], s.tmp[3], ALU.subtract))
                        dve.engine_nop().then_inc(s.ue, 1)
                        n_u += 1
                    if o == 0:
                        for j in range(nt):
                            dve.wait_ge(s.yf, n_y + 1)
                            dve.tensor_tensor(s.hv[:, s.t0 + j, cs], PS[:, 6 + n_y % 2, 0:256], s.hx1[:, s.t0 + j, cs],
                                              ALU.mult).then_inc(s.ye, 1)
                            n_y += 1
                    else:
                        for ct in range(2):
                            for n in range(s.L // s.tw):
                                dve.wait_ge(s.yf, n_y + 1)
                                c0 = s.t0 * P + n * s.tw
                                v = s.yT[:, 4 + half * 2 + ct, c0:c0 + s.tw]
                                dve.tensor_tensor(v, PS[:, 6 + n_y % 2, 0:s.tw], v, ALU.mult).then_inc(s.ye, 1)
                                n_y += 1

        class HyenaFold:

            def __init__(s, hv, hx1, yT, hbase, scratch):
                s.hv, s.hx1, s.yT = hv, hx1, yT
                s.fwd, s.inv = at(0, 2, 4, L_LAT), at(8192, 2, 8, 512)
                s.Hr, s.Hi = at(hbase, 8, 256), at(hbase + 2048, 8, 256)
                s.tap = at(hbase + 4096, 4, 4, 256)
                s.Q = [at(hbase + 4096, 8, 256), at(hbase + 6144, 8, 256)]
                o = scratch
                s.hdn = at(o, L_LAT + 1, parts=64)
                s.arg, s.rnd = at(o + 1026, L_LAT, parts=64), at(o + 2050, L_LAT, parts=64)
                s.dec = [at(o + 1026 + b * 1024, 2, 2, 256) for b in range(2)]
                s.tmp = [at(o + 3074 + b * 256, 256) for b in range(8)]
                s.big = [at(o + 3074 + b * 512, 512) for b in range(3)]
                s.z = at(o + 5122, L_LAT, parts=33)
                s.rev = at(o + 5122, 2, 512, parts=64)
                s.w3 = at(o + 6146, 2, 2, 512, parts=64)
                s.w1, s.w2 = at(o + 8194, 64, parts=33), at(o + 8258, 64, parts=64)
                s.v4 = at(o + 8322, 64, parts=4)
                s.c4 = at(o + 8386, 4, parts=64)
                s.rot = at(o + 8390, 2, 8)
                s.drow = at(o + 8406, 2, 512, parts=1)
                sm = lambda n: sem(f"hy_{n}")
                s.ld, s.dl = sm("in"), [sm("decay_in0"), sm("decay_in1")]
                s.full, s.hok = sm("mlp_full"), sm("mlp_ok")
                s.a1 = sm("arg")
                s.ff, s.fe = sm("filt_full"), sm("filt_evac")
                s.pf, s.pe_ = sm("spec_full"), sm("spec_evac")
                s.uf, s.ue = sm("fwd_full"), sm("fwd_evac")
                s.yf, s.ye = sm("inv_full"), sm("inv_evac")
                s.pm = sm("folded")

            def sync(s, sp):
                for dst, src in ((s.rot, I["rot_lat"]), (s.z, I["z_lat"]),
                                 (s.w1, I["hyena_w1"][0]), (s.w2, I["hyena_w2"][0]),
                                 (s.w3, I["hyena_w3"][0].rearrange("h (o d c) -> h o d c", o=2, d=2)),
                                 (s.drow, I["hyena_bias"][0:1]),
                                 (s.v4[0:1, :], I["hyena_b1"][0:1, :]), (s.v4[1:2, :], I["hyena_b2"][0:1, :]),
                                 (s.v4[2:4, :], I["hyena_freq"][0]), (s.fwd, I["fold_fwd"]), (s.inv, I["fold_inv"])):
                    sp.dma_start(dst, src).then_inc(s.ld, 16)
                for i in range(16):
                    if i >= 2:
                        sp.wait_ge(s.fe, i - 1)
                    else:
                        sp.wait_ge(s.hok, 3)
                    sp.dma_start(s.dec[i % 2], I["decay_lat"][i // 8, i % 4]).then_inc(s.dl[i % 2], 16)

            def pe(s, pe):
                pe.wait_ge(s.ld, 176)
                pe.transpose(PS[0:64, 7, 0:4], s.v4, ident[0:4, 0:4]).then_inc(s.full, 1)
                for layer in range(2):
                    if layer:
                        pe.wait_ge(s.hok, 2)
                    for n in range(2):
                        sl = slice(n * 512, (n + 1) * 512)
                        lhs, rhs = (s.w2, s.hdn[:, sl]) if layer else (s.w1, s.z[:, sl])
                        m = pe.matmul(PS[0:64, n + 2 * layer, :], lhs, rhs, start=True, stop=True)
                    m.then_inc(s.full, 1)
                pe.wait_ge(s.hok, 4)
                A1, B1 = s.fwd[:, 0], s.fwd[:, 1]
                A2, B2 = s.inv[:, 0], s.inv[:, 1]
                n_t = n_p = n_u = n_y = 0
                for r in range(4):
                    half, o = r // 2, r % 2
                    cs = slice(half * 256, half * 256 + 256)
                    for j in range(4):
                        if n_t:
                            pe.wait_ge(s.fe, n_t)
                        for d in range(2):
                            pe.matmul(PS[:, 0, d * 256:d * 256 + 256], s.hdn[:, j * P + d:j * P + d + P],
                                      s.w3[:, o, d, cs], start=True, stop=True)
                            m = pe.matmul(PS[:, 1, d * 256:d * 256 + 256], s.rev[:, d, j * P:j * P + P],
                                          s.w3[:, o, d, cs], start=True, stop=True)
                        m.then_inc(s.ff, 1)
                        n_t += 1
                    pe.wait_ge(s.fe, n_t)
                    for kt in range(8):
                        if n_p >= 2:
                            pe.wait_ge(s.pe_, n_p - 1)
                        b = 2 + n_p % 2 * 2
                        fp, fm, gp, gm = (s.tap[:, i] for i in range(4))
                        pairs = ((fp, gm), (gp, fm)) if kt < 4 else ((fm, gp), (gm, fp))
                        for q, (x, y) in enumerate(pairs):
                            for i, (tab, v) in enumerate(((A1, x), (B1, y))):
                                for j in range(4):
                                    m = pe.matmul(PS[:, b + q, 0:256], tab[:, j, kt * P:kt * P + P], v[:, j, :],
                                                  start=i == 0 and j == 0, stop=i == 1 and j == 3)
                        m.then_inc(s.pf, 1)
                        n_p += 1
                    pe.wait_ge(s.pm, r + 1)
                    pe.wait_ge(s.pe_, n_p)
                    for kt in range(8):
                        if n_u:
                            pe.wait_ge(s.ue, max(n_u - 1, 1))
                        b = 2 + n_u % 2 * 2
                        for q, tab in enumerate((A1, B1)):
                            t0 = 0 if (kt < 4) == (q == 0) else 4
                            for j in range(4):
                                m = pe.matmul(PS[:, b + q, 0:256], tab[:, j, kt * P:kt * P + P], s.hv[:, t0 + j, cs],
                                              start=j == 0, stop=j == 3)
                        m.then_inc(s.uf, 1)
                        n_u += 1
                    pe.wait_ge(s.ue, n_u)
                    for j in range(4 if o == 0 else 2):
                        if n_y:
                            pe.wait_ge(s.ye, n_y)
                        for q in range(2):
                            for kt in range(8):
                                plus = (kt < 4) == (q == 0)
                                tab, v = (A2, s.Q[0]) if plus else (B2, s.Q[1])
                                if o == 0:
                                    m = pe.matmul(PS[:, 6 + q, 0:256], tab[:, kt, j * P:j * P + P], v[:, kt, :],
                                                  start=kt == 0, stop=kt == 7)
                                else:
                                    m = pe.matmul(PS[:, 6 + q, :], v[:, kt, j * P:j * P + P], tab[:, kt, :],
                                                  start=kt == 0, stop=kt == 7)
                        m.then_inc(s.yf, 1)
                        n_y += 1

            def act(s, act, ch):
                act.wait_ge(s.full, 1)
                act.copy(s.c4, PS[0:64, 7, 0:4]).then_inc(s.hok, 1)
                for layer in range(2):
                    act.wait_ge(s.a1, layer + 1)
                    act.activation(s.hdn[:, 0:L_LAT], s.arg, ACT.Sin).then_inc(s.hok, 1)
                act.wait_ge(s.hok, 3)
                for d in range(2):
                    m = act.copy(s.rev[:, d, :], s.hdn[:, 1023 + d:511 + d:-1])
                m.then_inc(s.hok, 1)

            def dve(s, dve, ch):
                ch.link(dve.memset(s.hdn[:, L_LAT:L_LAT + 1], 0.0))
                for layer in range(2):
                    dve.wait_ge(s.hok, layer + 1)
                    dve.wait_ge(s.full, layer + 2)
                    for n in range(2):
                        sl = slice(n * 512, (n + 1) * 512)
                        ch.link(dve.tensor_scalar(s.arg[:, sl], PS[0:64, n + 2 * layer, :], s.c4[:, layer:layer + 1],
                                                  s.c4[:, 2 + layer:3 + layer], ALU.add, ALU.mult))
                    ch.link(dve.tensor_scalar(s.rnd, s.arg, 1.0 / (2 * math.pi), None, ALU.mult))
                    ch.link(dve.tensor_scalar(s.rnd, s.rnd, BIG, None, ALU.add))
                    ch.link(dve.tensor_scalar(s.rnd, s.rnd, -BIG, None, ALU.add))
                    hi = 6.28125
                    ch.link(dve.scalar_tensor_tensor(s.arg, s.rnd, -hi, s.arg, ALU.mult, ALU.add))
                    ch.link(dve.scalar_tensor_tensor(s.arg, s.rnd, -(2 * math.pi - hi), s.arg, ALU.mult, ALU.add))
                    dve.tensor_scalar(s.arg, s.arg, 3.1415925, -3.1415925, ALU.min, ALU.max).then_inc(s.a1, 1)
                dve.wait_ge(s.hok, 3)
                n_t = n_p = n_u = n_y = 0
                T = s.tmp
                for r in range(4):
                    half, o = r // 2, r % 2
                    cs = slice(half * 256, half * 256 + 256)
                    if o == 0:
                        for j in range(4):
                            a, b = s.hv[:, j, cs], s.hv[:, 4 + j, cs]
                            ch.link(dve.tensor_tensor(T[0], a, b, ALU.subtract))
                            ch.link(dve.tensor_tensor(a, a, b, ALU.add))
                            ch.link(dve.tensor_copy(b, T[0]))
                        dve.engine_nop().then_inc(s.pm, 1)
                    if r:
                        dve.wait_ge(s.yf, n_y)
                    for j in range(4):
                        dve.wait_ge(s.dl[n_t % 2], 16 * (n_t // 2 + 1))
                        dve.wait_ge(s.ff, n_t + 1)
                        dec = s.dec[n_t % 2]
                        for fold in range(2):
                            for d in range(2):
                                m = dve.tensor_tensor(T[2 * d + fold], PS[:, fold, d * 256:d * 256 + 256],
                                                      dec[:, fold, d, :], ALU.mult)
                        ch.link(m)
                        if j == 0:
                            ch.link(dve.tensor_tensor(T[0][0:1, :], T[0][0:1, :], s.drow[:, o, cs], ALU.add))
                        for d in range(2):
                            dve.tensor_tensor(s.tap[:, 2 * d, j, :], T[2 * d], T[2 * d + 1], ALU.add)
                            m = dve.tensor_tensor(s.tap[:, 2 * d + 1, j, :], T[2 * d], T[2 * d + 1], ALU.subtract)
                        ch.link(m)
                        dve.engine_nop().then_inc(s.fe, 1)
                        n_t += 1
                    for kt in range(8):
                        dve.wait_ge(s.pf, n_p + 1)
                        b = 2 + n_p % 2 * 2
                        c, sn = s.rot[:, 0, kt:kt + 1], s.rot[:, 1, kt:kt + 1]
                        ch.link(dve.tensor_copy(T[0], PS[:, b, 0:256]))
                        dve.tensor_tensor(T[1], T[0], PS[:, b + 1, 0:256], ALU.add)
                        ch.link(dve.tensor_tensor(T[2], T[0], PS[:, b + 1, 0:256], ALU.subtract))
                        dve.engine_nop().then_inc(s.pe_, 1)
                        dve.tensor_scalar(T[3], T[2], sn, None, ALU.mult)
                        ch.link(dve.tensor_scalar(T[4], T[2], c, None, ALU.mult))
                        dve.scalar_tensor_tensor(s.Hr[:, kt, :], T[1], c, T[3], ALU.mult, ALU.add)
                        ch.link(dve.scalar_tensor_tensor(s.Hi[:, kt, :], T[1], sn, T[4], ALU.mult, ALU.subtract))
                        n_p += 1
                    for kt in range(8):
                        dve.wait_ge(s.uf, n_u + 1)
                        b = 2 + n_u % 2 * 2
                        ch.link(dve.tensor_copy(T[0], PS[:, b, 0:256]))
                        dve.tensor_tensor(T[1], T[0], PS[:, b + 1, 0:256], ALU.add)
                        ch.link(dve.tensor_tensor(T[2], T[0], PS[:, b + 1, 0:256], ALU.subtract))
                        dve.tensor_tensor(T[3], T[1], s.Hr[:, kt, :], ALU.mult)
                        dve.tensor_tensor(T[4], T[2], s.Hi[:, kt, :], ALU.mult)
                        dve.tensor_tensor(T[5], T[2], s.Hr[:, kt, :], ALU.mult)
                        ch.link(dve.tensor_tensor(T[6], T[1], s.Hi[:, kt, :], ALU.mult))
                        dve.tensor_tensor(T[3], T[3], T[4], ALU.add)
                        ch.link(dve.tensor_tensor(T[5], T[5], T[6], ALU.subtract))
                        dve.tensor_tensor(s.Q[0][:, kt, :], T[3], T[5], ALU.add)
                        ch.link(dve.tensor_tensor(s.Q[1][:, kt, :], T[3], T[5], ALU.subtract))
                        dve.engine_nop().then_inc(s.ue, 1)
                        n_u += 1
                    if o == 0:
                        for j in range(4):
                            dve.wait_ge(s.yf, n_y + 1)
                            ch.link(dve.tensor_copy(T[0], PS[:, 6, 0:256]))
                            dve.tensor_tensor(T[1], T[0], PS[:, 7, 0:256], ALU.add)
                            ch.link(dve.tensor_tensor(T[2], T[0], PS[:, 7, 0:256], ALU.subtract))
                            dve.engine_nop().then_inc(s.ye, 1)
                            dve.tensor_tensor(T[1], T[1], s.hx1[:, j, cs], ALU.mult)
                            ch.link(dve.tensor_tensor(T[2], T[2], s.hx1[:, 4 + j, cs], ALU.mult))
                            dve.tensor_tensor(s.hv[:, j, cs], T[1], T[2], ALU.add)
                            ch.link(dve.tensor_tensor(s.hv[:, 4 + j, cs], T[1], T[2], ALU.subtract))
                            n_y += 1
                        dve.engine_nop().then_inc(s.pm, 1)
                    else:
                        for ct in range(2):
                            dve.wait_ge(s.yf, n_y + 1)
                            t, y1, y2 = s.big
                            ch.link(dve.tensor_copy(t, PS[:, 6, :]))
                            dve.tensor_tensor(y1, t, PS[:, 7, :], ALU.add)
                            ch.link(dve.tensor_tensor(y2, t, PS[:, 7, :], ALU.subtract))
                            dve.engine_nop().then_inc(s.ye, 1)
                            v = s.yT[:, 4 + half * 2 + ct, :]
                            dve.tensor_tensor(v[:, 0:512], v[:, 0:512], y1, ALU.mult)
                            ch.link(dve.tensor_tensor(v[:, 1023:511:-1], v[:, 1023:511:-1], y2, ALU.mult))
                            n_y += 1

        def layer_norm_tile(dve, ch, r, y, grow, lng, lnb, sd_ready, sd_need, var_ready, out):
            st = small[:, 0:12].rearrange("p (a b) -> p a b", a=2)
            for n in range(2):
                ch.link(dve.tensor_tensor(out[:, n * 512:(n + 1) * 512], y[n], grow[:, n * 512:(n + 1) * 512], ALU.mult))
            ch.link(dve.scalar_tensor_tensor(r, r, ALPHA, out, ALU.mult, ALU.add))
            for n in range(2):
                ch.link(dve.bn_stats(st[:, n, :], r[:, n * 512:(n + 1) * 512]))
            ch.link(dve.bn_aggr(small[:, 12:14], small[:, 0:12]))
            dve.tensor_scalar(small[:, 14:15], small[:, 13:14], EPS, None, ALU.add).then_inc(var_ready, 1)
            dve.wait_ge(sd_ready, sd_need)
            ch.link(dve.reciprocal(small[:, 16:17], small[:, 15:16]))
            ch.link(dve.tensor_scalar(r, r, small[:, 12:13], small[:, 16:17], ALU.subtract, ALU.mult))
            ch.link(dve.tensor_tensor(r, r, lng, ALU.mult))
            return dve.tensor_tensor(out, r, lnb, ALU.add)

        class OutProj:
            def __init__(s, l, yT, h, base):
                s.l, s.yT, s.h = l, yT, h
                s.W = at(base, KD, D)
                s.g = at(base + 8192, 2, D)
                s.ln = at(base + 10240, 2, D)
                s.x = [at(base + 12288 + b * D, D) for b in range(2)]
                s.wl, s.cl = sem(f"op_w_in"), sem(f"op_rows_in")
                s.xl = [sem(f"op_x_in_{b}") for b in range(2)]
                s.full, s.hs = sem("op_full"), sem("op_h_stored")
                s.var, s.sd, s.done = sem(f"op_var"), sem(f"op_sd"), sem(f"op_done")

            def sync(s, sp):
                w = I["even_w_out"] if s.l == 0 else I["odd_w_out"]
                sp.dma_start(s.W, w[0].rearrange("(k p) n -> p k n", p=P)).then_inc(s.wl, 16)
                for c in range(2):
                    sp.dma_start(s.g[:, c, :], modD[s.l, c:c + 1, 2 * D:3 * D].to_broadcast((P, D))).then_inc(s.cl, 16)
                sp.dma_start(s.ln[:, 0, :], I["ln_g"][s.l, 0:1, :].to_broadcast((P, D))).then_inc(s.cl, 16)
                sp.dma_start(s.ln[:, 1, :], I["ln_b"][s.l, 0:1, :].to_broadcast((P, D))).then_inc(s.cl, 16)
                for t in range(NT):
                    if t >= 2:
                        sp.wait_ge(s.done, t - 1)
                    sp.dma_start(s.x[t % 2], rows_of(t, s.l)).then_inc(s.xl[t % 2], 16)
                    if t >= 2:
                        sp.dma_start(mD[(t - 2) * P:(t - 1) * P, :], s.h[:, t - 2, :]).then_inc(s.hs, 16)
                for t in (NT - 2, NT - 1):
                    sp.wait_ge(s.done, t + 1)
                    sp.dma_start(mD[t * P:(t + 1) * P, :], s.h[:, t, :]).then_inc(s.hs, 16)
                sp.wait_ge(s.hs, 16 * NT)

            def pe(s, pe):
                pe.wait_ge(s.wl, 16)
                for t in range(NT):
                    if t >= 4:
                        pe.wait_ge(s.done, t - 3)
                    for n in range(2):
                        for k in range(KD):
                            m = pe.matmul(PS[:, t % 4 * 2 + n, :], s.yT[:, k, t * P:(t + 1) * P], s.W[:, k, n * 512:(n + 1) * 512],
                                          start=k == 0, stop=k == KD - 1)
                    m.then_inc(s.full, 1)

            def act(s, act, ch):
                for t in range(NT):
                    act.wait_ge(s.var, t + 1)
                    act.activation(small[:, 15:16], small[:, 14:15], ACT.Sqrt).then_inc(s.sd, 1)

            def dve(s, dve, ch):
                dve.wait_ge(s.cl, 64)
                for t in range(NT):
                    dve.wait_ge(s.full, t + 1)
                    dve.wait_ge(s.xl[t % 2], 16 * (t // 2 + 1))
                    b = t % 4 * 2
                    layer_norm_tile(dve, ch, s.x[t % 2], (PS[:, b, :], PS[:, b + 1, :]), s.g[:, t // NL, :],
                                    s.ln[:, 0, :], s.ln[:, 1, :], s.sd, t + 1, s.var,
                                    s.h[:, t, :]).then_inc(s.done, 1)

        class Router:
            def __init__(s, l, h, base, aff, slot, pick):
                s.l, s.h, s.aff, s.slot, s.pick = l, h, aff, slot, pick
                s.uT = at(base, KD, TOK)
                s.w = at(base + 9216, KD, E_N)
                o = base + 9216 + 128
                s.affT = at(o, TOK, parts=16)
                s.work = at(o + 1152, TOK, parts=16)
                s.ge = at(o + 2304, TOK, parts=16)
                s.eq = at(o + 3456, TOK, parts=16)
                s.cum = at(o + 4608, TOK, parts=16)
                s.m8 = at(o + 5760, 8 * 18, parts=16)
                s.one = at(o + 5904, TOK, parts=16)
                s.red = at(o + 7056, 2, NT)
                s.cnt = at(o + 7080, 4, parts=16)
                o += 7088
                s.hot = [at(o + b * 520, 520).bitcast(BF16) for b in range(2)]
                s.what = at(o + 1040, NT * E_N * 5 // 2).bitcast(BF16).rearrange("p (t e w) -> p t e w", t=NT, e=E_N)
                s.rest = at(o + 1400, NT, E_N)
                s.iota, s.parts = at(o + 1544, P), at(o + 1672, NT, 2)
                s.read, s.readc = at(o + 1690, E_N, 5), at(o + 1770, E_N, 5, parts=CAP_C)
                s.zero = at(o + 1850, D)
                sm = lambda n: sem(f"rt_{n}")
                s.ld = sm("w_in")
                s.full, s.ea, s.ed = sm("u_full"), sm("u_evac_act"), sm("u_evac_dve")
                s.lf, s.sub, s.ex, s.affok, s.tf, s.sl, s.sf = (sm(n) for n in (
                    "logits", "shifted", "exp", "aff", "aff_t", "slots", "slots_t"))
                s.zok, s.zst, s.cl, s.ho, s.hr = (sm(n) for n in ("zero", "zeroed", "const_in", "hot", "hot_read"))

            def sync(s, sp):
                sp.dma_start(s.w, I["moe_router"][s.l].rearrange("(k p) e -> p k e", p=P)).then_inc(s.ld, 16)
                sp.dma_start(s.iota, I["slot_iota"]).then_inc(s.cl, 16)
                sp.dma_start(s.parts, I["token_parts"]).then_inc(s.cl, 16)
                sp.wait_ge(s.zok, 1)
                for t in range(NT):
                    sp.dma_start(yD[t * P:(t + 1) * P, :], s.zero).then_inc(s.zst, 16)
                sp.wait_ge(s.zst, 16 * NT)

            def pe(s, pe):
                for t in range(NT):
                    if t >= 2:
                        pe.wait_ge(s.ea, t - 1)
                        pe.wait_ge(s.ed, t - 1)
                    for k in range(KD):
                        m = pe.transpose(PS[:, t % 2 * 2 + k // 4, k % 4 * P:k % 4 * P + P],
                                         s.h[:, t, k * P:(k + 1) * P], ident)
                    m.then_inc(s.full, 1)
                pe.wait_ge(s.ea, NT)
                pe.wait_ge(s.ed, NT)
                pe.wait_ge(s.ld, 16)
                for t in range(NT):
                    for k in range(KD):
                        m = pe.matmul(PS[:, 4, t * E_N:(t + 1) * E_N], s.uT[:, k, t * P:(t + 1) * P], s.w[:, k, :],
                                      start=k == 0, stop=k == KD - 1)
                m.then_inc(s.lf, 1)
                pe.wait_ge(s.affok, 1)
                for t in range(NT):
                    m = pe.transpose(PS[0:16, 5 + t // 4, t % 4 * P:t % 4 * P + P], s.aff[:, t, :], ident)
                m.then_inc(s.tf, 1)
                pe.wait_ge(s.sl, 1)
                for t in range(NT):
                    m = pe.transpose(PS[:, 4, t * E_N:(t + 1) * E_N], s.ge[:, t * P:(t + 1) * P], ident[0:16, 0:16])
                m.then_inc(s.sf, 1)
                for e in range(E_N):
                    pe.wait_ge(s.ho, e + 1)
                    hot = s.hot[e % 2]
                    for t in range(NL):
                        pe.matmul(PS[:, 5, e * 5:e * 5 + 5], hot[:, t * P:(t + 1) * P], s.what[:, t, e, :],
                                  start=t == 0, stop=t == NL - 1)
                    pe.matmul(PS[0:CAP_C, 6, e * 5:e * 5 + 5], hot[:, NL * P:NL * P + CAP_C], s.what[:, NL, e, :],
                              start=True, stop=True).then_inc(s.hr, 1)

            def evac(s, eng, bank, sm):
                for t in range(NT):
                    eng.wait_ge(s.full, t + 1)
                    for k in range(bank * 4, bank * 4 + 4):
                        m = modulate_tile(eng, s.uT[:, k, t * P:(t + 1) * P],
                                          PS[:, t % 2 * 2 + bank, k % 4 * P:k % 4 * P + P], 2, k, t < NL, bank == 0)
                    m.then_inc(sm, 1)

            def act(s, act, ch):
                s.evac(act, 0, s.ea)
                act.wait_ge(s.sub, 1)
                act.activation(s.aff, s.aff, ACT.Exp).then_inc(s.ex, 1)

            def dve(s, dve, ch):
                dve.memset(s.zero, 0.0).then_inc(s.zok, 1)
                s.evac(dve, 1, s.ed)
                dve.wait_ge(s.lf, 1)
                lg = PS[:, 4, 0:NT * E_N].rearrange("p (a b) -> p a b", a=NT)
                col = lambda i: s.red[:, i, :].rearrange("p (a b) -> p a b", b=1).to_broadcast((P, NT, E_N))
                ch.link(dve.tensor_reduce(s.red[:, 0, :], lg, AX.X, ALU.max))
                dve.tensor_tensor(s.aff, lg, col(0), ALU.subtract).then_inc(s.sub, 1)
                dve.wait_ge(s.ex, 1)
                ch.link(dve.tensor_reduce(s.red[:, 1, :], s.aff, AX.X, ALU.add))
                ch.link(dve.reciprocal(s.red[:, 1, :], s.red[:, 1, :]))
                dve.tensor_tensor(s.aff, s.aff, col(1), ALU.mult).then_inc(s.affok, 1)
                ch.link(dve.memset(s.one, 1.0))
                dve.wait_ge(s.tf, 1)
                for b in range(3):
                    w = 512 if b < 2 else 128
                    dve.tensor_copy(s.affT[:, b * 512:b * 512 + w], PS[0:16, 5 + b, 0:w])
                    ch.link(dve.tensor_copy(s.work[:, b * 512:b * 512 + w], PS[0:16, 5 + b, 0:w]))
                i = 0
                for off, L, cap in ((0, L_LAT, CAP_L), (L_LAT, L_CTX, CAP_C)):
                    w = s.work[:, off:off + L]
                    a = s.affT[:, off:off + L]
                    ge, eq, cum, one = (v[:, off:off + L] for v in (s.ge, s.eq, s.cum, s.one))
                    for r in range(cap // 8):
                        m8 = s.m8[:, 8 * i:8 * i + 8]
                        i += 1
                        ch.link(dve.max(m8, w))
                        if r < cap // 8 - 1:
                            ch.link(dve.match_replace(w, m8, w, -1.0))
                    thr = m8[:, 7:8]
                    ch.link(dve.tensor_scalar(ge, a, thr, None, ALU.is_gt))
                    ch.link(dve.tensor_reduce(s.cnt[:, 0:1], ge, AX.X, ALU.add))
                    ch.link(dve.tensor_scalar(s.cnt[:, 1:2], s.cnt[:, 0:1], -1.0, float(cap), ALU.mult, ALU.add))
                    ch.link(dve.tensor_scalar(eq, a, thr, None, ALU.is_equal))
                    ch.link(dve.tensor_tensor_scan(cum, one, eq, 0.0, ALU.mult, ALU.add))
                    ch.link(dve.tensor_scalar(cum, cum, s.cnt[:, 1:2], None, ALU.is_le))
                    ch.link(dve.tensor_tensor(eq, eq, cum, ALU.mult))
                    ch.link(dve.tensor_tensor(eq, eq, ge, ALU.add))
                    ch.link(dve.tensor_tensor_scan(cum, one, eq, 0.0, ALU.mult, ALU.add))
                    ch.link(dve.tensor_tensor(ge, cum, eq, ALU.mult))
                    ch.link(dve.tensor_scalar(ge, ge, -1.0, None, ALU.add))
                dve.engine_nop().then_inc(s.sl, 1)
                dve.wait_ge(s.sf, 1)
                ch.link(dve.tensor_copy(s.slot.rearrange("p a b -> p (a b)"), PS[:, 4, 0:NT * E_N]))
                dve.wait_ge(s.cl, 32)
                w = s.what
                for i in range(2):
                    dve.tensor_copy(w[:, :, :, i], s.parts[:, :, i:i + 1].to_broadcast((P, NT, E_N)))
                ch.link(dve.tensor_copy(w[:, :, :, 2], s.aff))
                ch.link(dve.tensor_tensor(s.rest, s.aff, w[:, :, :, 2], ALU.subtract))
                ch.link(dve.tensor_copy(w[:, :, :, 3], s.rest))
                ch.link(dve.tensor_tensor(s.rest, s.rest, w[:, :, :, 3], ALU.subtract))
                ch.link(dve.tensor_copy(w[:, :, :, 4], s.rest))
                for e in range(E_N):
                    if e >= 2:
                        dve.wait_ge(s.hr, e - 1)
                    for t in range(NT):
                        n = P if t < NL else CAP_C
                        m = dve.tensor_scalar(s.hot[e % 2][:, t * P:t * P + n], s.iota[:, 0:n], s.slot[:, t, e:e + 1],
                                              None, ALU.is_equal)
                    m.then_inc(s.ho, 1)
                dve.wait_ge(s.hr, E_N)
                for n, src, v, (idx, gate) in ((P, PS[:, 5, 0:5 * E_N], s.read, s.pick[0:2]),
                                               (CAP_C, PS[0:CAP_C, 6, 0:5 * E_N], s.readc, s.pick[2:4])):
                    ch.link(dve.tensor_copy(v.rearrange("p a b -> p (a b)"), src))
                    ch.link(dve.memset(idx, 0))
                    ch.link(dve.memset(gate, 0.0))
                    ch.link(dve.scalar_tensor_tensor(idx[:, 0:E_N], v[:, :, 0], float(P), v[:, :, 1], ALU.mult, ALU.add))
                    ch.link(dve.tensor_tensor(gate[:, 0:E_N], v[:, :, 2], v[:, :, 3], ALU.add))
                    ch.link(dve.tensor_tensor(gate[:, 0:E_N], gate[:, 0:E_N], v[:, :, 4], ALU.add))

        RING, EB = 4, 4

        class Experts:

            def __init__(s, l, pick, base):
                s.l = l
                s.idx, s.gate, s.idxc, s.gatec = pick
                o = [base]

                def take(n):
                    o[0] += n
                    return o[0] - n
                s.w13 = [at(take(2048), 2, KD, P) for _ in range(RING)]
                s.w2 = [at(take(D), D) for _ in range(RING)]
                s.rows = [at(take(D), D) for _ in range(2)]
                s.rowsc = [at(take(D), D, parts=CAP_C) for _ in range(2)]
                s.xs = [at(take(KD * SLOTS), KD, SLOTS) for _ in range(2)]
                s.hid = at(take(KF * SLOTS), KF, SLOTS)
                s.sil = [at(take(SLOTS), SLOTS) for _ in range(2)]
                s.oT = at(take(KD * SLOTS), KD, SLOTS)
                s.out = at(take(D), D)
                s.outc = at(take(D), D, parts=CAP_C)
                s.cur = [at(take(1), 1).bitcast(U32) for _ in range(2)]
                s.curc = [at(take(1), 1, parts=CAP_C).bitcast(U32) for _ in range(2)]
                s.g = [at(take(1), 1) for _ in range(2)]
                s.gateq = [at(take(1), 1, parts=CAP_C) for _ in range(2)]
                assert o[0] <= FREE, o
                sm = lambda n: sem(f"ex_{n}")
                s.wl = [sm(f"panel_in{r}") for r in range(RING)]
                s.used = sm("panel_used")
                s.passed = sm("pool_passed")
                s.picked, s.gin = sm("picked"), indirect[l][0:2]
                s.xt, s.xe = sm("rows_t"), sm("xs_ready")
                s.ab, s.sl, s.hd = sm("ab_full"), sm("silu"), sm("hid")
                s.oe, s.tf, s.te = sm("out_evac"), sm("out_t"), sm("out_rows")
                s.sc, s.added = indirect[l][2], sm("rows_added")

            def sync(s, sp):
                w1, w3, w2 = I["moe_w1"][s.l], I["moe_w3"][s.l], I["moe_w2"][s.l]
                per = EB * KF
                with sp.Fori(0, E_N // EB, 1) as b:
                    for n in range(per):
                        r = n % RING
                        e = b * EB + n // KF
                        f = n % KF
                        sp.wait_ge(s.used, b * per + n + 1)
                        for q, w in enumerate((w1, w3)):
                            src = w[bass.ds(e, 1), :, f * P:(f + 1) * P].rearrange("o (k p) n -> p (o k) n", p=P)
                            sp.dma_start(s.w13[r][:, q], src).then_inc(s.wl[r], 16)
                        src = w2[bass.ds(e, 1), f * P:(f + 1) * P, :].rearrange("o p n -> p (o n)")
                        sp.dma_start(s.w2[r], src).then_inc(s.wl[r], 16)

            def pool(s, pool):
                def pick(e, q):
                    for dst, src in ((s.cur[q], s.idx), (s.curc[q], s.idxc), (s.g[q], s.gate), (s.gateq[q], s.gatec)):
                        pool.tensor_copy(dst, src[:, bass.ds(e, 1)]).then_inc(s.picked, 1)

                def gather(q):
                    for dst, idx in ((s.rows[q], s.cur[q]), (s.rowsc[q], s.curc[q])):
                        pool.indirect_dma_start(dst, None, mD, bass.IndirectOffsetOnAxis(idx, 0)).then_inc(s.gin[q], 16)

                pool.nop().then_inc(s.added, 1)
                pick(0, 0)
                pool.wait_ge(s.picked, 4)
                gather(0)
                with pool.Fori(0, E_N // EB, 1) as b:
                    for x in range(EB):
                        e = b * EB + x
                        pick(e + 1, (x + 1) % 2)
                        pool.wait_ge(s.picked, e * 4 + 8)
                        pool.wait_ge(s.xt, e + 1)
                        pool.nop().then_inc(s.passed, 1)
                        gather((x + 1) % 2)
                        pool.wait_ge(s.te, e * 3 + 4)
                        pool.nop().then_inc(s.passed, 1)
                        for src, idx in ((s.out, s.cur[x % 2]), (s.outc, s.curc[x % 2])):
                            pool.indirect_dma_start(yD, bass.IndirectOffsetOnAxis(idx, 0), src, None,
                                                    compute_op=ALU.add).then_inc(s.sc, 16)
                        pool.wait_ge(s.sc, e * 32 + 32)
                        pool.nop().then_inc(s.added, 1)
                pool.wait_ge(s.gin[0], 16 * (E_N + 2))

            def pe(s, pe):
                per = EB * KF
                slots = lambda m: PS[:, m // 3, m % 3 * SLOTS:m % 3 * SLOTS + SLOTS]
                pe.nop().then_inc(s.used, RING)
                pe.nop().then_inc(s.te, 1)
                pe.nop().then_inc(s.xt, 1)

                def turn_rows(pair, q):
                    pe.wait_ge(s.gin[q], pair * 32 + 32)
                    for k in range(KD):
                        pe.transpose(PS[:, 3 + k // 4, k % 4 * P:k % 4 * P + P], s.rows[q][:, k * P:(k + 1) * P], ident)
                    for k in range(KD):
                        m = pe.transpose(PS[:, 5, k * CAP_C:(k + 1) * CAP_C], s.rowsc[q][:, k * P:(k + 1) * P],
                                         ident[0:CAP_C, 0:CAP_C])
                    m.then_inc(s.xt, 1)

                def turn_out(e):
                    pe.wait_ge(s.oe, e + 1)
                    pe.wait_ge(s.xe, e + 2)
                    for m_ in range(KD):
                        pe.transpose(PS[:, 3 + m_ // 4, m_ % 4 * P:m_ % 4 * P + P], s.oT[:, m_, 0:CAP_L], ident)
                    for m_ in range(4):
                        m = pe.transpose(PS[0:CAP_C, 5, m_ * P:m_ * P + P], s.oT[:, m_, CAP_L:SLOTS], ident)
                    m.then_inc(s.tf, 1)
                    pe.wait_ge(s.te, e * 3 + 2)
                    for m_ in range(4, KD):
                        m = pe.transpose(PS[0:CAP_C, 3, m_ % 4 * P:m_ % 4 * P + P], s.oT[:, m_, CAP_L:SLOTS], ident)
                    m.then_inc(s.tf, 1)

                turn_rows(0, 0)
                with pe.Fori(0, E_N // EB, 1) as b:
                    for x in range(EB):
                        e = b * EB + x

                        def down(f):
                            n = x * KF + f
                            pe.wait_ge(s.hd, b * per + n + 1)
                            for m_ in range(KD):
                                m = pe.matmul(slots(m_), s.w2[n % RING][:, m_ * P:(m_ + 1) * P], s.hid[:, f, :],
                                              start=f == 0 and m_ % 3 == 0, stop=f == KF - 1, skip_group_check=True)
                            m.then_inc(s.used, 1)

                        pe.wait_ge(s.xe, e + 1)
                        for f in range(KF):
                            n = x * KF + f
                            pe.wait_ge(s.wl[n % RING], b * (48 * per // RING) + 48 * (n // RING + 1))
                            if n >= 2:
                                pe.wait_ge(s.hd, b * per + n - 1)
                            for q in range(2):
                                for k in range(KD):
                                    m = pe.matmul(PS[:, 6 + n % 2, q * 256:q * 256 + SLOTS], s.w13[n % RING][:, q, k, :],
                                                  s.xs[x % 2][:, k, :], start=k == 0, stop=k == KD - 1)
                            m.then_inc(s.ab, 1)
                            if f:
                                down(f - 1)
                            elif x:
                                turn_out(e - 1)
                            if f == 7:
                                pe.wait_ge(s.te, e * 3 + 1)
                                turn_rows(b * (EB // 2) + (x + 1) // 2, (x + 1) % 2)
                        down(KF - 1)
                        if x == EB - 1:
                            turn_out(e)

            def act(s, act, ch):
                per = EB * KF

                def take_rows(e, q):
                    act.wait_ge(s.xt, e + 2)
                    for m_ in range(KD):
                        modulate_tile(act, s.xs[q][:, m_, 0:CAP_L], PS[:, 3 + m_ // 4, m_ % 4 * P:m_ % 4 * P + P], 2, m_, True, True)
                        m = modulate_tile(act, s.xs[q][:, m_, CAP_L:SLOTS], PS[:, 5, m_ * CAP_C:(m_ + 1) * CAP_C], 2, m_, False, True)
                    m.then_inc(s.xe, 1)

                def take_out(e, q):
                    act.wait_ge(s.added, e + 1)
                    act.wait_ge(s.picked, e * 4 + 4)
                    act.wait_ge(s.tf, e * 2 + 1)
                    act.activation(s.out[:, 0:512], PS[:, 3, :], ACT.Copy, scale=s.g[q]).then_inc(s.te, 1)
                    act.activation(s.out[:, 512:1024], PS[:, 4, :], ACT.Copy, scale=s.g[q])
                    act.activation(s.outc[:, 0:512], PS[0:CAP_C, 5, :], ACT.Copy, scale=s.gateq[q]).then_inc(s.te, 1)
                    act.wait_ge(s.tf, e * 2 + 2)
                    act.activation(s.outc[:, 512:1024], PS[0:CAP_C, 3, :], ACT.Copy, scale=s.gateq[q]).then_inc(s.te, 1)

                take_rows(0, 0)
                with act.Fori(0, E_N // EB, 1) as b:
                    for x in range(EB):
                        e = b * EB + x
                        for f in range(KF):
                            n = x * KF + f
                            act.wait_ge(s.ab, b * per + n + 1)
                            if n >= 2:
                                act.wait_ge(s.hd, b * per + n - 1)
                            act.activation(s.sil[n % 2], PS[:, 6 + n % 2, 0:SLOTS], ACT.Silu).then_inc(s.sl, 1)
                            if f == 0 and x:
                                take_out(e - 1, (x - 1) % 2)
                            if f == 7:
                                take_rows(e + 1, (x + 1) % 2)
                        act.wait_ge(s.used, b * per + (x + 1) * KF + RING)
                        for i in range(3):
                            w = 3 if i < 2 else 2
                            m = act.copy(s.oT[:, 3 * i:3 * i + w, :].rearrange("p a b -> p (a b)"), PS[:, i, 0:w * SLOTS])
                        m.then_inc(s.oe, 1)
                        if x == EB - 1:
                            take_out(e, x % 2)

            def dve(s, dve, ch):
                per = EB * KF
                with dve.Fori(0, E_N // EB, 1) as b:
                    for n in range(per):
                        dve.wait_ge(s.sl, b * per + n + 1)
                        dve.tensor_tensor(s.hid[:, n % KF, :], PS[:, 6 + n % 2, 256:256 + SLOTS], s.sil[n % 2],
                                          ALU.mult).then_inc(s.hd, 1)

        class MoeEnd:

            def __init__(s, l, h, base, mod):
                s.l, s.h, s.mod = l, h, mod
                s.y = [at(base + 6144 + b * D, D) for b in range(2)]
                s.yl = [sem("me_sum_in0"), sem("me_sum_in1")]
                s.g, s.ln = at(base, 2, D), at(base + 2048, 2, D)
                s.o = [at(base + 4096 + b * D, D) for b in range(2)]
                sm = lambda n: sem(f"me_{n}")
                s.cl, s.var, s.sd, s.done = sm("rows_in"), sm("var"), sm("sd"), sm("done")
                s.st = [sm("stored0"), sm("stored1")]

            def sync(s, sp):
                for c in range(2):
                    sp.dma_start(s.g[:, c, :], modD[s.l, c:c + 1, 5 * D:6 * D].to_broadcast((P, D))).then_inc(s.cl, 16)
                sp.dma_start(s.ln[:, 0, :], I["ln_g"][s.l, 1:2, :].to_broadcast((P, D))).then_inc(s.cl, 16)
                sp.dma_start(s.ln[:, 1, :], I["ln_b"][s.l, 1:2, :].to_broadcast((P, D))).then_inc(s.cl, 16)
                for t in range(2):
                    sp.dma_start(s.y[t], yD[t * P:(t + 1) * P, :]).then_inc(s.yl[t], 16)
                if s.mod:
                    for c in range(2):
                        sp.dma_start(s.mod.bias[c:c + 1, :], I["ada_b"][s.mod.l:s.mod.l + 1, :]).then_inc(s.mod.ld, 16)
                    for n in range(4):
                        s.mod.load(sp, n)
                for t in range(NT):
                    if s.mod and t + 4 < 12:
                        s.mod.load(sp, t + 4)
                    sp.wait_ge(s.done, t + 1)
                    if t + 2 < NT:
                        sp.dma_start(s.y[t % 2], yD[(t + 2) * P:(t + 3) * P, :]).then_inc(s.yl[t % 2], 16)
                    if s.l < DEPTH - 1:
                        dst = hD[t * P:(t + 1) * P, :]
                    else:
                        dst = O["y_sample"][0, t * P:(t + 1) * P, :] if t < NL else O["y_prompt"][0]
                    sp.dma_start(dst, s.o[t % 2]).then_inc(s.st[t % 2], 16)
                sp.wait_ge(s.st[0], 16 * 5)
                sp.wait_ge(s.st[1], 16 * 4)
                if s.mod:
                    s.mod.store(sp)

            def pe(s, pe):
                if s.mod:
                    s.mod.pe(pe)

            def act(s, act, ch):
                for t in range(NT):
                    act.wait_ge(s.var, t + 1)
                    act.activation(small[:, 15:16], small[:, 14:15], ACT.Sqrt).then_inc(s.sd, 1)

            def dve(s, dve, ch):
                dve.wait_ge(s.cl, 64)
                for t in range(NT):
                    if t >= 2:
                        dve.wait_ge(s.st[t % 2], 16 * (t // 2))
                    dve.wait_ge(s.yl[t % 2], 16 * (t // 2 + 1))
                    y = s.y[t % 2]
                    layer_norm_tile(dve, ch, s.h[:, t, :], (y[:, 0:512], y[:, 512:1024]), s.g[:, t // NL, :],
                                    s.ln[:, 0, :], s.ln[:, 1, :], s.sd, t + 1, s.var, s.o[t % 2]).then_inc(s.done, 1)
                    if s.mod:
                        if t == 0:
                            dve.wait_ge(s.mod.ld, 32)
                        s.mod.add_bias(dve, t)
                if s.mod:
                    for n in range(NT, 12):
                        s.mod.add_bias(dve, n)
                    s.mod.columns(dve, ch)

        class Retention:
            def __init__(s, uT, yT, base):
                s.uT, s.yT = uT, yT
                o = [base]

                def take(n):
                    o[0] += n
                    return o[0] - n
                s.W = at(take(KD * 512), KD, 2, 256)
                s.v = at(take(NT * 256), NT, 256)
                s.g = at(take(NT * 256), NT, 256)
                s.k = [at(take(NT * 256), NT, 256) for _ in range(2)]
                s.qT = at(take(2 * TOK), 2, TOK)
                s.kT = at(take(2 * TOK), 2, TOK)
                s.qd = [at(take(2 * L_LAT), 2, L_LAT) for _ in range(2)]
                s.attn = at(take(TOK), NT, P)
                s.Sb = at(take(2 * NL * 256), 2, NL, 256)
                s.Sf = [at(take(512), 2, 256) for _ in range(2)]
                s.rope = at(take(2 * L_LAT), 2, NL, 128)
                s.qk = at(take(512), 2, 256)
                s.rp = [at(take(256), 256) for _ in range(2)]
                s.dist = at(take(4 * P), 4, P)
                s.prow = at(take(2 * P), 2, P)
                s.pcol = at(take(2), 2)
                s.lg = at(take(8), 8)
                s.gstep = at(take(8), 8)
                s.cd = at(take(4), 4)
                s.dm = at(take(P), P)
                s.dt = at(take(P), P)
                s.gr = at(take(2 * P), 2, P)
                s.stt = at(take(16), 16)
                assert o[0] <= FREE, (o, FREE)
                sm = lambda n: sem(f"re_{n}")
                s.cl, s.s0 = sm("const_in"), sm("s0_in")
                s.wl, s.wu = sm("w_in"), sm("w_used")
                s.lgq, s.lgx = sm("lg_req"), sm("lg_ok")
                s.pf, s.pe_ = sm("proj_full"), sm("proj_evac")
                s.ro, s.tf, s.te = sm("rope"), sm("t_full"), sm("t_evac")
                s.vf, s.ve = sm("vg_full"), sm("vg_evac")
                s.dreq, s.dok, s.mok = sm("decay_req"), sm("decay_exp"), sm("decay_ok")
                s.af, s.ae = sm("att_full"), sm("att_ok")
                s.uf, s.ub = sm("upd_full"), sm("state_ok")
                s.of, s.oe, s.var, s.sd, s.yo = sm("o_full"), sm("o_read"), sm("o_var"), sm("o_sd"), sm("y_ok")
                s.yf, s.yv = sm("y_t_full"), sm("y_t_evac")
                s.st = sm("state_stored")

            def sync(s, sp):
                for dst, src in ((s.rope, I["rope"]), (s.dist, I["time_dist"]), (s.prow, I["pos_rows"]),
                                 (s.pcol, I["pos_cols"]),
                                 (s.lg, I["ret_decay"].rearrange("o d h -> o (d h)").to_broadcast((P, 8)))):
                    sp.dma_start(dst, src).then_inc(s.cl, 16)
                for h in range(C_H):
                    for part in range(2):
                        if h or part:
                            sp.wait_ge(s.wu, 2 * h + part)
                        for j in range(2):
                            c0 = (2 * part + j) * D + h * 256
                            sp.dma_start(s.W[:, :, j, :], I["odd_w_in"][0, :, c0:c0 + 256]
                                         .rearrange("(k p) n -> p k n", p=P)).then_inc(s.wl, 16)
                        if part == 1:
                            if h:
                                sp.wait_ge(s.st, 64 * h)
                                sp.wait_ge(s.of, NT * h)
                            for dst, d in ((s.Sf[0], 0), (s.Sb[:, :, NL - 1, :], 1)):
                                sp.dma_start(dst, I["state_ret"][0, 0, d, h].rearrange("(a p) e -> p a e", p=P)).then_inc(s.s0, 16)
                    for i, d in enumerate((1, 0)):
                        sp.wait_ge(s.ub, h * 32 + (16 if d == 1 else 32))
                        src = s.Sf[1] if d == 1 else s.Sf[0]
                        for a in range(2):
                            sp.dma_start(O["new_state_ret"][0, 0, d, h, a * P:(a + 1) * P, :], src[:, a, :]).then_inc(s.st, 16)
                sp.wait_ge(s.st, 64 * C_H)

            UPD, OUT = (4, 0, 1, 2), (5, 7)

            def pe(s, pe):
                for h in range(C_H):
                    pe.wait_ge(s.wl, 64 * h + 32)

                    def turn(t):
                        pe.wait_ge(s.ro, h * NT + t + 1)
                        n = h * NT + t
                        if n:
                            pe.wait_ge(s.te, n)
                        for i in range(4):
                            m = pe.transpose(PS[:, 2, i * P:(i + 1) * P], s.qk[:, i // 2, i % 2 * P:i % 2 * P + P], ident)
                        m.then_inc(s.tf, 1)
                    for t in range(NT):
                        n = h * NT + t
                        if n >= 2:
                            pe.wait_ge(s.pe_, n - 1)
                        if t == 0 and h:
                            pe.wait_ge(s.ub, 32 * h)
                            pe.wait_ge(s.oe, NT * h)
                        for k in range(KD):
                            m = pe.matmul(PS[:, n % 2, :], s.uT[:, k, t * P:(t + 1) * P],
                                          s.W[:, k, :, :].rearrange("p a b -> p (a b)"), start=k == 0, stop=k == KD - 1)
                        m.then_inc(s.pf, 1)
                        if t:
                            turn(t - 1)
                    pe.wait_ge(s.pf, (h + 1) * NT)
                    pe.nop().then_inc(s.wu, 1)
                    turn(NT - 1)
                    pe.wait_ge(s.wl, 64 * h + 64)
                    for t in range(NT):
                        n = h * NT + t
                        if n >= 2:
                            pe.wait_ge(s.ve, n - 1)
                        for k in range(KD):
                            m = pe.matmul(PS[:, 6 + n % 2, :], s.uT[:, k, t * P:(t + 1) * P],
                                          s.W[:, k, :, :].rearrange("p a b -> p (a b)"), start=k == 0, stop=k == KD - 1)
                        m.then_inc(s.vf, 1)
                    pe.wait_ge(s.vf, (h + 1) * NT)
                    pe.nop().then_inc(s.wu, 1)
                    pe.wait_ge(s.te, (h + 1) * NT)
                    for t in range(NT):
                        n = h * NT + t
                        if n >= 2:
                            pe.wait_ge(s.ae, n - 1)
                        for a in range(2):
                            m = pe.matmul(PS[:, 4 + n % 2, 0:P], s.kT[:, a, t * P:(t + 1) * P], s.qT[:, a, t * P:(t + 1) * P],
                                          start=a == 0, stop=a == 1)
                        m.then_inc(s.af, 1)
                    pe.wait_ge(s.ve, (h + 1) * NT)
                    pe.wait_ge(s.ae, (h + 1) * NT)
                    u = 0

                    def update(d, c):
                        nonlocal u
                        for a in range(2):
                            if h * 32 + u >= 4:
                                pe.wait_ge(s.ub, h * 32 + u - 3)
                            pe.matmul(PS[:, s.UPD[u % 4], 0:256], s.k[d][:, c, a * P:(a + 1) * P], s.v[:, c, :],
                                      start=True, stop=True).then_inc(s.uf, 1)
                            u += 1
                    for c in range(NL - 1, 0, -1):
                        update(1, c)
                    update(1, NL)
                    update(0, 0)
                    for c in range(NT):
                        n = h * NT + c
                        if n >= 2:
                            pe.wait_ge(s.oe, n - 1)
                        out = PS[:, s.OUT[n % 2], 0:256]
                        m = pe.matmul(out, s.attn[:, c, :], s.v[:, c, :], start=True, stop=c == NL)
                        if c < NL:
                            pe.wait_ge(s.ub, h * 32 + 16 + 2 * c)
                            if c == 0:
                                pe.wait_ge(s.mok, 2 * h + 2)
                            sl = slice(c * P, (c + 1) * P)
                            for a in range(2):
                                pe.matmul(out, s.qd[1][:, a, sl], s.Sb[:, a, c, :], start=False, stop=False)
                            for a in range(2):
                                m = pe.matmul(out, s.qd[0][:, a, sl], s.Sf[c % 2][:, a, :], start=False, stop=a == 1)
                        m.then_inc(s.of, 1)
                        if c < NL - 2:
                            update(0, c + 1)
                        elif c == NL - 2:
                            update(0, NL)
                        if c:
                            s.turn_y(pe, h, c - 1)
                    s.turn_y(pe, h, NT - 1)

            def turn_y(s, pe, h, c):
                n = h * NT + c
                pe.wait_ge(s.yo, n + 1)
                if n:
                    pe.wait_ge(s.yv, n)
                for a in range(2):
                    m = pe.transpose(PS[:, 3, a * P:(a + 1) * P], s.rp[n % 2][:, a * P:(a + 1) * P], ident)
                m.then_inc(s.yf, 1)

            def act(s, act, ch):
                act.wait_ge(s.cl, 80)
                act.activation(s.lg, s.lg, ACT.Exp, scale=-1.0).then_inc(s.lgx, 1)
                act.wait_ge(s.lgq, 1)
                act.activation(s.lg, s.lg, ACT.Ln).then_inc(s.lgx, 1)
                act.wait_ge(s.lgq, 2)
                act.activation(s.gstep, s.gstep, ACT.Exp).then_inc(s.lgx, 1)
                for h in range(C_H):
                    for n in range(2):
                        act.wait_ge(s.dreq, 2 * h + n + 1)
                        if n == 0:
                            act.activation(s.gr, s.gr, ACT.Exp)
                            act.activation(s.cd[:, 0:2], s.cd[:, 0:2], ACT.Exp)
                            act.activation(s.dm, s.dm, ACT.Exp).then_inc(s.dok, 1)
                        else:
                            act.activation(s.dt, s.dt, ACT.Exp).then_inc(s.dok, 1)

                    def turn(t):
                        n = h * NT + t
                        act.wait_ge(s.tf, n + 1)
                        if t == 0 and h:
                            act.wait_ge(s.of, h * NT)
                        act.copy(s.qT[:, :, t * P:(t + 1) * P], PS[:, 2, 0:256].rearrange("p (a b) -> p a b", a=2))
                        act.copy(s.kT[:, :, t * P:(t + 1) * P],
                                 PS[:, 2, 256:512].rearrange("p (a b) -> p a b", a=2)).then_inc(s.te, 1)
                    for t in range(NT):
                        turn(t)
                    for t in range(NT):
                        n = h * NT + t
                        act.wait_ge(s.vf, n + 1)
                        if t == 0 and h:
                            act.wait_ge(s.uf, h * 32)
                            act.wait_ge(s.yo, h * NT)
                        act.copy(s.v[:, t, :], PS[:, 6 + n % 2, 0:256])
                        act.activation(s.g[:, t, :], PS[:, 6 + n % 2, 256:512], ACT.Silu).then_inc(s.ve, 1)
                    for c in range(NT):
                        act.wait_ge(s.var, h * NT + c + 1)
                        act.activation(s.stt[:, 9:10], s.stt[:, 8:9], ACT.Sqrt).then_inc(s.sd, 1)
                        if c:
                            s.act_y(act, h, c - 1)
                    s.act_y(act, h, NT - 1)

            def act_y(s, act, h, c):
                n = h * NT + c
                act.wait_ge(s.yf, n + 1)
                act.copy(s.yT[:, 2 * h:2 * h + 2, c * P:(c + 1) * P],
                         PS[:, 3, 0:256].rearrange("p (a b) -> p a b", a=2)).then_inc(s.yv, 1)

            def dve(s, dve, ch):
                dve.wait_ge(s.cl, 80)
                dve.wait_ge(s.lgx, 1)
                dve.tensor_scalar(s.lg, s.lg, 1.0, None, ALU.add).then_inc(s.lgq, 1)
                dve.wait_ge(s.lgx, 2)
                ch.link(dve.tensor_scalar(s.lg, s.lg, -1.0, None, ALU.mult))
                dve.tensor_scalar(s.gstep, s.lg, float(P), None, ALU.mult).then_inc(s.lgq, 1)
                dve.wait_ge(s.lgx, 3)
                for h in range(C_H):
                    lg = [s.lg[:, d * C_H + h:d * C_H + h + 1] for d in range(2)]
                    gc = [s.gstep[:, d * C_H + h:d * C_H + h + 1] for d in range(2)]
                    for d in range(2):
                        dve.tensor_scalar(s.gr[:, d, :], s.prow[:, d, :], lg[d], None, ALU.mult)
                        dve.tensor_scalar(s.cd[:, d:d + 1], s.pcol[:, d:d + 1], lg[d], None, ALU.mult)
                    dve.tensor_scalar(s.dt, s.dist[:, 2, :], lg[1], None, ALU.mult)
                    dve.tensor_scalar(s.dm, s.dist[:, 0, :], lg[0], None, ALU.mult).then_inc(s.dreq, 1)
                    dve.wait_ge(s.dok, 2 * h + 1)
                    ch.link(dve.tensor_tensor(s.dm, s.dm, s.dist[:, 1, :], ALU.mult))
                    dve.engine_nop().then_inc(s.dreq, 1)
                    dve.wait_ge(s.dok, 2 * h + 2)
                    ch.link(dve.tensor_tensor(s.dt, s.dt, s.dist[:, 3, :], ALU.mult))
                    ch.link(dve.tensor_tensor(s.dm, s.dm, s.dt, ALU.add))
                    dve.engine_nop().then_inc(s.mok, 1)
                    for t in range(NT):
                        n = h * NT + t
                        dve.wait_ge(s.pf, n + 1)
                        if n:
                            dve.wait_ge(s.tf, n)
                        ps = PS[:, n % 2, :]
                        if t < NL:
                            x = ps.rearrange("p (a b c) -> p a b c", a=4, b=2)
                            o = s.qk.rearrange("p a b -> p (a b)").rearrange("p (a b c) -> p a b c", a=4, b=2)
                            tmp = s.rp[0].rearrange("p (a c) -> p a c", a=4)
                            for i in range(2):
                                for j in range(2):
                                    tab = s.rope[:, i if j == 0 else 1 - i, t, :].rearrange("p (b c) -> p b c", b=2)
                                    for qk in range(2):
                                        dst = (o[:, 2 * qk:2 * qk + 2, i, :] if j == 0 else tmp[:, 2 * qk:2 * qk + 2, :])
                                        m = dve.tensor_tensor(dst, x[:, 2 * qk:2 * qk + 2, j, :], tab, ALU.mult)
                                ch.link(m)
                                ch.link(dve.tensor_tensor(o[:, :, i, :], o[:, :, i, :], tmp, ALU.subtract if i == 0 else ALU.add))
                        else:
                            ch.link(dve.tensor_copy(s.qk.rearrange("p a b -> p (a b)"), ps))
                        dve.engine_nop().then_inc(s.pe_, 1)
                        ch.link(dve.tensor_scalar(s.qk[:, 1, :], s.qk[:, 1, :], C_HD ** -0.5, None, ALU.mult))
                        for d in range(2):
                            m = dve.tensor_scalar(s.k[d][:, t, :], s.qk[:, 1, :], s.cd[:, d:d + 1], None, ALU.mult)
                        m.then_inc(s.ro, 1)
                    dve.wait_ge(s.te, (h + 1) * NT)
                    for d in range(2):
                        gr = s.gr[:, d:d + 1, :].to_broadcast((P, NL, P))
                        for a in range(2):
                            m = dve.tensor_tensor(s.qd[d][:, a, :].rearrange("p (c t) -> p c t", t=P),
                                                  s.qT[:, a, 0:L_LAT].rearrange("p (c t) -> p c t", t=P), gr, ALU.mult)
                    m.then_inc(s.mok, 1)
                    for t in range(NT):
                        dve.wait_ge(s.af, h * NT + t + 1)
                        dve.tensor_tensor(s.attn[:, t, :], PS[:, 4 + (h * NT + t) % 2, 0:P], s.dm, ALU.mult).then_inc(s.ae, 1)
                    dve.wait_ge(s.s0, 32 * (h + 1))
                    u = h * 32
                    for c in range(NL - 1, 0, -1):
                        for a in range(2):
                            u += 1
                            dve.wait_ge(s.uf, u)
                            if c < NL - 1:
                                dve.wait_ge(s.ub, u - 2)
                            dve.scalar_tensor_tensor(s.Sb[:, a, c - 1, :], s.Sb[:, a, c, :], gc[1],
                                                     PS[:, s.UPD[(u - 1) % 4], 0:256], ALU.mult, ALU.add).then_inc(s.ub, 1)
                    for a in range(2):
                        u += 1
                        dve.wait_ge(s.uf, u)
                        dve.tensor_copy(s.Sf[1][:, a, :], PS[:, s.UPD[(u - 1) % 4], 0:256]).then_inc(s.ub, 1)
                    for c in range(NT):
                        n = h * NT + c
                        if c < NL:
                            if c == 0:
                                dve.wait_ge(s.st, 64 * h + 32)
                            else:
                                dve.wait_ge(s.of, n)
                            for a in range(2):
                                u += 1
                                dve.wait_ge(s.uf, u)
                                U = PS[:, s.UPD[(u - 1) % 4], 0:256]
                                if c < NL - 1:
                                    if c:
                                        dve.wait_ge(s.ub, u - 2)
                                    dve.scalar_tensor_tensor(s.Sf[(c + 1) % 2][:, a, :], s.Sf[c % 2][:, a, :], gc[0],
                                                             U, ALU.mult, ALU.add).then_inc(s.ub, 1)
                                else:
                                    dve.tensor_copy(s.Sf[0][:, a, :], U).then_inc(s.ub, 1)
                        o = PS[:, s.OUT[n % 2], 0:256]
                        dve.wait_ge(s.of, n + 1)
                        st = s.stt[:, 0:6]
                        ch.link(dve.bn_stats(st, o))
                        ch.link(dve.bn_aggr(s.stt[:, 6:8], st))
                        dve.tensor_scalar(s.stt[:, 8:9], s.stt[:, 7:8], EPS, None, ALU.add).then_inc(s.var, 1)
                        dve.wait_ge(s.sd, n + 1)
                        ch.link(dve.reciprocal(s.stt[:, 10:11], s.stt[:, 9:10]))
                        if n >= 2:
                            dve.wait_ge(s.yf, n - 1)
                        ch.link(dve.tensor_scalar(s.rp[n % 2], o, s.stt[:, 6:7], s.stt[:, 10:11],
                                                  ALU.subtract, ALU.mult))
                        dve.engine_nop().then_inc(s.oe, 1)
                        dve.tensor_tensor(s.rp[n % 2], s.rp[n % 2], s.g[:, c, :], ALU.mult).then_inc(s.yo, 1)

        uT0 = at(0, KD, TOK)
        yT0 = at(33792, KD, TOK)
        hv, hx1 = at(24576, NT, 512), at(29184, NT, 512)
        h0, h1 = at(0, NT, D), at(18432, NT, D)
        uT1, yT1 = at(0, KD, TOK), at(9216, KD, TOK)

        def picks(o):
            n = E_N + 1
            return at(o, NT, E_N), at(o + 144, NT, E_N), (
                at(o + 288, n).bitcast(U32), at(o + 288 + n, n),
                at(o + 288 + 2 * n, n, parts=CAP_C).bitcast(U32), at(o + 288 + 3 * n, n, parts=CAP_C))
        aff0, slot0, pick0 = picks(9216)
        aff1, slot1, pick1 = picks(27648)
        stages = [
            Modulation(0, 0), MixerInput(0, uT0, 9216), Hgrn(uT0, yT0, 9216, 43008, 33792 + 4 * TOK),
            HyenaIn(uT0, 9216, hv, hx1, yT0),
            HyenaFold(hv, hx1, yT0, 16384, 43008),
            HyenaConv("ctx", hv, hx1, yT0, at(0, 2, 1, P), 16384, 43008),
            OutProj(0, yT0, h0, 18432), Router(0, h0, 9600, aff0, slot0, pick0),
            Experts(0, pick0, 9600), MoeEnd(0, h0, 9600, Modulation(1, 19000)),
            MixerInput(1, uT1, 9216), Retention(uT1, yT1, 18432),
            OutProj(1, yT1, h1, 27648), Router(1, h1, 28032, aff1, slot1, pick1),
            Experts(1, pick1, 28032), MoeEnd(1, h1, 28032, None),
        ]
        if I.get("_stop"):
            stages = stages[:I["_stop"]]

        cuts = [c for c in (0, 5, 10) if c < len(stages)] + [len(stages)]
        for lo, hi in zip(cuts, cuts[1:]):
            run_block(nc, stages[lo:hi], stage_end, (Experts,), act_seq, dve_seq)
            if hi < len(stages):
                nums = sorted(v.num for v in taken.values())
                assert nums == list(range(nums[0], nums[-1] + 1))
                nc.all_engine_barrier(sems_to_clear=range(nums[0], nums[-1] + 1))
                n_stage.clear()


def run_block(nc, stages, stage_end, with_pool, act_seq, dve_seq):
    with nc.Block() as block:
        @block.sync
        def _(sp):
            for s in stages:
                s.sync(sp)
                stage_end(sp, "sp")

        @block.gpsimd
        def _(pool):
            for s in stages:
                if isinstance(s, with_pool):
                    s.pool(pool)
                stage_end(pool, "pool")

        @block.tensor
        def _(pe):
            for s in stages:
                s.pe(pe)
                stage_end(pe, "pe")

        @block.scalar
        def _(act):
            ch = Chain(act, act_seq)
            for s in stages:
                s.act(act, ch)
                stage_end(act, "act")

        @block.vector
        def _(dve):
            ch = Chain(dve, dve_seq)
            for s in stages:
                s.dve(dve, ch)
                stage_end(dve, "dve")


OUTS = {"y_prompt": (1, L_CTX, D), "y_sample": (1, L_LAT, D),
        "new_state_hgrn": (1, 1, 2, A_H, P, P), "new_state_ret": (1, 1, 2, C_H, C_HD, C_HD)}


def kernel(**inputs):
    from concourse import bacc
    from concourse.bass_utils import run_bass_kernel_spmd

    nc = bacc.Bacc("TRN2", target_bir_lowering=False, num_devices=1)
    arrays = {n: np.ascontiguousarray(a) for n, a in inputs.items() if n != "hgrn_lb"}
    arrays.update({n: np.ascontiguousarray(a) for n, a in CONST.items()})
    I = {n: nc.dram_tensor(n, a.shape, F32, kind="ExternalInput").ap() for n, a in arrays.items()}
    O = {n: nc.dram_tensor(n + "_out", shape, F32, kind="ExternalOutput").ap() for n, shape in OUTS.items()}
    build(nc, I, O)
    r = run_bass_kernel_spmd(nc, [arrays], core_ids=[0])
    return tuple(r.results[0][n + "_out"] for n in OUTS)
```
